# Optimizing a Trainium2 kernel written in Bass

```python
import jax, jax.numpy as jnp
from jax import lax
import numpy as np

D_MODEL = 1024
BATCH = 1
SEQ = 128
DEPTH = 4
DEC_BATCH = 1
DEC_SEQ = 512
PAST_LEN = 128

GRID_W = 64
N_MIXERS = 3
N_ATTN_LAYERS = (DEPTH + 2) // 3
N_RWKV_LAYERS = (DEPTH + 1) // 3
N_POOL_LAYERS = DEPTH // 3
MLA_HEADS = 16
Q_LORA_RANK = 384
KV_LORA_RANK = 256
QK_NOPE_DIM = 64
QK_ROPE_DIM = 32
V_HEAD_DIM = 64
ROPE_THETA = 10000.0
Q_BLOCK = 128
RWKV_HEAD = 64
RWKV_HEADS = D_MODEL // RWKV_HEAD
DECAY_LORA = 64
AAA_LORA = 64
GATE_LORA = 128
RWKV_GN_EPS = 64e-5
POOL_WINDOWS = (2, 4, 8, 16)
POOL_GROUP = D_MODEL // len(POOL_WINDOWS)
D_FF = -(-8 * D_MODEL // (3 * 256)) * 256
ALPHA = (2 * DEPTH) ** 0.25
BETA = (8 * DEPTH) ** -0.25
LN_EPS = 1e-5
RMS_EPS = 1e-6

kernel_name = 'hybrid_mla_rwkv7_pool_diffusion_step'

def layer_norm(x, g, b):
    xf = x.astype(jnp.float32)
    mu = xf.mean(-1, keepdims=True)
    var = jnp.square(xf - mu).mean(-1, keepdims=True)
    return ((xf - mu) * lax.rsqrt(var + LN_EPS) * g + b).astype(x.dtype)

def rms_norm(x, g):
    xf = x.astype(jnp.float32)
    return (xf * lax.rsqrt(jnp.square(xf).mean(-1, keepdims=True) + RMS_EPS) * g).astype(x.dtype)

def adaln(cond, w, b):
    m = (jax.nn.silu(cond) @ w + b)[..., None, :]
    return jnp.split(m, 6, axis=-1)

def modulate(x, shift, scale):
    return x * (1.0 + scale) + shift

def swiglu(h, wg, wu, wd):
    return (jax.nn.silu(h @ wg) * (h @ wu)) @ wd

def axial_rope(n_tokens, dtype):
    rows = n_tokens // GRID_W
    row = jnp.repeat(jnp.arange(rows, dtype=jnp.float32), GRID_W)
    col = jnp.tile(jnp.arange(GRID_W, dtype=jnp.float32), rows)
    n_freq = QK_ROPE_DIM // 4
    inv_freq = ROPE_THETA ** (-jnp.arange(n_freq, dtype=jnp.float32) / n_freq)
    ang = jnp.stack([row[:, None] * inv_freq, col[:, None] * inv_freq], axis=1)
    return jnp.cos(ang).astype(dtype), jnp.sin(ang).astype(dtype)

def rope_2d(x, cos, sin):
    xs = x.reshape(*x.shape[:-1], 2, 2, QK_ROPE_DIM // 4)
    x1, x2 = xs[..., 0, :], xs[..., 1, :]
    out = jnp.stack([x1 * cos - x2 * sin, x1 * sin + x2 * cos], axis=-2)
    return out.reshape(x.shape)

def mla_queries(h, wq_a, q_norm, wq_b):
    B, T, _ = h.shape
    q = (rms_norm(h @ wq_a, q_norm) @ wq_b).reshape(B, T, MLA_HEADS, QK_NOPE_DIM + QK_ROPE_DIM)
    return q[..., :QK_NOPE_DIM], q[..., QK_NOPE_DIM:]

def mla_compress_kv(h, wkv_a, kv_norm):
    kv = h @ wkv_a
    return rms_norm(kv[..., :KV_LORA_RANK], kv_norm), kv[..., KV_LORA_RANK:]

def mla_expand_kv(ckv, wkv_b):
    B, L, _ = ckv.shape
    kv = (ckv @ wkv_b).reshape(B, L, MLA_HEADS, QK_NOPE_DIM + V_HEAD_DIM)
    return kv[..., :QK_NOPE_DIM], kv[..., QK_NOPE_DIM:]

def mla_attend(q_nope, q_pe, k_nope, k_pe, v):
    B, T, H, _ = q_nope.shape
    nb = T // Q_BLOCK
    scale = (QK_NOPE_DIM + QK_ROPE_DIM) ** -0.5

    def blocks(t):
        return jnp.moveaxis(t.reshape(B, nb, Q_BLOCK, *t.shape[2:]), 1, 0)

    def one_block(qs):
        qn, qp = qs
        s = jnp.einsum('bqhd,bkhd->bhqk', qn, k_nope) + jnp.einsum('bqhr,bkr->bhqk', qp, k_pe)
        p = jax.nn.softmax(s.astype(jnp.float32) * scale, axis=-1).astype(v.dtype)
        return jnp.einsum('bhqk,bkhd->bqhd', p, v)

    o = lax.map(one_block, (blocks(q_nope), blocks(q_pe)))
    return jnp.moveaxis(o, 0, 1).reshape(B, T, H * V_HEAD_DIM)

def mla_context(h, wq_a, q_norm, wq_b, wkv_a, kv_norm, wkv_b, wo):
    q_nope, q_pe = mla_queries(h, wq_a, q_norm, wq_b)
    ckv, kpe = mla_compress_kv(h, wkv_a, kv_norm)
    k_nope, v = mla_expand_kv(ckv, wkv_b)
    return mla_attend(q_nope, q_pe, k_nope, kpe, v) @ wo, ckv, kpe

def mla_latent(h, ckv_ctx, kpe_ctx, cos, sin, wq_a, q_norm, wq_b, wkv_a, kv_norm, wkv_b, wo):
    q_nope, q_pe = mla_queries(h, wq_a, q_norm, wq_b)
    q_pe = rope_2d(q_pe, cos[:, None], sin[:, None])
    ckv, kpe = mla_compress_kv(h, wkv_a, kv_norm)
    kpe = rope_2d(kpe, cos, sin)
    k_nope, v = mla_expand_kv(jnp.concatenate([ckv_ctx, ckv], axis=1), wkv_b)
    k_pe = jnp.concatenate([kpe_ctx, kpe], axis=1)
    return mla_attend(q_nope, q_pe, k_nope, k_pe, v) @ wo

def split_heads(t):
    return t.reshape(*t.shape[:-1], RWKV_HEADS, RWKV_HEAD)

def token_shift_centred(x):
    prev = jnp.pad(x[:, :-1], ((0, 0), (1, 0), (0, 0)))
    nxt = jnp.pad(x[:, 1:], ((0, 0), (0, 1), (0, 0)))
    return 0.5 * (prev + nxt)

def wkv7_scan(r, w, k, v, a, b, s0, reverse):
    f32 = jnp.float32
    seq = tuple(jnp.moveaxis(t.astype(f32), 1, 0) for t in (r, w, k, v, a, b))

    def step(S, inp):
        rt, wt, kt, vt, at, bt = inp
        sa = jnp.einsum('bhvk,bhk->bhv', S, at)
        S = S * wt[:, :, None, :] + sa[..., None] * bt[:, :, None, :] + vt[..., None] * kt[:, :, None, :]
        return S, jnp.einsum('bhvk,bhk->bhv', S, rt)

    s_fin, y = lax.scan(step, s0.astype(f32), seq, reverse=reverse)
    return jnp.moveaxis(y, 0, 1), s_fin

def rwkv7_bidir(h, s0_f, s0_b, mu, wr, wk, wv, w0, w1, w2, a0, a1, a2, g1, g2,
                k_k, k_a, r_k, lnx_g, lnx_b, wo):
    B, T, D = h.shape
    xx = token_shift_centred(h) - h
    xr, xw, xk, xv, xa, xg = (h + xx * mu[i] for i in range(6))
    r = split_heads(xr @ wr)
    k = xk @ wk
    v = split_heads(xv @ wv)
    g = jax.nn.sigmoid(xg @ g1) @ g2
    kkf = split_heads(k * k_k).astype(jnp.float32)
    kk = kkf / jnp.maximum(jnp.sqrt(jnp.sum(kkf * kkf, -1, keepdims=True)), 1e-12)

    def direction(d, s0, reverse):
        logw = -jax.nn.softplus(-(w0[d] + jnp.tanh(xw @ w1[d]) @ w2[d]).astype(jnp.float32)) - 0.5
        decay = jnp.exp(-jnp.exp(logw))
        a = jax.nn.sigmoid(a0[d] + (xa @ a1[d]) @ a2[d])
        kd = k * (1.0 + (a - 1.0) * k_a)
        y, s = wkv7_scan(r, split_heads(decay), split_heads(kd), v, -kk, kk * split_heads(a), s0, reverse)
        return y, s, kd

    y_f, s_f, k_f = direction(0, s0_f, False)
    y_b, s_b, k_b = direction(1, s0_b, True)
    y = y_f + y_b
    mu_y = y.mean(-1, keepdims=True)
    var_y = jnp.square(y - mu_y).mean(-1, keepdims=True)
    yn = ((y - mu_y) * lax.rsqrt(var_y + RWKV_GN_EPS)).reshape(B, T, D) * lnx_g + lnx_b
    bonus = jnp.sum(r * split_heads(k_f + k_b) * r_k, -1, keepdims=True) * v
    out = (yn.astype(h.dtype) + bonus.reshape(B, T, D)) * g
    return out @ wo, s_f, s_b

def multiscale_pool(h, w_grp, scale):
    B, T, D = h.shape
    C = POOL_GROUP
    hf = h.astype(jnp.float32)
    cs = jnp.pad(lax.cumsum(hf, axis=1), ((0, 0), (1, 0), (0, 0)))
    t = jnp.arange(T)
    parts = []
    for gi, win in enumerate(POOL_WINDOWS):
        lo = jnp.clip(t - win // 2, 0, T)
        hi = jnp.clip(t - win // 2 + win, 0, T)
        sl = slice(gi * C, (gi + 1) * C)
        cnt = (hi - lo).astype(jnp.float32)[None, :, None]
        parts.append((cs[:, hi, sl] - cs[:, lo, sl]) / cnt - hf[:, :, sl])
    pooled = jnp.stack(parts, axis=2).astype(h.dtype)
    out = jnp.einsum('btgc,gcd->btgd', pooled, w_grp).reshape(B, T, D)
    return out * scale

def setup_inputs(seed: int = 0):
    key = jax.random.key(seed)
    keys = iter(jax.random.split(key, 64))
    f32 = jnp.float32
    D, H, N = D_MODEL, RWKV_HEADS, RWKV_HEAD
    NA, NB, NC = N_ATTN_LAYERS, N_RWKV_LAYERS, N_POOL_LAYERS
    G, C = len(POOL_WINDOWS), POOL_GROUP
    qk_dim = QK_NOPE_DIM + QK_ROPE_DIM

    def nrm(shape, scale):
        return scale * jax.random.normal(next(keys), shape, f32)

    def uni(shape, lo, hi):
        return jax.random.uniform(next(keys), shape, f32, lo, hi)

    return {
        'x_prompt': nrm((BATCH, SEQ, D), 1.0),
        'x_sample': nrm((DEC_BATCH, DEC_SEQ, D), 1.0),
        'cache_ckv': nrm((DEC_BATCH, NA, PAST_LEN, KV_LORA_RANK), 1.0),
        'cache_kpe': nrm((DEC_BATCH, NA, PAST_LEN, QK_ROPE_DIM), 1.0),
        'state_wkv': nrm((DEC_BATCH, NB, 2, H, N, N), 0.5),
        'c': nrm((DEC_BATCH, D), 1.0),
        'c_ctx': nrm((D,), 1.0),
        'ada_w': nrm((DEPTH, D, 6 * D), D ** -0.5),
        'ada_b': nrm((DEPTH, 6 * D), 0.02),
        'ln_g': 1.0 + nrm((DEPTH, 2, D), 0.1),
        'ln_b': nrm((DEPTH, 2, D), 0.02),
        'ffn_wg': nrm((DEPTH, D, D_FF), D ** -0.5),
        'ffn_wu': nrm((DEPTH, D, D_FF), D ** -0.5),
        'ffn_wd': nrm((DEPTH, D_FF, D), BETA * D_FF ** -0.5),
        'mla_wq_a': nrm((NA, D, Q_LORA_RANK), D ** -0.5),
        'mla_q_norm': 1.0 + nrm((NA, Q_LORA_RANK), 0.1),
        'mla_wq_b': nrm((NA, Q_LORA_RANK, MLA_HEADS * qk_dim), Q_LORA_RANK ** -0.5),
        'mla_wkv_a': nrm((NA, D, KV_LORA_RANK + QK_ROPE_DIM), D ** -0.5),
        'mla_kv_norm': 1.0 + nrm((NA, KV_LORA_RANK), 0.1),
        'mla_wkv_b': nrm((NA, KV_LORA_RANK, MLA_HEADS * (QK_NOPE_DIM + V_HEAD_DIM)), KV_LORA_RANK ** -0.5),
        'mla_wo': nrm((NA, MLA_HEADS * V_HEAD_DIM, D), BETA * (MLA_HEADS * V_HEAD_DIM) ** -0.5),
        'rwkv_mu': uni((NB, 6, D), 0.0, 1.0),
        'rwkv_wr': nrm((NB, D, D), D ** -0.5),
        'rwkv_wk': nrm((NB, D, D), D ** -0.5),
        'rwkv_wv': nrm((NB, D, D), D ** -0.5),
        'rwkv_w0': uni((NB, 2, D), -6.0, 0.0),
        'rwkv_w1': nrm((NB, 2, D, DECAY_LORA), D ** -0.5),
        'rwkv_w2': nrm((NB, 2, DECAY_LORA, D), 0.5 * DECAY_LORA ** -0.5),
        'rwkv_a0': nrm((NB, 2, D), 0.1),
        'rwkv_a1': nrm((NB, 2, D, AAA_LORA), D ** -0.5),
        'rwkv_a2': nrm((NB, 2, AAA_LORA, D), AAA_LORA ** -0.5),
        'rwkv_g1': nrm((NB, D, GATE_LORA), D ** -0.5),
        'rwkv_g2': nrm((NB, GATE_LORA, D), GATE_LORA ** -0.5),
        'rwkv_k_k': 0.85 + nrm((NB, D), 0.05),
        'rwkv_k_a': 1.0 + nrm((NB, D), 0.05),
        'rwkv_r_k': nrm((NB, H, N), 0.1),
        'rwkv_lnx_g': 1.0 + nrm((NB, D), 0.1),
        'rwkv_lnx_b': nrm((NB, D), 0.02),
        'rwkv_wo': nrm((NB, D, D), BETA * D ** -0.5),
        'pool_w': nrm((NC, G, C, C), BETA * C ** -0.5),
        'pool_scale': 1.0 + nrm((NC, D), 0.1),
    }

def reference(x_prompt, x_sample, cache_ckv, cache_kpe, state_wkv, c, c_ctx,
              ada_w, ada_b, ln_g, ln_b, ffn_wg, ffn_wu, ffn_wd,
              mla_wq_a, mla_q_norm, mla_wq_b, mla_wkv_a, mla_kv_norm, mla_wkv_b, mla_wo,
              rwkv_mu, rwkv_wr, rwkv_wk, rwkv_wv, rwkv_w0, rwkv_w1, rwkv_w2,
              rwkv_a0, rwkv_a1, rwkv_a2, rwkv_g1, rwkv_g2, rwkv_k_k, rwkv_k_a, rwkv_r_k,
              rwkv_lnx_g, rwkv_lnx_b, rwkv_wo, pool_w, pool_scale):
    cos, sin = axial_rope(x_sample.shape[1], x_sample.dtype)
    yp, ys = x_prompt, x_sample
    new_ckv, new_kpe, new_wkv = [], [], []
    for layer in range(DEPTH):
        kind, j = layer % N_MIXERS, layer // N_MIXERS
        mp = adaln(c_ctx, ada_w[layer], ada_b[layer])
        ms = adaln(c, ada_w[layer], ada_b[layer])
        hp = modulate(yp, mp[0], mp[1])
        hs = modulate(ys, ms[0], ms[1])
        if kind == 0:
            wts = (mla_wq_a[j], mla_q_norm[j], mla_wq_b[j], mla_wkv_a[j], mla_kv_norm[j], mla_wkv_b[j], mla_wo[j])
            op, ckv, kpe = mla_context(hp, *wts)
            os_ = mla_latent(hs, cache_ckv[:, j], cache_kpe[:, j], cos, sin, *wts)
            new_ckv.append(ckv)
            new_kpe.append(kpe)
        elif kind == 1:
            wts = (rwkv_mu[j], rwkv_wr[j], rwkv_wk[j], rwkv_wv[j], rwkv_w0[j], rwkv_w1[j], rwkv_w2[j],
                   rwkv_a0[j], rwkv_a1[j], rwkv_a2[j], rwkv_g1[j], rwkv_g2[j], rwkv_k_k[j], rwkv_k_a[j],
                   rwkv_r_k[j], rwkv_lnx_g[j], rwkv_lnx_b[j], rwkv_wo[j])
            zeros = jnp.zeros((yp.shape[0], RWKV_HEADS, RWKV_HEAD, RWKV_HEAD), jnp.float32)
            op, s_f, s_b = rwkv7_bidir(hp, zeros, zeros, *wts)
            os_, _, _ = rwkv7_bidir(hs, state_wkv[:, j, 0], state_wkv[:, j, 1], *wts)
            new_wkv.append(jnp.stack([s_f, s_b], axis=1).astype(yp.dtype))
        else:
            op = multiscale_pool(hp, pool_w[j], pool_scale[j])
            os_ = multiscale_pool(hs, pool_w[j], pool_scale[j])
        yp = layer_norm(ALPHA * yp + mp[2] * op, ln_g[layer, 0], ln_b[layer, 0])
        ys = layer_norm(ALPHA * ys + ms[2] * os_, ln_g[layer, 0], ln_b[layer, 0])
        fp = swiglu(modulate(yp, mp[3], mp[4]), ffn_wg[layer], ffn_wu[layer], ffn_wd[layer])
        fs = swiglu(modulate(ys, ms[3], ms[4]), ffn_wg[layer], ffn_wu[layer], ffn_wd[layer])
        yp = layer_norm(ALPHA * yp + mp[5] * fp, ln_g[layer, 1], ln_b[layer, 1])
        ys = layer_norm(ALPHA * ys + ms[5] * fs, ln_g[layer, 1], ln_b[layer, 1])
    return (yp, ys, jnp.stack(new_ckv, axis=1), jnp.stack(new_kpe, axis=1), jnp.stack(new_wkv, axis=1))


_drawn_inputs = setup_inputs


def setup_inputs(seed=0):
    import zlib

    import numpy as np

    out = dict(_drawn_inputs(seed))
    spreads = {}
    factors = {'cache_ckv': 7.492,
     'cache_kpe': 8.0,
     'state_wkv': 8.0,
     'mla_q_norm': 8.0,
     'rwkv_lnx_g': 6.398,
     'rwkv_lnx_b': 8.0,
     'pool_scale': 3.048}
    for name, (base, spread) in spreads.items():
        noise = np.random.default_rng([zlib.crc32(name.encode()), seed]).standard_normal(out[name].shape)
        drawn = base * np.exp(spread * noise) if base else spread * noise
        out[name] = __import__('jax').numpy.asarray(drawn.astype(out[name].dtype))
    for name, factor in factors.items():
        out[name] = (out[name] * factor).astype(out[name].dtype)
    return out
```

```python
from collections import namedtuple
from contextlib import ExitStack

import numpy as np

import concourse.bass as bass
from concourse import mybir

F32 = mybir.dt.float32
F32R = mybir.dt.float32r
U32 = mybir.dt.uint32
ALU = mybir.AluOpType
ACT = mybir.ActivationFunctionType
AX = mybir.AxisListType

P = 128
D = 1024
KD = D // P
TS, TP = 512, 128
T = TS + TP
HT = T // 2
DEPTH = 4
PAST = 128
GRID_W = 64
HEADS = 16
QR, KVR = 384, 256
NOPE, ROPE, VD = 64, 32, 64
FF = 2816
NF = FF // P
FHALF = (12, 10)
ALPHA = (2 * DEPTH) ** 0.25
LN_EPS, RMS_EPS, GN_EPS = 1e-5, 1e-6, 64e-5
SM_SCALE = float(NOPE + ROPE) ** -0.5
KAPPA = float(np.exp(-0.5))
WINDOWS = (2, 4, 8, 16)
NCH = TS // P + 1
KEYS = PAST + T
CH = 8
RAW, RS = 3, 4
MIXER = [i % 3 for i in range(DEPTH)]
ADA_SLOTS, ADA_EARLY = 6, 3
FFN_WORDS = (2 * KD + 2 * FHALF[0] + 6) * T
GROUPS = [(d, h) for h in range(2) for d in range(2)]
LEVELS = 6

C_MLA_IN, C_MLA_V, C_MLA_HEADS, C_OUT = 6, 2, HEADS // 2, KD
C_RWKV_LORA, C_RWKV_UP, C_RWKV_RKV = 3, 5, 24
C_POOL = 2
C_FFN = (NF * 2 * KD + NF * KD) // CH
C_MIX = [C_MLA_IN + C_MLA_V + C_MLA_HEADS + C_OUT, C_RWKV_LORA + C_RWKV_UP + C_RWKV_RKV + C_OUT, C_POOL]
LAYER_BASE = [0]
for _l in range(DEPTH):
    LAYER_BASE.append(LAYER_BASE[-1] + C_MIX[MIXER[_l]] + C_FFN)
NCHUNK = LAYER_BASE[-1]
RW_CHAIN = 57

_CST = {}
_n = 0
for _k, _w in (("ident", 128), ("ones", 128), ("blk", 128), ("hsel", 2), ("lnp", DEPTH * 2 * 2 * KD),
               ("adab", DEPTH * 48), ("qn", 2 * 3), ("kvn", 2 * 2), ("mu", 6 * KD), ("psc", KD), ("rw", KD * 7),
               ("cond", 2 * KD)):
    _CST[_k] = (_n, _n + _w)
    _n += _w
NCST = _n

class Chain:

    def __init__(self, eng, sem):
        self.eng, self.sem, self.n, self.loop = eng, sem, 0, None

    def enter(self, i, per):
        self.loop, self.start = (i, per), self.n

    def leave(self, iters):
        i, per = self.loop
        assert self.n - self.start == per, (self.n - self.start, per)
        self.n, self.loop = self.start + per * iters, None

    def __call__(self, ins):
        self.n += 1
        ins.then_inc(self.sem, 1)
        self.eng.wait_ge(self.sem, self.n if self.loop is None else self.loop[0] * self.loop[1] + self.n)

class Weights:

    def __init__(self, pe, hi, lo, split, used):
        self.pe, self.hi, self.lo, self.split, self.used = pe, hi, lo, split, used
        self.tile, self.loop, self.owed = 0, None, False

    def enter(self, i, per):
        self.loop, self.start = (i, per), self.tile

    def leave(self, iters):
        i, per = self.loop
        assert self.tile - self.start == per * CH
        self.tile, self.loop = self.start + per * iters * CH, None

    def next(self, n=1):
        c, k = divmod(self.tile, CH)
        if k == 0:
            w = c + 1
            self.pe.wait_ge(self.split, w if self.loop is None else self.loop[0] * self.loop[1] + w)
            self.owed = c > 0
        self.tile += n
        s = c % RS
        return self.hi[:, s, k * P:(k + n) * P], self.lo[:, s, k * P:(k + n) * P]

    def first(self, ins):
        if self.owed:
            ins.then_inc(self.used, 1)
            self.owed = False

def build(nc, a, o):
    ctx = ExitStack()
    with ctx:
        def sb(name, shape, dt=F32, st=None):
            return (st or ctx).enter_context(nc.sbuf_tensor(name, shape, dt))

        def sem(name):
            return ctx.enter_context(nc.semaphore(name))

        def halves(t):
            return t.rearrange("p (h t) -> p h t", h=2)

        x = sb("x", [P, KD, T])
        raw = sb("w_raw", [P, RAW, CH * P])
        whi = sb("w_hi", [P, RS, CH * P], F32R)
        wlo = sb("w_lo", [P, RS, CH * P], F32R)
        zrow = sb("zrow", [P, 1])
        cst = sb("cst", [P, NCST])
        mod = sb("mod", [P, 48, 2])
        eps = sb("eps", [P, 4])
        sc_c = sb("silu_c", [P, KD, 2])
        ps = ctx.enter_context(nc.psum_tensor("ps", [P, 8, 512], F32))

        def C(k):
            return cst[:, _CST[k][0]:_CST[k][1]]
        ident, ones = C("ident"), C("ones")
        lnp = C("lnp").rearrange("p (l s g k) -> p l s g k", l=DEPTH, s=2, g=2)
        adab = C("adab").rearrange("p (l n) -> p l n", l=DEPTH)
        mu_c = C("mu").rearrange("p (i k) -> p i k", i=6)
        psc = C("psc")
        rwp = C("rw").rearrange("p (j n) -> p j n", j=KD)
        cond = C("cond").rearrange("p (k c) -> p k c", c=2)

        def pair(b, n=HT, m=P):
            return ps[0:m, 2 * b:2 * b + 2, 0:n]

        PIECES = ((0, 0, HT, 0), (1, 0, TS - HT, 0), (1, TS - HT, HT, 1))

        w_land = [sem(f"w_land{i}") for i in range(RAW)]
        w_split = sem("w_split")
        w_hi_done = sem("w_hi_done")
        w_used = sem("w_used")
        chain_dve, chain_act = sem("chain_dve"), sem("chain_act")
        stage_end = sem("stage_end")
        stage_free = sem("stage_free")
        s_init, s_const = sem("s_init"), sem("s_const")
        ada_land = [sem(f"ada_land{i}") for i in range(ADA_SLOTS)]
        ada_mm, ada_row = sem("ada_mm"), sem("ada_row")
        outs_done = sem("outs_done")

        class M:
            pass

        def scope(fill):
            m = M()
            with ExitStack() as st:
                fill(m, lambda n, s, dt=F32: sb(n, s, dt, st))
            return m

        def f_ada(L):
            def f(m, g):
                m.rows = g(f"ada_rows{L}", [2, 6 * D])
                low = [g(f"ada_ring{L}_{i}", [P, 4, 512]) for i in range(ADA_EARLY, ADA_SLOTS)]
                g(f"ada_gap{L}", [P, FFN_WORDS - 6 * D - (ADA_SLOTS - ADA_EARLY) * 2048])
                m.ring = [g(f"ada_ring{L}_{i}", [P, 4, 512]) for i in range(ADA_EARLY)] + low
            return f

        def f_ffn(L):
            def f(m, g):
                m.hhi, m.hlo = g(f"f_hhi{L}", [P, KD, T], F32R), g(f"f_hlo{L}", [P, KD, T], F32R)
                m.t32 = g(f"f_t32{L}", [P, 2, T])
                m.sil, m.a32 = g(f"f_sil{L}", [P, 2, T]), g(f"f_a32{L}", [P, 2, T])
                m.ahi, m.alo = g(f"f_ahi{L}", [P, FHALF[0], T], F32R), g(f"f_alo{L}", [P, FHALF[0], T], F32R)
            return f

        def f_ln(t):
            def f(m, g):
                m.sq = g(f"ln_sq{t}", [P, KD, T])
                m.rs = g(f"ln_rs{t}", [P, T])
            return f

        def f_mla(L):
            def f(m, g):
                m.hhi, m.hlo = g(f"m_hhi{L}", [P, KD, T], F32R), g(f"m_hlo{L}", [P, KD, T], F32R)
                m.t32 = g(f"m_t32{L}", [P, 2, T])
                m.tab, m.dup = g(f"m_tab{L}", [P, 3, T]), g(f"m_dup{L}", [P, P])
                m.qhi, m.qlo = g(f"m_qhi{L}", [P, 3, T], F32R), g(f"m_qlo{L}", [P, 3, T], F32R)
                m.khi, m.klo = g(f"m_khi{L}", [P, 2, KEYS], F32R), g(f"m_klo{L}", [P, 2, KEYS], F32R)
                m.K = g(f"m_K{L}", [P, 2, KEYS])
                with ExitStack() as e:
                    h = lambda n, s, dt=F32: sb(n, s, dt, e)
                    m.q32 = h(f"m_q32{L}", [P, 3, T])
                    m.c32 = h(f"m_c32{L}", [P, 2, KEYS])
                    m.sq = h(f"m_sq{L}", [P, 3, T])
                    m.rs = h(f"m_rs{L}", [P, 2, T])
                    m.kraw = h(f"m_kraw{L}", [P, T])
                m.V = g(f"m_V{L}", [P, 6, D])
                m.Q = g(f"m_Q{L}", [P, 2, T])
                m.pr = g(f"m_P{L}", [P, 2, T])
                m.pt = g(f"m_PT{L}", [P, 2, T])
                m.O = g(f"m_O{L}", [P, 5, P])
                m.nm = g(f"m_nm{L}", [P, 4, 2])
                m.rc = g(f"m_rc{L}", [P, 4])
                m.mx = g(f"m_mx{L}", [P, 2])
            return f

        def f_rwa(m, g):
            m.hid = {k: (g(f"r_{k}hi", [P, T], F32R), g(f"r_{k}lo", [P, T], F32R)) for k in "wag"}
            m.hset = [(g(f"r_hhi{i}", [P, KD, T], F32R), g(f"r_hlo{i}", [P, KD, T], F32R)) for i in range(2)]
            m.t32 = g("r_t32", [P, 2, T])
            m.xx = g("r_xx", [P, KD, T])
            m.o32 = g("r_o32", [P, 2, T])

        def f_rwb(m, g):
            m.par = g("s_par", [P, 7])
            m.LR = g("s_LR", [P, 5, T])
            m.r, m.k, m.v = g("s_r", [P, T]), g("s_k", [P, T]), g("s_v", [P, NCH, P])
            m.S0 = g("s_S0", [P, 2, P])
            m.lnx = g("s_lnx", [P, 2, P])
            m.kk, m.t1, m.t2 = g("s_kk", [P, T]), g("s_t1", [P, T]), g("s_t2", [P, T])
            m.PS, m.D1, m.D2 = g("s_PS", [P, T]), g("s_D1", [P, T]), g("s_D2", [P, T])
            m.onesT = g("s_ones", [P, P])
            m.E = g("s_E", [P, 3, T])
            m.F = g("s_F", [P, 2, 2, NCH])
            m.Fi = g("s_Fi", [P, 2, NCH])
            m.Fc = g("s_Fc", [P, 2, NCH])
            m.AR = [g(f"s_AR{d}", [P, NCH, 2, P]) for d in range(2)]
            m.BT = [g(f"s_BT{d}", [P, T]) for d in range(2)]
            m.KT = [g(f"s_KT{d}", [P, T]) for d in range(2)]
            m.kds = g("s_kds", [P, T])
            m.AM = [[g(f"s_AM{d}{b}", [P, 2, 512]) for b in range(2)] for d in range(2)]
            m.X, m.XT, m.XF = ([g(f"s_{n}{d}", [P, 256]) for d in range(2)] for n in ("X", "XT", "XF"))
            m.Y = [g(f"s_Y{d}", [P, 256]) for d in range(2)]
            m.BK = [[g(f"s_BK{d}{b}", [P, 256]) for b in range(2)] for d in range(2)]
            m.R = [g(f"s_R{d}", [P, P]) for d in range(2)]
            m.U = [g(f"s_U{d}", [P, P]) for d in range(2)]
            m.S = [g(f"s_Sc{d}", [P, P]) for d in range(2)]
            m.So = [g(f"s_So{d}", [P, P]) for d in range(2)]
            m.st, m.pad = g("s_st", [P, 2, P]), g("s_pad", [P, 2])
            m.yd = [g(f"s_y{d}", [P, NCH, P]) for d in range(2)]
            m.y2 = g("s_y2", [P, NCH, P])
            m.mu, m.var = g("s_mu", [P, NCH * 2]), g("s_var", [P, NCH * 2])
            m.bon = g("s_bon", [P, NCH * 2])
            m.z = g("s_z", [P, T])
            m.pm = g("s_pm", [P, 2, 512])
            m.lm = g("s_lm", [P, 2, LEVELS + 1, P])
            m.i2 = g("s_i2", [P, 256])

        def f_rwc(m, g):
            m.hhi, m.hlo = g("t_hhi", [P, KD, T], F32R), g("t_hlo", [P, KD, T], F32R)
            m.z32 = g("t_z32", [P, KD, T])

        def f_pool(m, g):
            m.hhi, m.hlo = g("p_hhi", [P, KD, T], F32R), g("p_hlo", [P, KD, T], F32R)
            m.t32 = g("p_t32", [P, 2, T])
            m.hp = g("p_hp", [P, 2, T + 64])
            m.b = g("p_b", [P, 2, T + 64])
            m.cnt = g("p_cnt", [P, 4, T])
            m.gs = g("p_gs", [P, KD, 2])

        m_ada = [scope(f_ada(L)) for L in range(DEPTH)]
        m_ffn = [scope(f_ffn(L)) for L in range(DEPTH)]
        m_ln = [scope(f_ln(t)) for t in range(2 * DEPTH)]
        m_mla = {L: scope(f_mla(L)) for L in range(DEPTH) if MIXER[L] == 0}
        m_rwa, m_rwb, m_rwc, m_pool = scope(f_rwa), scope(f_rwb), scope(f_rwc), scope(f_pool)

        r_d = nc.dram_tensor("r_scratch", (KD, P, T), F32, kind="Internal").ap()
        k_d = nc.dram_tensor("k_scratch", (KD, P, T), F32, kind="Internal").ap()
        v_d = nc.dram_tensor("v_scratch", (NCH, P, D), F32, kind="Internal").ap()
        up_d = nc.dram_tensor("up_scratch", (KD, 5, P, T), F32, kind="Internal").ap()
        x_d = nc.dram_tensor("x_scratch", (KD, P, T), F32, kind="Internal").ap()
        z_d = nc.dram_tensor("z_scratch", (KD, P, T), F32, kind="Internal").ap()

        def sems(tag, names):
            return namedtuple("Sems", names)(*[sem(f"{tag}_{n}") for n in names.split()])

        def uses(tag, counts, n, primed=()):
            q = sems(tag, " ".join(counts))
            at = namedtuple("At", list(counts))
            use = namedtuple("Use", ["at", *counts])
            return [use(at(*[(k in primed) + u * v for k, v in counts.items()]), *q) for u in range(n)]

        splits = [t for t in range(2 * DEPTH) if t % 2 or MIXER[t // 2] != 1]
        q_split = dict(zip(splits, uses("split", dict(val=KD, hi=KD, lo=KD), len(splits))))
        q_ln = uses("ln", dict(mean=1, cen=KD, sq=KD, var=1), 2 * DEPTH)
        q_ffn = uses("ffn", dict(mm=NF, sil=NF, act=NF, hi=NF, lo=NF, down=2 * KD, upd=2 * KD), DEPTH)
        q_out = uses("out", dict(mm=KD, upd=KD), DEPTH)
        q_mla = dict(zip(m_mla, uses("mla", dict(
            tab=112, in_mm=6, in_ev=6, st=2, v_mm=15, v_ev=12, head_mm=24, q_ev=16, k_ev=16, sc=80, nmax=80, pexp=80, tr=80,
            ptc=80, av=80, oev=80, ot=40, ohi=40, olo=40, cd=3, rsd=1, hi2=2, rec=80, mx=80), len(m_mla), ("oev", "olo"))))
        q_rwa = sems("rwa", "val hi lo mm ev hid hidlo st xst")
        s_rst = [sem("rwa_store0"), sem("rwa_store1")]
        q_rwb = sems("rwb", "ld kksq nrm nr dec ex til sc0 sc1 x10 x11 tok0 tok1 inv0 inv1 x0 x1 r0 r1 rev0 rev1 "
                            "t0 t1 tev0 tev1 u0 u1 uev0 uev1 y0 y1 yev0 yev1 S0 S1 sqy rsd prod bon zt z zst st")
        q_pool = sems("pool", "cst st hp")

        class Ends:

            def __init__(self, eng):
                self.eng, self.n = eng, 0

            def __call__(self):
                self.n += 1
                self.eng.drain().then_inc(stage_end, 1)
                self.eng.wait_ge(stage_end, 3 * self.n)

        ENDS_OF_MIXER = [4, 4, 2]

        def ends_of_layers(L):
            return 1 + sum(2 + ENDS_OF_MIXER[MIXER[l]] + 2 + 1 + 2 for l in range(L))

        block = ctx.enter_context(nc.Block())

        @block.sync
        def _(sp):
            sp.dma_start(cst[:, :], a["cst"]).then_inc(s_const, 16)
            sp.dma_start(x[:, :, :], a["x"].rearrange("k p t -> p k t")).then_inc(s_const, 16)
            done = 0

            def chunk(slot, n, src, wait):
                if wait is not None:
                    sp.wait_ge(w_split, wait)
                sp.dma_start(raw[:, slot, :], src).then_inc(w_land[slot], 16)

            def stream(first, last):
                n = first
                while n < last:
                    loops = (last - n) // RAW
                    if n >= RAW and n % RAW == 0 and loops > 1:
                        with sp.Fori(0, loops) as i:
                            for u in range(RAW):
                                chunk(u, n, a["w"][i * RAW + (n + u)], i * RAW + (n + u - RAW + 1))
                        n += loops * RAW
                    else:
                        chunk(n % RAW, n, a["w"][n], n - RAW + 1 if n >= RAW else None)
                        n += 1

            for L in range(DEPTH):
                src = a["ada_w"][L].rearrange("(k p) n -> p k n", p=P)
                for u in range(24):
                    unit, slot = 24 * L + u, u % ADA_SLOTS
                    if L and u == 0:
                        sp.wait_ge(stage_end, 3 * (ends_of_layers(L) - 5))
                    if L and u == ADA_EARLY:
                        sp.wait_ge(stage_end, 3 * ends_of_layers(L))
                    if u >= ADA_SLOTS:
                        sp.wait_ge(ada_mm, unit - ADA_SLOTS + 1)
                    sp.dma_start(m_ada[L].ring[slot][:, :, :],
                                 src[:, 4 * (u % 2):4 * (u % 2) + 4, (u // 2) * 512:(u // 2 + 1) * 512]
                                 ).then_inc(ada_land[slot], 16)
                stream(LAYER_BASE[L], LAYER_BASE[L + 1])

        @block.gpsimd
        def _(pool):
            nc.gpsimd.memset(zrow[:, :], 0.0).then_inc(s_init, 1)
            pool.wait_ge(s_init, 1)

            def split(raw_slot, slot, land, used, n1):
                pool.wait_ge(w_land[raw_slot], land)
                if used is not None:
                    pool.wait_ge(w_used, used)
                nc.gpsimd.tensor_tensor(whi[:, slot, :], raw[:, raw_slot, :], zrow[:, 0:1].to_broadcast([P, CH * P]), ALU.add).then_inc(w_hi_done, 1)
                pool.wait_ge(w_hi_done, n1)
                nc.gpsimd.tensor_tensor(wlo[:, slot, :], raw[:, raw_slot, :], whi[:, slot, :].bitcast(F32),
                                        ALU.subtract).then_inc(w_split, 1)

            body = RAW * RS
            n = 0
            for n in range(body):
                split(n % RAW, n % RS, 16 * (n // RAW + 1), n - RS + 1 if n >= RS else None, n + 1)
            loops = (NCHUNK - body) // body
            with pool.Fori(1, loops + 1) as i:
                for u in range(body):
                    split(u % RAW, u % RS, i * (16 * RS) + 16 * (u // RAW + 1), i * body + (u - RS + 1), i * body + (u + 1))
            for n in range(body * (loops + 1), NCHUNK):
                split(n % RAW, n % RS, 16 * (n // RAW + 1), n - RS + 1, n + 1)

        @block.tensor
        def _(pe):
            W = Weights(pe, whi, wlo, w_split, w_used)
            end = Ends(pe)
            mm = nc.tensor.matmul

            def panel(KT, hi, lo, b):
                for kt in range(KT):
                    wh, wl = W.next()
                    n = 0
                    for w, r in ((wh, hi(kt)), (wl, hi(kt)), (wh, lo(kt))):
                        for h in range(2):
                            last = mm(ps[:, 2 * b + h, 0:HT], w, r[:, h * HT:(h + 1) * HT],
                                      start=kt == 0 and n < 2, stop=kt == KT - 1 and n >= 4)
                            W.first(last)
                            n += 1
                return last

            def ada(L):
                m = m_ada[L]
                for cb in range(12):
                    g = 12 * L + cb
                    if cb >= 2:
                        pe.wait_ge(ada_row, g - 1)
                    for kh in range(2):
                        unit = 2 * g + kh
                        pe.wait_ge(ada_land[unit % ADA_SLOTS], 16 * (unit // ADA_SLOTS + 1))
                        for k in range(4):
                            last = mm(ps[0:2, cb % 2, :], sc_c[:, 4 * kh + k, :], m.ring[unit % ADA_SLOTS][:, k, :],
                                      start=kh == 0 and k == 0, stop=kh == 1 and k == 3)
                        last.then_inc(ada_mm, 1)
                pe.wait_ge(ada_row, 12 * (L + 1))
                for n in range(48):
                    mm(ps[:, 2, 2 * n:2 * n + 2], m.rows[0:2, n * P:(n + 1) * P], ident[0:2, 0:2], start=True, stop=True)
                end()
                end()

            def norm(t):
                m, q = m_ln[t], q_ln[t]
                for kt in range(KD):
                    for h in range(2):
                        last = mm(ps[:, h, 0:HT], ones, x[:, kt, h * HT:(h + 1) * HT], start=kt == 0, stop=kt == KD - 1)
                last.then_inc(q.mean, 1)
                for kt in range(KD):
                    pe.wait_ge(q.sq, q.at.sq + kt + 1)
                    for h in range(2):
                        last = mm(ps[:, 2 + h, 0:HT], ones, m.sq[:, kt, h * HT:(h + 1) * HT], start=kt == 0, stop=kt == KD - 1)
                last.then_inc(q.var, 1)
                end()
                end()

            def ffn(L):
                m, q = m_ffn[L], q_ffn[L]
                pe.wait_ge(q_split[2 * L + 1].lo, q_split[2 * L + 1].at.lo + KD)
                f0, dn = 0, 0
                for nf in FHALF:
                    def gate_up(u, i):
                        if i is not None:
                            pe.wait_ge(q.act, q.at.act + i * 2 + (f0 + u - 1))
                        elif f0 + u >= 2:
                            pe.wait_ge(q.act, q.at.act + f0 + u - 1)
                        panel(KD, lambda k: m.hhi[:, k, :], lambda k: m.hlo[:, k, :], 2 * (u % 2))
                        panel(KD, lambda k: m.hhi[:, k, :], lambda k: m.hlo[:, k, :], 2 * (u % 2) + 1).then_inc(q.mm, 1)
                    if f0:
                        pe.wait_ge(q.upd, q.at.upd + dn)
                    gate_up(0, None)
                    gate_up(1, None)
                    with pe.Fori(0, nf // 2 - 1) as i:
                        W.enter(i, 4)
                        gate_up(2, i)
                        gate_up(3, i)
                        W.leave(nf // 2 - 1)
                    f0 += nf
                    pe.wait_ge(q.act, q.at.act + f0)
                    pe.wait_ge(q.lo, q.at.lo + f0)
                    for c in range(KD):
                        if c >= 4:
                            pe.wait_ge(q.upd, q.at.upd + dn - 3)
                        panel(nf, lambda k: m.ahi[:, k, :], lambda k: m.alo[:, k, :], c % 4).then_inc(q.down, 1)
                        dn += 1
                end()

            def out_proj(L, hhi, hlo):
                q = q_out[L]
                for c in range(KD):
                    if c >= 4:
                        pe.wait_ge(q.upd, q.at.upd + c - 3)
                    panel(KD, lambda k: hhi[:, k, :], lambda k: hlo[:, k, :], c % 4).then_inc(q.mm, 1)
                end()

            def mla(L):
                m, q = m_mla[L], q_mla[L]
                pe.wait_ge(q_split[2 * L].lo, q_split[2 * L].at.lo + KD)
                for p in range(6):
                    if p >= 4:
                        pe.wait_ge(q.in_ev, q.at.in_ev + p - 3)
                    panel(KD, lambda k: m.hhi[:, k, :], lambda k: m.hlo[:, k, :], p % 4).then_inc(q.in_mm, 1)
                pe.wait_ge(q.in_ev, q.at.in_ev + 6)
                pe.wait_ge(q.st, q.at.st + 1)
                for kt in range(3):
                    for h in range(2):
                        last = mm(ps[:, h, 0:HT], ones, m.sq[:, kt, h * HT:(h + 1) * HT], start=kt == 0, stop=kt == 2)
                last.then_inc(q.v_mm, 1)
                pe.wait_ge(q.st, q.at.st + 2)
                for kt in range(2):
                    for h in range(2):
                        last = mm(ps[:, 2 + h, 0:HT], ones, m.sq[:, kt, h * HT:(h + 1) * HT], start=kt == 0, stop=kt == 1)
                last.then_inc(q.v_mm, 1)
                for h in range(2):
                    last = mm(ps[:, 4 + h, 0:HT], m.dup[0:64, :], m.kraw[0:64, h * HT:(h + 1) * HT], start=True, stop=True)
                last.then_inc(q.v_mm, 1)
                end()
                ch = [W.next(8)]
                held = W.owed
                ch.append(W.next(8))
                assert held
                n = 0
                for kb in range(6):
                    for h in range(2):
                        if n >= 4:
                            pe.wait_ge(q.v_ev, q.at.v_ev + n - 3)
                        i = 0
                        for kt in range(2):
                            wh, wl = ch[kt]
                            khi, klo = m.khi[:, kt, kb * P:(kb + 1) * P], m.klo[:, kt, kb * P:(kb + 1) * P]
                            for l, r in ((khi, wh), (klo, wh), (khi, wl)):
                                last = mm(ps[:, n % 4, :], l, r[:, h * 512:(h + 1) * 512], start=i == 0, stop=i == 5)
                                W.first(last)
                                i += 1
                        last.then_inc(q.v_mm, 1)
                        n += 1
                pe.drain().then_inc(w_used, 1)
                end()
                with pe.Fori(0, 2) as j4:
                  W.enter(j4, 4)
                  for ju in range(4):
                    j = j4 * 4 + ju
                    pe.wait_ge(q.oev, q.at.oev + j * 10)
                    pe.wait_ge(q.olo, q.at.olo + j * 5)
                    for hh in range(2):
                        panel(3, lambda k: m.qhi[:, k, :], lambda k: m.qlo[:, k, :], hh).then_inc(q.head_mm, 1)
                    for kt in range(2):
                        wh, wl = W.next()
                        n = 0
                        for w, r in ((wh, m.khi), (wl, m.khi), (wh, m.klo)):
                            for h in range(2):
                                last = mm(ps[:, 4 + h, 0:KEYS // 2], w, r[:, kt, h * (KEYS // 2):(h + 1) * (KEYS // 2)],
                                          start=kt == 0 and n < 2, stop=kt == 1 and n >= 4)
                                W.first(last)
                                n += 1
                    last.then_inc(q.head_mm, 1)

                    def scores(u):
                        hh, qt = divmod(u, 5)
                        if u < 2:
                            pe.wait_ge(q.q_ev, q.at.q_ev + j * 2 + 2)
                            pe.wait_ge(q.k_ev, q.at.k_ev + j * 2 + 2)
                        else:
                            pe.wait_ge(q.pexp, q.at.pexp + j * 10 + (u - 1))
                        k0, nk = (0, T) if qt < 4 else (T, P)
                        b = 2 * (u % 2)
                        if nk == P:
                            last = mm(ps[:, b, 0:P], m.Q[:, hh, qt * P:(qt + 1) * P], m.K[:, hh, k0:k0 + P], start=True, stop=True)
                        else:
                            for h in range(2):
                                last = mm(ps[:, b + h, 0:HT], m.Q[:, hh, qt * P:(qt + 1) * P],
                                          m.K[:, hh, h * HT:(h + 1) * HT], start=True, stop=True)
                        last.then_inc(q.sc, 1)

                    def turn(u):
                        hh, qt = divmod(u, 5)
                        pe.wait_ge(q.pexp, q.at.pexp + j * 10 + (u + 1))
                        if u >= 1:
                            pe.wait_ge(q.ptc, q.at.ptc + j * 10 + u)
                        for kb in range(5 if qt < 4 else 1):
                            last = nc.tensor.transpose(ps[:, 4 + kb // 4, (kb % 4) * P:(kb % 4 + 1) * P],
                                                       m.pr[:, u % 2, kb * P:(kb + 1) * P], ident)
                        last.then_inc(q.tr, 1)

                    def av(u):
                        hh, qt = divmod(u, 5)
                        pe.wait_ge(q.ptc, q.at.ptc + j * 10 + (u + 1))
                        if u >= 1:
                            pe.wait_ge(q.oev, q.at.oev + j * 10 + u)
                        nk = 5 if qt < 4 else 1
                        for kb in range(nk):
                            kt = kb if qt < 4 else 5
                            last = mm(ps[:, 6, 0:64], m.pt[:, u % 2, kb * P:(kb + 1) * P],
                                      m.V[:, kt, bass.ds(j * P + hh * 64, 64)], start=kb == 0, stop=kb == nk - 1)
                        last.then_inc(q.av, 1)

                    scores(0)
                    for u in range(11):
                        if u < 9:
                            scores(u + 1)
                        if u < 10:
                            turn(u)
                        if u:
                            av(u - 1)
                    for qt in range(5):
                        pe.wait_ge(q.oev, q.at.oev + j * 10 + 10)
                        if qt >= 1:
                            pe.wait_ge(q.olo, q.at.olo + j * 5 + qt)
                        nc.tensor.transpose(ps[:, 7, 0:P], m.O[:, qt, :], ident).then_inc(q.ot, 1)
                  W.leave(2)
                pe.wait_ge(q.olo, q.at.olo + 5 * (HEADS // 2))
                end()
                out_proj(L, m.hhi, m.hlo)

            def rwkv(L):
                m, q = m_rwa, q_rwa
                n = 0

                def groups(hi, lo, count, KT=KD):
                    nonlocal n
                    for c in range(count):
                        if n >= 4:
                            pe.wait_ge(q.ev, n - 3)
                        panel(KT, lambda k: hi(c, k), lambda k: lo(c, k), n % 4).then_inc(q.mm, 1)
                        n += 1

                for idx in range(6):
                    hi, lo = m.hset[idx % 2]
                    pe.wait_ge(q.lo, KD * (idx + 1))
                    if idx < 5:
                        groups(lambda c, k: hi[:, k, :], lambda c, k: lo[:, k, :], 1 if idx < 3 else KD)
                        if idx == 2:
                            pe.wait_ge(q.hidlo, 3)
                            groups(lambda c, k: m.hid["wwaag"[c % 5]][0][:, :], lambda c, k: m.hid["wwaag"[c % 5]][1][:, :],
                                   5 * KD, 1)
                    else:
                        pe.wait_ge(q.ev, n)
                        for h in range(2):
                            if h:
                                pe.wait_ge(q.ev, n + 5)
                            for kt in range(KD):
                                wh, wl = W.next(4)
                                for tt in range(NCH):
                                    t0 = tt * P
                                    for p, (l, r) in enumerate(((hi, wh), (lo, wh), (hi, wl))):
                                        last = mm(ps[:, tt, :], l[:, kt, t0:t0 + P], r, start=kt == 0 and p == 0,
                                                  stop=kt == KD - 1 and p == 2)
                                        W.first(last)
                            last.then_inc(q.mm, 1)
                end()
                m, q = m_rwb, q_rwb
                sc, x1, tok, inv, xs = (q.sc0, q.sc1), (q.x10, q.x11), (q.tok0, q.tok1), (q.inv0, q.inv1), (q.x0, q.x1)
                rr, rev, uu, uev = (q.r0, q.r1), (q.rev0, q.rev1), (q.u0, q.u1), (q.uev0, q.uev1)
                yy, yev, SS = (q.y0, q.y1), (q.yev0, q.yev1), (q.S0, q.S1)
                tt_, tev = (q.t0, q.t1), (q.tev0, q.tev1)
                with pe.Fori(0, KD) as j:
                    pe.wait_ge(q.zt, j * 2 + 1)
                    pe.wait_ge(q.kksq, j + 1)
                    for h in range(2):
                        last = mm(ps[:, 2 + h, 0:HT], C("blk"), m.t1[:, h * HT:(h + 1) * HT], start=True, stop=True)
                    last.then_inc(q.nrm, 1)
                    pe.wait_ge(q.nr, j + 1)
                    def scores(s):
                        for d in range(2):
                            c = chunk_of(d, s)
                            if s == 0:
                                pe.wait_ge(q.til, j * 2 + (d + 1))
                            else:
                                pe.wait_ge(xs[d], j * 130 + 26 * s)
                                if s >= 2:
                                    pe.wait_ge(yev[d], j * 5 + (s - 1))
                            for hh in range(2):
                                rows = slice(64 * hh, 64 * hh + 64)
                                rhs = m.AR[d][rows, c, :, :].rearrange("p a t -> p (a t)")
                                mm(ps[:, 4 * d + hh, 0:256], m.BT[d][rows, c * P:(c + 1) * P], rhs, start=True, stop=True)
                                mm(ps[:, 4 * d + hh, 256:512], m.KT[d][rows, c * P:(c + 1) * P], rhs, start=True, stop=True)
                            nc.tensor.transpose(ps[:, 4 * d + 2, 0:P], m.BT[d][:, c * P:(c + 1) * P], ident)
                            nc.tensor.transpose(ps[:, 4 * d + 2, P:2 * P], m.KT[d][:, c * P:(c + 1) * P], ident).then_inc(sc[d], 1)

                    def start_inverse(s):
                        for d, hh in GROUPS:
                            pe.wait_ge(x1[d], j * 5 + (s + 1))
                            nc.tensor.transpose(ps[:, 4 * d + hh, 0:P], m.XT[d][:, hh * P:(hh + 1) * P], ident).then_inc(inv[d], 1)

                    def level_a(s, l):
                        for d, hh in GROUPS:
                            X = m.X[d][:, hh * P:(hh + 1) * P]
                            pe.wait_ge(xs[d], j * 130 + (26 * s + 4 * l - 3 + hh))
                            mm(ps[:, 4 * d + hh, 0:P], m.AM[d][s % 2][:, hh, 0:P], X, start=True, stop=True).then_inc(inv[d], 1)
                            if l > 1:
                                if l == 2 and hh and s == 0:
                                    pe.wait_ge(tok[d], j * 5 + 1)
                                elif l == 2 and hh:
                                    pe.wait_ge(yev[d], j * 5 + s)
                                elif l == 2 and s:
                                    pe.wait_ge(SS[d], j * 6 + (s + 1))
                                nc.tensor.transpose(ps[:, 4 * d + 3 - hh, 0:P], X, ident).then_inc(tt_[d], 1)

                    def level_b(s, l):
                        for d, hh in GROUPS:
                            XT, Y = m.XT[d][:, hh * P:(hh + 1) * P], m.Y[d][:, hh * P:(hh + 1) * P]
                            pe.wait_ge(xs[d], j * 130 + (26 * s + 4 * l - 1 + hh))
                            if l >= 2:
                                pe.wait_ge(tev[d], j * 50 + (10 * s + 2 * l - 3 + hh))
                            w, r = (XT, Y) if l < LEVELS else (Y, XT)
                            mm(ps[:, 4 * d + hh, P:2 * P], w, r, start=True, stop=True).then_inc(inv[d], 1)

                    def rhs(s):
                        for d in range(2):
                            c = chunk_of(d, s)
                            pe.wait_ge(SS[d], j * 6 + (s + 1))
                            pe.wait_ge(tok[d], j * 5 + min(s + 2, NCH))
                            out = ps[:, 4 * d + 2, 256:384]
                            mm(out, m.AR[d][:, c, 0, :], m.S[d][:, :], start=True, stop=False)
                            for hh in range(2):
                                last = mm(out[:, 64 * hh:64 * hh + 64], m.AM[d][s % 2][:, hh, 256:384],
                                          m.v[:, c, 64 * hh:64 * hh + 64], start=False, stop=hh == 1)
                            last.then_inc(rr[d], 1)

                    def solve(s):
                        for d in range(2):
                            pe.wait_ge(rev[d], j * 5 + (s + 1))
                            pe.wait_ge(xs[d], j * 130 + (26 * s + 26))
                            for hh in range(2):
                                last = mm(ps[:, 4 * d + 2, 384 + 64 * hh:448 + 64 * hh], m.XF[d][:, hh * P:(hh + 1) * P],
                                          m.R[d][:, 64 * hh:64 * hh + 64], start=True, stop=True)
                            last.then_inc(uu[d], 1)

                    def output(s):
                        for d in range(2):
                            c = chunk_of(d, s)
                            am, bk = m.AM[d][s % 2], m.BK[d][s % 2]
                            pe.wait_ge(uev[d], j * 5 + (s + 1))
                            out = ps[:, 4 * d + 2, 256:384]
                            mm(out, m.AR[d][:, c, 1, :], m.S[d][:, :], start=True, stop=False)
                            for hh in range(2):
                                half = slice(64 * hh, 64 * hh + 64)
                                mm(out[:, half], am[:, hh, P:2 * P], m.U[d][:, half], start=False, stop=False)
                                mm(out[:, half], am[:, hh, 384:512], m.v[:, c, half], start=False, stop=hh == 1)
                            out = ps[:, 4 * d + 3, 0:P]
                            mm(out, bk[:, 0:P], m.U[d][:, :], start=True, stop=False)
                            last = mm(out, bk[:, P:2 * P], m.v[:, c, :], start=False, stop=True)
                            last.then_inc(yy[d], 1)

                    for s in range(NCH):
                        scores(s)
                        if s:
                            rhs(s - 1)
                        start_inverse(s)
                        level_a(s, 1)
                        if s:
                            solve(s - 1)
                        level_b(s, 1)
                        if s:
                            output(s - 1)
                        for l in range(2, LEVELS + 1):
                            level_a(s, l)
                            level_b(s, l)
                    rhs(NCH - 1)
                    solve(NCH - 1)
                    output(NCH - 1)
                    pe.wait_ge(q.prod, j + 1)
                    pe.wait_ge(q.S0, j * 6 + 6)
                    for c in range(NCH):
                        last = mm(ps[:, 0, 2 * c:2 * c + 2], m.t1[:, c * P:(c + 1) * P], C("hsel"), start=True, stop=True)
                    last.then_inc(q.bon, 1)
                    pe.wait_ge(q.zt, j * 2 + 2)
                    for c in range(NCH):
                        last = nc.tensor.transpose(ps[:, 2 + c // 4, (c % 4) * P:(c % 4 + 1) * P], m.y2[:, c, :], ident)
                    last.then_inc(q.z, 1)
                end()
                end()
                out_proj(L, m_rwc.hhi, m_rwc.hlo)

            def pooling(L):
                m, q = m_pool, q_out[L]
                end()
                for c in range(KD):
                    if c >= 4:
                        pe.wait_ge(q.upd, q.at.upd + c - 3)
                    g = c // 2
                    panel(2, lambda k: m.hhi[:, 2 * g + k, :], lambda k: m.hlo[:, 2 * g + k, :], c % 4).then_inc(q.mm, 1)
                end()

            pe.wait_ge(s_const, 32)
            end()
            for L in range(DEPTH):
                ada(L)
                (mla, rwkv, pooling)[MIXER[L]](L)
                norm(2 * L)
                ffn(L)
                norm(2 * L + 1)

        @block.scalar
        def _(act):
            end = Ends(act)
            ch = Chain(act, chain_act)
            af = nc.scalar.activation

            def ada(L):
                m = m_ada[L]
                for cb in range(12):
                    g = 12 * L + cb
                    act.wait_ge(ada_mm, 2 * g + 2)
                    nc.scalar.copy(m.rows[0:2, cb * 512:(cb + 1) * 512], ps[0:2, cb % 2, :]).then_inc(ada_row, 1)
                end()
                end()

            def split_h(t, L, part, t32, hhi):
                q = q_split[t]
                for kt in range(KD + 1):
                    if kt < KD:
                        if kt >= 2:
                            act.wait_ge(q.lo, q.at.lo + kt - 1)
                        for cd, (t0, t1) in enumerate(((0, TS), (TS, T))):
                            last = af(t32[:, kt % 2, t0:t1], x[:, kt, t0:t1], ACT.Identity,
                                      bias=mod[:, part * KD + kt, cd:cd + 1], scale=mod[:, (part + 1) * KD + kt, cd:cd + 1])
                        last.then_inc(q.val, 1)
                    if kt >= 1:
                        act.wait_ge(q.val, q.at.val + kt)
                        nc.scalar.copy(hhi[:, kt - 1, :], t32[:, (kt - 1) % 2, :]).then_inc(q.hi, 1)

            def norm(t):
                m, q = m_ln[t], q_ln[t]
                for kt in range(KD):
                    act.wait_ge(q.cen, q.at.cen + kt + 1)
                    af(m.sq[:, kt, :], x[:, kt, :], ACT.Square).then_inc(q.sq, 1)
                act.wait_ge(q.var, q.at.var + 1)
                ch(af(halves(m.rs[:, :]), pair(1), ACT.Sqrt, bias=eps[:, 0:1], scale=1.0 / D))
                end()
                end()

            def ffn(L):
                m, q = m_ffn[L], q_ffn[L]
                split_h(2 * L + 1, L, 3, m.t32, m.hhi)
                f0 = 0
                for nf in FHALF:
                    with act.Fori(0, nf // 2) as i:
                        for u in range(2):
                            act.wait_ge(q.mm, q.at.mm + i * 2 + (f0 + u + 1))
                            af(halves(m.sil[:, u, :]), pair(2 * u), ACT.Silu).then_inc(q.sil, 1)
                            act.wait_ge(q.act, q.at.act + i * 2 + (f0 + u + 1))
                            nc.scalar.copy(m.ahi[:, i * 2 + u, :], m.a32[:, u, :]).then_inc(q.hi, 1)
                    f0 += nf
                    act.wait_ge(q.down, q.at.down + KD * (1 if f0 < NF else 2))
                end()

            def mla(L):
                m, q = m_mla[L], q_mla[L]
                jj = L // 3
                act.dma_start(m.tab[:, :, :], a["tab"]).then_inc(q.tab, 16)
                act.dma_start(m.dup[:, :], a["dup"]).then_inc(q.tab, 16)
                act.dma_start(m.c32[:, :, 0:PAST], a["ckvT"][jj]).then_inc(q.tab, 16)
                for hh, r0 in ((0, 64), (0, 96), (1, 0), (1, 32)):
                    act.dma_start(m.K[r0:r0 + 32, hh, 0:PAST], a["kpeT"][jj]).then_inc(q.tab, 16)
                split_h(2 * L, L, 0, m.t32, m.hhi)
                for p in range(5):
                    act.wait_ge(q.in_mm, q.at.in_mm + p + 1)
                    dst = m.q32[:, p, :] if p < 3 else m.c32[:, p - 3, PAST:KEYS]
                    nc.scalar.copy(halves(dst), pair(p % 4)).then_inc(q.in_ev, 1)
                act.wait_ge(q.in_ev, q.at.in_ev + 6)
                for kt in range(3):
                    last = af(m.sq[:, kt, :], m.q32[:, kt, :], ACT.Square)
                last.then_inc(q.st, 1)
                act.wait_ge(q.v_mm, q.at.v_mm + 1)
                for kt in range(2):
                    last = af(m.sq[:, kt, :], m.c32[:, kt, PAST:KEYS], ACT.Square)
                last.then_inc(q.st, 1)
                ch(af(halves(m.rs[:, 0, :]), pair(0), ACT.Sqrt, bias=eps[:, 1:2], scale=1.0 / QR))
                act.wait_ge(q.v_mm, q.at.v_mm + 2)
                af(halves(m.rs[:, 1, :]), pair(1), ACT.Sqrt, bias=eps[:, 1:2], scale=1.0 / KVR).then_inc(q.rsd, 1)
                act.wait_ge(q.v_mm, q.at.v_mm + 3)
                for h in range(2):
                    nc.scalar.copy(m.K[64:128, 0, PAST + h * HT:PAST + (h + 1) * HT], ps[64:128, 4 + h, 0:HT])
                    nc.scalar.copy(m.K[0:64, 1, PAST + h * HT:PAST + (h + 1) * HT], ps[0:64, 4 + h, 0:HT])
                act.wait_ge(q.cd, q.at.cd + 2)
                act.dma_start(o["ckv"][jj], m.c32[:, :, PAST + TS:KEYS]).then_inc(outs_done, 16)
                act.dma_start(o["kpe"][jj], m.kraw[0:32, TS:T]).then_inc(outs_done, 16)
                act.wait_ge(q.cd, q.at.cd + 3)
                nc.scalar.copy(m.qhi[:, :, :], m.q32[:, :, :]).then_inc(q.hi2, 1)
                nc.scalar.copy(m.khi[:, :, :], m.c32[:, :, :]).then_inc(q.hi2, 1)
                act.wait_ge(outs_done, 32 * (jj + 1))
                end()
                for n in range(12):
                    act.wait_ge(q.v_mm, q.at.v_mm + 3 + n + 1)
                    nc.scalar.copy(m.V[:, n // 2, (n % 2) * 512:(n % 2 + 1) * 512], ps[:, n % 4, :]).then_inc(q.v_ev, 1)
                end()
                with act.Fori(0, HEADS // 2) as j:
                    act.wait_ge(q.head_mm, q.at.head_mm + j * 3 + 3)
                    act.wait_ge(q.oev, q.at.oev + j * 10)
                    kp = lambda t: t.rearrange("p (h t) -> p h t", h=2)
                    nc.scalar.copy(kp(m.K[0:64, 0, :]), ps[0:64, 4:6, 0:KEYS // 2]).then_inc(q.k_ev, 1)
                    nc.scalar.copy(kp(m.K[64:128, 1, :]), ps[64:128, 4:6, 0:KEYS // 2]).then_inc(q.k_ev, 1)
                    for u in range(10):
                        qt = u % 5
                        act.wait_ge(q.nmax, q.at.nmax + j * 10 + (u + 1))
                        if u >= 2:
                            act.wait_ge(q.tr, q.at.tr + j * 10 + (u - 1))
                        b = 2 * (u % 2)
                        if qt < 4:
                            af(halves(m.pr[:, u % 2, :]), ps[:, b:b + 2, 0:HT], ACT.Exp, bias=m.nm[:, 2 * (u % 2), 0:1],
                               scale=SM_SCALE, accum_out=m.nm[:, 2 * (u % 2), 1:2]).then_inc(q.pexp, 1)
                        else:
                            af(m.pr[:, u % 2, 0:P], ps[:, b, 0:P], ACT.Exp, bias=m.nm[:, 2 * (u % 2), 0:1],
                               scale=SM_SCALE, accum_out=m.nm[:, 2 * (u % 2), 1:2]).then_inc(q.pexp, 1)
                    for qt in range(5):
                        act.wait_ge(q.ot, q.at.ot + j * 5 + (qt + 1))
                        nc.scalar.copy(m.hhi[:, j, qt * P:(qt + 1) * P], ps[:, 7, 0:P]).then_inc(q.ohi, 1)
                end()
                end()

            def rwkv(L):
                m, q = m_rwa, q_rwa
                act.dma_start(x_d.rearrange("k p t -> p k t"), x[:, :, :]).then_inc(q.xst, 16)
                act.wait_ge(q.xst, 16)
                for kt in range(KD):
                    for cd, (t0, t1) in enumerate(((0, TS), (TS, T))):
                        last = af(x[:, kt, t0:t1], x[:, kt, t0:t1], ACT.Identity,
                                  bias=mod[:, kt, cd:cd + 1], scale=mod[:, KD + kt, cd:cd + 1])
                last.then_inc(q.st, 1)
                FUNC = (ACT.Tanh, ACT.Copy, ACT.Sigmoid)
                n = 0

                def hi_part(idx):
                    for kt in range(KD):
                        act.wait_ge(q.val, KD * idx + kt + 1)
                        nc.scalar.copy(m.hset[idx % 2][0][:, kt, :], m.t32[:, kt % 2, :]).then_inc(q.hi, 1)

                def out_buffer(k):
                    if k >= 2:
                        act.wait_ge(s_rst[k % 2], 16 * (k // 2))
                    return m.o32[:, k % 2, :]

                def store(k, dst, width=T):
                    act.wait_ge(q.ev, k + 4)
                    act.dma_start(dst, m.o32[:, k % 2, 0:width]).then_inc(s_rst[k % 2], 16)

                hi_part(0)
                for idx in range(6):
                    if idx + 1 < 6:
                        hi_part(idx + 1)
                    if idx < 3:
                        act.wait_ge(q.mm, n + 1)
                        if idx:
                            act.wait_ge(q.hidlo, idx)
                        dst = halves(m.o32[:, 0, :])
                        if idx == 1:
                            nc.scalar.copy(dst, pair(n % 4)).then_inc(q.ev, 1)
                        else:
                            af(dst, pair(n % 4), FUNC[idx]).then_inc(q.ev, 1)
                        act.wait_ge(q.ev, n + 1)
                        nc.scalar.copy(m.hid["wag"[idx]][0][:, :], m.o32[:, 0, :]).then_inc(q.hid, 1)
                        n += 1
                        if idx == 2:
                            act.wait_ge(q.hidlo, 3)
                            for c in range(5 * KD):
                                act.wait_ge(q.mm, n + 1)
                                dst = halves(out_buffer(n - 3))
                                if c % 5 < 4:
                                    af(dst, pair(n % 4), ACT.Sigmoid, bias=rwp[:, c // 5, c % 5:c % 5 + 1]).then_inc(q.ev, 1)
                                else:
                                    nc.scalar.copy(dst, pair(n % 4)).then_inc(q.ev, 1)
                                store(n - 3, up_d[c // 5, c % 5])
                                n += 1
                    elif idx < 5:
                        for c in range(KD):
                            act.wait_ge(q.mm, n + 1)
                            nc.scalar.copy(halves(out_buffer(n - 3)), pair(n % 4)).then_inc(q.ev, 1)
                            store(n - 3, (r_d if idx == 3 else k_d)[c])
                            n += 1
                    else:
                        for h in range(2):
                            act.wait_ge(q.mm, n + h + 1)
                            for tt in range(NCH):
                                k = n - 3 + h * NCH + tt
                                nc.scalar.copy(out_buffer(k)[:, 0:512], ps[:, tt, :]).then_inc(q.ev, 1)
                                store(k, v_d[tt][:, h * 512:(h + 1) * 512], 512)
                for b in range(2):
                    act.wait_ge(s_rst[b], 16 * (n - 3 + 2 * NCH) // 2)
                end()
                m, q = m_rwb, q_rwb
                act.dma_start(m.pm[:, :, :], a["pmask"]).then_inc(q.zst, 16)
                act.dma_start(m.lm[:, :, :, :], a["lmask"]).then_inc(q.zst, 16)
                act.dma_start(m.i2[:, :], a["ident2"]).then_inc(q.zst, 16)
                sc, tok = (q.sc0, q.sc1), (q.tok0, q.tok1)
                rr, rev, uu, uev = (q.r0, q.r1), (q.rev0, q.rev1), (q.u0, q.u1), (q.uev0, q.uev1)
                yy, yev, tt_, tev = (q.y0, q.y1), (q.yev0, q.yev1), (q.t0, q.t1), (q.tev0, q.tev1)
                with act.Fori(0, KD) as j:
                    act.wait_ge(q.zt, j * 2 + 1)
                    act.dma_start(m.k[:, :], k_d[j]).then_inc(q.ld, 16)
                    act.dma_start(m.r[:, :], r_d[j]).then_inc(q.ld, 16)
                    act.dma_start(m.v[:, :, :], v_d.rearrange("c p (j n) -> j p c n", n=P)[j]).then_inc(q.ld, 16)
                    act.dma_start(m.LR[:, :, :], up_d.rearrange("j n p t -> j p n t")[j]).then_inc(q.ld, 16)
                    act.dma_start(m.S0[:, :, :], a["s0"][j]).then_inc(q.ld, 16)
                    act.dma_start(m.lnx[:, :, :], a["lnx"][j]).then_inc(q.ld, 16)
                    act.dma_start(m.par[:, :], a["rw"][j]).then_inc(q.ld, 16)
                    act.wait_ge(q.nrm, j + 1)
                    af(halves(m.t2[:, :]), pair(1), ACT.Sqrt, bias=eps[:, 3:4]).then_inc(q.nr, 1)
                    for d in range(2):
                        act.wait_ge(q.dec, j * 2 + (d + 1))
                        src = ((m.D1, -1), (m.D2, -1), (m.D1, 1)) if d == 0 else ((m.D2, 1), (m.D1, 1), (m.D2, -1))
                        for e, (t, sg) in enumerate(src):
                            af(m.E[:, e, :], t[:, :], ACT.Exp, scale=sg * KAPPA)
                        for e in range(2):
                            last = af(m.F[:, d, e if d == 0 else 1 - e, :], m.Fi[:, e, :], ACT.Exp, scale=-KAPPA)
                        last.then_inc(q.ex, 1)
                    def turned_keys(s):
                        for d in range(2):
                            act.wait_ge(sc[d], j * 5 + (s + 1))
                            nc.scalar.copy(m.BK[d][s % 2][:, :], ps[:, 4 * d + 2, 0:256]).then_inc(tok[d], 1)

                    def rhs(s):
                        for d in range(2):
                            act.wait_ge(rr[d], j * 5 + (s + 1))
                            nc.scalar.copy(m.R[d][:, :], ps[:, 4 * d + 2, 256:384]).then_inc(rev[d], 1)

                    def solve(s):
                        for d in range(2):
                            act.wait_ge(uu[d], j * 5 + (s + 1))
                            nc.scalar.copy(m.U[d][:, :], ps[:, 4 * d + 2, 384:512]).then_inc(uev[d], 1)

                    def output(s):
                        for d in range(2):
                            act.wait_ge(yy[d], j * 5 + (s + 1))
                            nc.scalar.copy(m.yd[d][:, chunk_of(d, s), :], ps[:, 4 * d + 2, 256:384]).then_inc(yev[d], 1)

                    for s in range(NCH):
                        turned_keys(s)
                        if s:
                            rhs(s - 1)
                            solve(s - 1)
                            output(s - 1)
                        for l in range(2, LEVELS + 1):
                            for d, hh in GROUPS:
                                act.wait_ge(tt_[d], j * 50 + (10 * s + 2 * l - 3 + hh))
                                nc.scalar.copy(m.XT[d][:, hh * P:(hh + 1) * P], ps[:, 4 * d + 3 - hh, 0:P]).then_inc(tev[d], 1)
                    rhs(NCH - 1)
                    solve(NCH - 1)
                    output(NCH - 1)
                    for d in range(2):
                        act.wait_ge((q.S0, q.S1)[d], j * 6 + 6)
                        act.dma_start(o["wkv"][j][d], m.So[d][:, :]).then_inc(q.zst, 16)
                    act.wait_ge(q.sqy, j + 1)
                    af(m.var[:, :], m.mu[:, :], ACT.Sqrt, bias=eps[:, 2:3], scale=1.0 / 64).then_inc(q.rsd, 1)
                    act.wait_ge(q.zt, j * 2 + 3)
                    act.dma_start(z_d[j], m.z[:, :]).then_inc(q.zst, 16)
                act.wait_ge(q.zst, 48 * KD + 48)
                end()
                m = m_rwc
                act.dma_start(m.z32[:, :, :], z_d.rearrange("j p t -> p j t")).then_inc(q.ld, 16)
                act.dma_start(x[:, :, :], x_d.rearrange("k p t -> p k t")).then_inc(q.ld, 16)
                act.wait_ge(q.ld, 16 * (7 * KD + 2))
                for kt in range(KD):
                    nc.scalar.copy(m.hhi[:, kt, :], m.z32[:, kt, :]).then_inc(q.st, 1)
                end()
                end()

            def pooling(L):
                m, q = m_pool, q_pool
                act.dma_start(m.cnt[:, :, :], a["icnt"]).then_inc(q.cst, 16)
                qq = q_split[2 * L]
                for kt in range(KD):
                    if kt >= 2:
                        act.wait_ge(qq.lo, qq.at.lo + kt - 1)
                    else:
                        act.wait_ge(q.st, 1)
                    for cd, (t0, t1, d0) in enumerate(((0, TS, 16), (TS, T, 48))):
                        last = af(m.hp[:, kt % 2, t0 + d0:t1 + d0], x[:, kt, t0:t1], ACT.Identity,
                                  bias=mod[:, kt, cd:cd + 1], scale=mod[:, KD + kt, cd:cd + 1])
                    last.then_inc(q.hp, 1)
                    act.wait_ge(qq.val, qq.at.val + kt + 1)
                    nc.scalar.copy(m.hhi[:, kt, :], m.t32[:, kt % 2, :]).then_inc(qq.hi, 1)
                end()
                end()

            act.wait_ge(s_const, 32)
            act.wait_ge(s_init, 2)
            ch(af(sc_c[:, :, :], cond, ACT.Silu))
            end()
            for L in range(DEPTH):
                ada(L)
                (mla, rwkv, pooling)[MIXER[L]](L)
                norm(2 * L)
                ffn(L)
                norm(2 * L + 1)
            act.dma_start(o["x"].rearrange("k p t -> p k t"), x[:, :, :]).then_inc(outs_done, 16)
            act.wait_ge(outs_done, 16 * (2 * len(m_mla) + 1))

        @block.vector
        def _(dve):
            end = Ends(dve)
            ch = Chain(dve, chain_dve)
            tt, ts, stt, cp = nc.vector.tensor_tensor, nc.vector.tensor_scalar, nc.vector.scalar_tensor_tensor, nc.vector.tensor_copy

            def ada(L):
                end()
                cols = ps[:, 2, 0:96].rearrange("p (n c) -> p n c", c=2)
                ch(tt(mod[:, :, :], cols, adab[:, L, :].unsqueeze(2).to_broadcast([P, 48, 2]), ALU.add))
                for part in (1, 4):
                    s = mod[:, part * KD:(part + 1) * KD, :]
                    ch(ts(s, s, 1.0, None, ALU.add))
                end()

            def split_lo(t, t32, hhi, hlo):
                q = q_split[t]
                for kt in range(KD):
                    dve.wait_ge(q.hi, q.at.hi + kt + 1)
                    tt(hlo[:, kt, :], t32[:, kt % 2, :], hhi[:, kt, :].bitcast(F32), ALU.subtract).then_inc(q.lo, 1)

            def scale_x():
                for kt in range(KD):
                    last = ts(x[:, kt, :], x[:, kt, :], ALPHA, None, ALU.mult)
                ch(last)

            def gated(c, b, gate, done):
                for h, t0, t1, cd in PIECES:
                    xs = x[:, c, h * HT + t0:h * HT + t1]
                    last = stt(xs, ps[:, 2 * b + h, t0:t1], gate[:, c, cd:cd + 1], xs, ALU.mult, ALU.add)
                last.then_inc(done, 1)

            def norm(t):
                m, q = m_ln[t], q_ln[t]
                L, s = divmod(t, 2)
                dve.wait_ge(q.mean, q.at.mean + 1)
                ch(ts(halves(m.rs[:, :]), pair(0), 1.0 / D, None, ALU.mult))
                for kt in range(KD):
                    tt(x[:, kt, :], x[:, kt, :], m.rs[:, :], ALU.subtract).then_inc(q.cen, 1)
                end()
                ch(nc.vector.reciprocal(m.rs[:, :], m.rs[:, :]))
                for kt in range(KD):
                    last = tt(m.sq[:, kt, :], x[:, kt, :], m.rs[:, :], ALU.mult)
                ch(last)
                for kt in range(KD):
                    last = ts(x[:, kt, :], m.sq[:, kt, :], lnp[:, L, s, 0, kt:kt + 1], lnp[:, L, s, 1, kt:kt + 1], ALU.mult, ALU.add)
                ch(last)
                end()

            def ffn(L):
                m, q = m_ffn[L], q_ffn[L]
                split_lo(2 * L + 1, m.t32, m.hhi, m.hlo)
                scale_x()
                gate = mod[:, 5 * KD:6 * KD, :]
                f0, dn = 0, 0
                for nf in FHALF:
                    with dve.Fori(0, nf // 2) as i:
                        for u in range(2):
                            dve.wait_ge(q.sil, q.at.sil + i * 2 + (f0 + u + 1))
                            tt(halves(m.a32[:, u, :]), halves(m.sil[:, u, :]), pair(2 * u + 1), ALU.mult).then_inc(q.act, 1)
                            dve.wait_ge(q.hi, q.at.hi + i * 2 + (f0 + u + 1))
                            tt(m.alo[:, i * 2 + u, :], m.a32[:, u, :], m.ahi[:, i * 2 + u, :].bitcast(F32), ALU.subtract).then_inc(q.lo, 1)
                    f0 += nf
                    for c in range(KD):
                        dve.wait_ge(q.down, q.at.down + dn + 1)
                        gated(c, c % 4, gate, q.upd)
                        dn += 1
                    dve.wait_ge(q.upd, q.at.upd + dn)
                end()

            def out_proj(L, gate):
                q = q_out[L]
                scale_x()
                for c in range(KD):
                    dve.wait_ge(q.mm, q.at.mm + c + 1)
                    gated(c, c % 4, gate, q.upd)
                end()

            def mla(L):
                m, q = m_mla[L], q_mla[L]
                jj = L // 3
                qn = C("qn").rearrange("p (l k) -> p l k", l=2)[:, jj, :]
                kvn = C("kvn").rearrange("p (l k) -> p l k", l=2)[:, jj, :]
                split_lo(2 * L, m.t32, m.hhi, m.hlo)
                dve.wait_ge(q.tab, q.at.tab + 16 * 7)
                dve.wait_ge(q.in_mm, q.at.in_mm + 6)
                dve.wait_ge(q.in_ev, q.at.in_ev + 5)
                tt(halves(m.kraw[:, :]), pair(1), halves(m.tab[:, 2, :]), ALU.mult).then_inc(q.in_ev, 1)
                dve.wait_ge(q.rsd, q.at.rsd + 1)
                ch(nc.vector.reciprocal(m.rs[:, :, :], m.rs[:, :, :]))
                for kt in range(2):
                    c = m.c32[:, kt, PAST:KEYS]
                    stt(c, c, kvn[:, kt:kt + 1], m.rs[:, 1, :], ALU.mult, ALU.mult).then_inc(q.cd, 1)
                for kt in range(3):
                    c = m.q32[:, kt, :]
                    last = stt(c, c, qn[:, kt:kt + 1], m.rs[:, 0, :], ALU.mult, ALU.mult)
                last.then_inc(q.cd, 1)
                dve.wait_ge(q.hi2, q.at.hi2 + 1)
                tt(m.qlo[:, :, :], m.q32[:, :, :], m.qhi[:, :, :].bitcast(F32), ALU.subtract)
                dve.wait_ge(q.hi2, q.at.hi2 + 2)
                ch(tt(m.klo[:, :, :], m.c32[:, :, :], m.khi[:, :, :].bitcast(F32), ALU.subtract))
                end()
                end()
                with dve.Fori(0, HEADS // 2) as j:
                    for hh in range(2):
                        dve.wait_ge(q.head_mm, q.at.head_mm + j * 3 + (hh + 1))
                        tt(halves(m.Q[:, hh, :]), pair(hh), halves(m.tab[:, hh, :]), ALU.mult).then_inc(q.q_ev, 1)

                    def tail(u):
                        hh, qt = divmod(u, 5)
                        dve.wait_ge(q.rec, q.at.rec + j * 10 + (u + 1))
                        dve.wait_ge(q.av, q.at.av + j * 10 + (u + 1))
                        ts(m.O[:, qt, hh * 64:(hh + 1) * 64], ps[:, 6, 0:64], m.rc[:, u % 4:u % 4 + 1], None,
                           ALU.mult).then_inc(q.oev, 1)

                    for u in range(10):
                        qt = u % 5
                        n, b = u % 2, 2 * (u % 2)
                        dve.wait_ge(q.sc, q.at.sc + j * 10 + (u + 1))
                        if qt < 4:
                            nc.vector.tensor_reduce(m.mx[:, n:n + 1], ps[:, b:b + 2, 0:HT], AX.XY, ALU.max).then_inc(q.mx, 1)
                        else:
                            nc.vector.tensor_reduce(m.mx[:, n:n + 1], ps[:, b, 0:P], AX.X, ALU.max).then_inc(q.mx, 1)
                        dve.wait_ge(q.mx, q.at.mx + j * 10 + (u + 1))
                        ts(m.nm[:, 2 * n, 0:1], m.mx[:, n:n + 1], -SM_SCALE, None, ALU.mult).then_inc(q.nmax, 1)
                        if u:
                            copy_pt(dve, q, m, j, u - 1)
                        if u >= 2:
                            tail(u - 2)
                    tail(8)
                    copy_pt(dve, q, m, j, 9)
                    tail(9)
                    for qt in range(5):
                        dve.wait_ge(q.ohi, q.at.ohi + j * 5 + (qt + 1))
                        tt(m.hlo[:, j, qt * P:(qt + 1) * P], ps[:, 7, 0:P], m.hhi[:, j, qt * P:(qt + 1) * P].bitcast(F32),
                           ALU.subtract).then_inc(q.olo, 1)
                end()
                out_proj(L, mod[:, 2 * KD:3 * KD, :])

            def copy_pt(dve, q, m, j, u):
                n = u % 2
                dve.wait_ge(q.tr, q.at.tr + j * 10 + (u + 1))
                if u % 5 < 4:
                    cp(m.pt[:, n, 0:512], ps[:, 4, :])
                    cp(m.pt[:, n, 512:640], ps[:, 5, 0:P]).then_inc(q.ptc, 1)
                else:
                    cp(m.pt[:, n, 0:P], ps[:, 4, 0:P]).then_inc(q.ptc, 1)
                nc.vector.reciprocal(m.rc[:, u % 4:u % 4 + 1], m.nm[:, 2 * n, 1:2]).then_inc(q.rec, 1)

            def rwkv(L):
                m, q = m_rwa, q_rwa
                dve.wait_ge(q.st, 1)
                last = None
                for kt in range(KD):
                    for t0, t1 in ((0, TS), (TS, T)):
                        h, xx = x[:, kt, :], m.xx[:, kt, :]
                        tt(xx[:, t0 + 1:t1 - 1], h[:, t0:t1 - 2], h[:, t0 + 2:t1], ALU.add)
                        cp(xx[:, t0:t0 + 1], h[:, t0 + 1:t0 + 2])
                        last = cp(xx[:, t1 - 1:t1], h[:, t1 - 2:t1 - 1])
                ch(last)
                for kt in range(KD):
                    last = stt(m.xx[:, kt, :], m.xx[:, kt, :], 0.5, x[:, kt, :], ALU.mult, ALU.subtract)
                ch(last)
                ORDER = (1, 4, 5, 0, 2, 3)
                MMS = (1, 2, 3 + 5 * KD, 3 + 6 * KD, 3 + 7 * KD)

                def lo_part(n):
                    idx, kt = divmod(n, KD)
                    dve.wait_ge(q.hi, n + 1)
                    hi, lo = m.hset[idx % 2]
                    tt(lo[:, kt, :], m.t32[:, kt % 2, :], hi[:, kt, :].bitcast(F32), ALU.subtract).then_inc(q.lo, 1)

                def hidden(k):
                    dve.wait_ge(q.hid, k + 1)
                    hi, lo = m.hid["wag"[k]]
                    tt(lo[:, :], m.o32[:, 0, :], hi[:, :].bitcast(F32), ALU.subtract).then_inc(q.hidlo, 1)

                for idx in range(6):
                    for kt in range(KD):
                        n = idx * KD + kt
                        if idx >= 2 and kt == 0:
                            lo_part(n - 1)
                            if idx <= 4:
                                hidden(idx - 2)
                            dve.wait_ge(q.mm, MMS[idx - 2])
                        if n >= 2:
                            dve.wait_ge(q.lo, n - 1)
                        stt(m.t32[:, kt % 2, :], m.xx[:, kt, :], mu_c[:, ORDER[idx], kt:kt + 1], x[:, kt, :],
                            ALU.mult, ALU.add).then_inc(q.val, 1)
                        if n >= 1 and not (idx >= 2 and kt == 0):
                            lo_part(n - 1)
                lo_part(6 * KD - 1)
                end()
                m, q = m_rwb, q_rwb
                sc, x1, inv, xs = (q.sc0, q.sc1), (q.x10, q.x11), (q.inv0, q.inv1), (q.x0, q.x1)
                yy, SS = (q.y0, q.y1), (q.S0, q.S1)
                dve.wait_ge(q.zst, 48)
                ch(nc.vector.memset(m.onesT[:, :], 1.0))
                for d in range(2):
                    for b in range(2):
                        last = nc.vector.memset(m.AM[d][b][:, :, :], 0.0)
                ch(last)

                def c3(t):
                    return t.rearrange("p (c t) -> p c t", c=NCH)
                with dve.Fori(0, KD) as j:
                    ch.enter(j, RW_CHAIN)

                    def par(n):
                        return m.par[:, n:n + 1]
                    dve.wait_ge(q.ld, j * 112 + 112)
                    ch(ts(m.kk[:, :], m.k[:, :], par(4), None, ALU.mult))
                    tt(m.t1[:, :], m.kk[:, :], m.kk[:, :], ALU.mult).then_inc(q.kksq, 1)
                    dve.wait_ge(q.nr, j + 1)
                    ch(ts(m.t2[:, :], m.t2[:, :], 1e-12, None, ALU.max))
                    ch(nc.vector.reciprocal(m.t2[:, :], m.t2[:, :]))
                    ch(tt(m.kk[:, :], m.kk[:, :], m.t2[:, :], ALU.mult))
                    for d in range(2):
                        for c in range(NCH):
                            last = nc.vector.tensor_tensor_scan(m.PS[:, c * P:(c + 1) * P], m.onesT[:, :],
                                                                m.LR[:, d, c * P:(c + 1) * P], 0.0, ALU.mult, ALU.add)
                        ch(last)
                        mid = c3(m.PS[:, :])[:, :, 63:64]
                        ch(tt(c3(m.D1[:, :]), c3(m.PS[:, :]), mid.to_broadcast([P, NCH, P]), ALU.subtract))
                        cp(m.Fi[:, 0:1, :].rearrange("p a c -> p c a"), mid)
                        cp(m.Fi[:, 1:2, :].rearrange("p a c -> p c a"), c3(m.D1[:, :])[:, :, P - 1:P])
                        tt(m.D2[:, :], m.D1[:, :], m.LR[:, d, :], ALU.subtract).then_inc(q.dec, 1)
                        ch(ts(m.t1[:, :], m.LR[:, 2 + d, :], -1.0, None, ALU.add))
                        ch(ts(m.t1[:, :], m.t1[:, :], par(5), 1.0, ALU.mult, ALU.add))
                        ch(tt(m.t1[:, :], m.t1[:, :], m.k[:, :], ALU.mult))
                        if d == 0:
                            cp(m.kds[:, :], m.t1[:, :])
                        else:
                            tt(m.kds[:, :], m.kds[:, :], m.t1[:, :], ALU.add)
                        ch(tt(m.t2[:, :], m.kk[:, :], m.LR[:, 2 + d, :], ALU.mult))
                        dve.wait_ge(q.ex, j * 2 + (d + 1))
                        tt(m.BT[d][:, :], m.t2[:, :], m.E[:, 2, :], ALU.mult)
                        tt(m.KT[d][:, :], m.t1[:, :], m.E[:, 2, :], ALU.mult)
                        tt(m.AR[d][:, :, 1, :], c3(m.r[:, :]), c3(m.E[:, 0, :]), ALU.mult)
                        stt(m.AR[d][:, :, 0, :], c3(m.kk[:, :]), -1.0, c3(m.E[:, 1, :]), ALU.mult, ALU.mult).then_inc(q.til, 1)
                        before, after = (slice(1, 4), slice(0, 3)) if d == 0 else (slice(0, 3), slice(1, 4))
                        ch(tt(m.Fc[:, d, after], m.F[:, d, 1, after], m.F[:, d, 0, before], ALU.mult))
                        ts(m.S[d][:, :], m.S0[:, d, :], m.F[:, d, 0, chunk_of(d, 0):chunk_of(d, 0) + 1], None, ALU.mult).then_inc(SS[d], 1)
                    h2p = lambda t: t.rearrange("p (h t) -> p h t", h=2)

                    def masked_scores(s):
                        for d in range(2):
                            am = m.AM[d][s % 2]
                            dve.wait_ge(sc[d], j * 5 + (s + 1))
                            nc.vector.memset(m.pad[:, d:d + 1], 0.0)
                            for hh in range(2):
                                last = nc.vector.copy_predicated(am[:, hh, :], m.pm[:, d, :].bitcast(U32), ps[:, 4 * d + hh, :])
                            ch(last)
                            ch(tt(h2p(m.XT[d][:, :]), am[:, :, 0:P], m.lm[:, d, 0:1, :].to_broadcast([P, 2, P]), ALU.mult))
                            tt(m.XT[d][:, :], m.XT[d][:, :], m.i2[:, :], ALU.add).then_inc(x1[d], 1)
                        for d, hh in GROUPS:
                            dve.wait_ge(inv[d], j * 130 + (26 * s + 1 + hh))
                            cp(m.X[d][:, hh * P:(hh + 1) * P], ps[:, 4 * d + hh, 0:P]).then_inc(xs[d], 1)

                    def level(s, l):
                        for d, hh in GROUPS:
                            dve.wait_ge(inv[d], j * 130 + (26 * s + 4 * l - 1 + hh))
                            tt(m.Y[d][:, hh * P:(hh + 1) * P], ps[:, 4 * d + hh, 0:P], m.lm[:, d, l, :], ALU.mult).then_inc(xs[d], 1)
                        for d, hh in GROUPS:
                            dve.wait_ge(inv[d], j * 130 + (26 * s + 4 * l + 1 + hh))
                            old, new = (m.X[d], m.X[d]) if l < LEVELS else (m.XT[d], m.XF[d])
                            tt(new[:, hh * P:(hh + 1) * P], old[:, hh * P:(hh + 1) * P], ps[:, 4 * d + hh, P:2 * P],
                               ALU.add).then_inc(xs[d], 1)

                    def state(s):
                        for d in range(2):
                            c = chunk_of(d, s)
                            dve.wait_ge(yy[d], j * 5 + (s + 1))
                            if s == NCH - 2:
                                nc.vector.memset(m.S[d][:, :], 0.0).then_inc(SS[d], 1)
                                continue
                            by, dst = (m.Fc[:, d, c:c + 1], m.S[d]) if s < NCH - 2 else (m.F[:, d, 1, c:c + 1], m.So[d])
                            ch(stt(m.st[:, d, :], ps[:, 4 * d + 3, 0:P], by, C("blk"), ALU.mult, ALU.mult))
                            if s == NCH - 1:
                                dve.wait_ge(q.zst, j * 48 + 48)
                            stt(dst[:, :], m.S[d][:, :], by, m.st[:, d, :], ALU.mult, ALU.add).then_inc(SS[d], 1)

                    for s in range(NCH):
                        masked_scores(s)
                        level(s, 1)
                        if s:
                            state(s - 1)
                        for l in range(2, LEVELS + 1):
                            level(s, l)
                    state(NCH - 1)
                    stt(m.t1[:, :], m.kds[:, :], par(6), m.r[:, :], ALU.mult, ALU.mult).then_inc(q.prod, 1)
                    dve.wait_ge(q.yev0, j * 5 + 5)
                    dve.wait_ge(q.yev1, j * 5 + 5)
                    h2 = lambda t: t[:, :, :].rearrange("p c (h n) -> p (c h) n", h=2)
                    y, y2 = h2(m.yd[0]), h2(m.y2)
                    ch(tt(m.yd[0][:, :, :], m.yd[0][:, :, :], m.yd[1][:, :, :], ALU.add))
                    ch(nc.vector.tensor_reduce(m.mu[:, :], y, AX.X, ALU.add))
                    ch(ts(m.mu[:, :], m.mu[:, :], 1.0 / 64, None, ALU.mult))
                    B10 = [P, 2 * NCH, 64]
                    ch(tt(y, y, m.mu[:, :].unsqueeze(2).to_broadcast(B10), ALU.subtract))
                    ch(tt(y2, y, y, ALU.mult))
                    nc.vector.tensor_reduce(m.mu[:, :], y2, AX.X, ALU.add).then_inc(q.sqy, 1)
                    dve.wait_ge(q.bon, j + 1)
                    ch(cp(m.bon[:, :], ps[:, 0, 0:2 * NCH]))
                    ch(tt(y2, h2(m.v), m.bon[:, :].unsqueeze(2).to_broadcast(B10), ALU.mult))
                    dve.wait_ge(q.rsd, j + 1)
                    ch(nc.vector.reciprocal(m.var[:, :], m.var[:, :]))
                    ch(tt(y, y, m.var[:, :].unsqueeze(2).to_broadcast(B10), ALU.mult))
                    lx = lambda n: m.lnx[:, n:n + 1, :].to_broadcast([P, NCH, P])
                    ch(tt(m.yd[0][:, :, :], m.yd[0][:, :, :], lx(0), ALU.mult))
                    ch(tt(m.yd[0][:, :, :], m.yd[0][:, :, :], lx(1), ALU.add))
                    tt(m.y2[:, :, :], m.y2[:, :, :], m.yd[0][:, :, :], ALU.add).then_inc(q.zt, 1)
                    dve.wait_ge(q.z, j + 1)
                    dve.wait_ge(q.zst, j * 48 + 48)
                    tt(m.z[:, 0:512], ps[:, 2, :], m.LR[:, 4, 0:512], ALU.mult)
                    tt(m.z[:, 512:T], ps[:, 3, 0:P], m.LR[:, 4, 512:T], ALU.mult).then_inc(q.zt, 1)
                    ch.leave(KD)
                end()
                m = m_rwc
                for kt in range(KD):
                    dve.wait_ge(q.st, kt + 1)
                    last = tt(m.hlo[:, kt, :], m.z32[:, kt, :], m.hhi[:, kt, :].bitcast(F32), ALU.subtract)
                ch(last)
                end()
                out_proj(L, mod[:, 2 * KD:3 * KD, :])

            def pooling(L):
                m, q = m_pool, q_pool
                ch(tt(m.gs[:, :, :], mod[:, 2 * KD:3 * KD, :], psc.unsqueeze(2).to_broadcast([P, KD, 2]), ALU.mult))
                nc.vector.memset(m.b[:, :, :], 0.0)
                nc.vector.memset(m.hp[:, :, :], 0.0).then_inc(q.st, 1)
                dve.wait_ge(q.st, 1)
                dve.wait_ge(q.cst, 16)
                qq = q_split[2 * L]
                N = T + 64
                for kt in range(KD):
                    g = kt // 2
                    dve.wait_ge(q.hp, kt + 1)
                    hp, cur, w = m.hp[:, kt % 2, :], m.hp[:, kt % 2, :], 1
                    n = 0
                    while w < WINDOWS[g]:
                        dst = m.b[:, n % 2, :]
                        ch(tt(dst[:, 0:N - 16], cur[:, 0:N - 16], cur[:, w:N - 16 + w], ALU.add))
                        cur, w, n = dst, 2 * w, n + 1
                    hw = WINDOWS[g] // 2
                    t32 = m.t32[:, kt % 2, :]
                    if kt >= 2:
                        dve.wait_ge(qq.lo, qq.at.lo + kt - 1)
                    for t0, t1, d0 in ((0, TS, 16), (TS, T, 48)):
                        last = tt(t32[:, t0:t1], cur[:, t0 + d0 - hw:t1 + d0 - hw], m.cnt[:, g, t0:t1], ALU.mult)
                    ch(last)
                    for t0, t1, d0 in ((0, TS, 16), (TS, T, 48)):
                        last = tt(t32[:, t0:t1], t32[:, t0:t1], hp[:, t0 + d0:t1 + d0], ALU.subtract)
                    last.then_inc(qq.val, 1)
                    dve.wait_ge(qq.hi, qq.at.hi + kt + 1)
                    tt(m.hlo[:, kt, :], t32, m.hhi[:, kt, :].bitcast(F32), ALU.subtract).then_inc(qq.lo, 1)
                end()
                out_proj(L, m.gs)

            primed = [q_mla[min(q_mla)].oev, q_mla[min(q_mla)].olo, q_rwb.zt, s_init]
            for k, v in enumerate((LN_EPS, RMS_EPS, GN_EPS, 0.0)):
                nc.vector.memset(eps[:, k:k + 1], v).then_inc(primed[k], 1)
            dve.wait_ge(s_const, 32)
            end()
            for L in range(DEPTH):
                ada(L)
                (mla, rwkv, pooling)[MIXER[L]](L)
                norm(2 * L)
                ffn(L)
                norm(2 * L + 1)

def chunk_of(d, s):
    return s if d == 0 or s == NCH - 1 else NCH - 2 - s

def tables():
    nf = ROPE // 4
    inv = (10000.0 ** (-np.arange(nf, dtype=np.float32) / np.float32(nf))).astype(np.float32)
    t = np.arange(TS)
    ang = np.stack([(t // GRID_W).astype(np.float32)[:, None] * inv, (t % GRID_W).astype(np.float32)[:, None] * inv], 1)
    cos, sin = np.cos(ang).astype(np.float32), np.sin(ang).astype(np.float32)
    Ct, St = np.ones((ROPE, T), np.float32), np.zeros((ROPE, T), np.float32)
    for d in range(ROPE):
        ax, half, f = d // (2 * nf), (d // nf) % 2, d % nf
        Ct[d, :TS] = cos[:, ax, f]
        St[d, :TS] = sin[:, ax, f] * (1 if half else -1)
    one = np.ones((NOPE, T), np.float32)
    tab = np.stack([np.concatenate([one, Ct, St]), np.concatenate([Ct, St, one]), np.concatenate([Ct, St, 0 * one])], 1)
    i = np.arange(P)
    row, col = i[:, None], i[None, :]
    pm = np.zeros((P, 2, 512), np.float32)
    lm = np.zeros((P, 2, LEVELS + 1, P), np.float32)
    for d, (lt, le) in enumerate(((row < col, row <= col), (row > col, row >= col))):
        pm[:, d] = np.concatenate([lt, le, lt, le], 1)
        for l in range(LEVELS + 1):
            n = 1 << l
            same = row // (2 * n) == col // (2 * n)
            later_row = (row // n) % 2 > (col // n) % 2
            early_row = (row // n) % 2 < (col // n) % 2
            want = same & (early_row if (l == 0) == (d == 0) else later_row)
            lm[:, d, l] = want
    dup = np.zeros((P, P), np.float32)
    for k in range(P):
        dup[k % 32, k] = dup[32 + k % 32, k] = 1
    hsel = np.zeros((P, 2), np.float32)
    hsel[:64, 0] = hsel[64:, 1] = 1
    blk = (row // 64 == col // 64).astype(np.float32)
    icnt = np.zeros((4, T), np.float32)
    for g, w in enumerate(WINDOWS):
        for n, off in ((TS, 0), (TP, TS)):
            tt = np.arange(n)
            icnt[g, off:off + n] = np.float32(1) / (np.clip(tt - w // 2 + w, 0, n) - np.clip(tt - w // 2, 0, n)).astype(np.float32)
    return dict(tab=np.ascontiguousarray(tab), pmask=pm, lmask=lm, icnt=icnt,
                ident2=np.concatenate([np.eye(P, dtype=np.float32)] * 2, 1),
                ident=np.eye(P, dtype=np.float32), ones=np.ones((P, P), np.float32), blk=blk, dup=dup, hsel=hsel)

def weight_tiles(w):
    out = []

    def panel(W, col, k0=0, kn=None):
        kn = W.shape[0] // P if kn is None else kn
        for k in range(k0, k0 + kn):
            out.append(W[k * P:(k + 1) * P, col:col + P])

    nf = ROPE // 4
    swap = np.array([d // (2 * nf) * 2 * nf + (1 - (d // nf) % 2) * nf + d % nf for d in range(ROPE)])
    for L in range(DEPTH):
        j = L // 3
        if MIXER[L] == 0:
            for c in range(QR // P):
                panel(w["mla_wq_a"][j], c * P)
            kva = w["mla_wkv_a"][j]
            for c in range(KVR // P):
                panel(kva, c * P)
            pe = kva[:, KVR:]
            panel(np.concatenate([pe, pe[:, swap], np.zeros((D, 64), np.float32)], 1), 0)
            kvb = w["mla_wkv_b"][j].reshape(KVR, HEADS, NOPE + VD)
            v = np.ascontiguousarray(kvb[:, :, NOPE:]).reshape(KVR, HEADS * VD)
            for k in range(2):
                for c in range(8):
                    panel(v, c * P, k, 1)
            qb = w["mla_wq_b"][j].reshape(QR, HEADS, NOPE + ROPE)
            for p in range(HEADS // 2):
                a, b = qb[:, 2 * p], qb[:, 2 * p + 1]
                panel(np.concatenate([a[:, :NOPE], a[:, NOPE:], a[:, NOPE:][:, swap]], 1), 0)
                panel(np.concatenate([b[:, NOPE:], b[:, NOPE:][:, swap], b[:, :NOPE]], 1), 0)
                panel(np.concatenate([kvb[:, 2 * p, :NOPE], kvb[:, 2 * p + 1, :NOPE]], 1), 0)
            for c in range(KD):
                panel(w["mla_wo"][j], c * P)
        elif MIXER[L] == 1:
            for n in ("rwkv_w1", "rwkv_a1"):
                panel(np.concatenate([w[n][j, 0], w[n][j, 1]], 1), 0)
            panel(w["rwkv_g1"][j], 0)
            zero = np.zeros((64, P), np.float32)
            for c in range(KD):
                for n in ("rwkv_w2", "rwkv_a2"):
                    u = w[n][j][:, :, c * P:(c + 1) * P]
                    out.append(np.concatenate([u[0], zero]))
                    out.append(np.concatenate([zero, u[1]]))
                panel(w["rwkv_g2"][j], c * P)
            for n in ("rwkv_wr", "rwkv_wk"):
                for c in range(KD):
                    panel(w[n][j], c * P)
            for h in range(2):
                for k in range(KD):
                    for c in range(4):
                        panel(w["rwkv_wv"][j], (4 * h + c) * P, k, 1)
            for c in range(KD):
                panel(w["rwkv_wo"][j], c * P)
        else:
            for c in range(KD):
                panel(w["pool_w"][j, c // 2], (c % 2) * P)
        f0 = 0
        for nf_ in FHALF:
            for f in range(f0, f0 + nf_):
                panel(w["ffn_wg"][L], f * P)
                panel(w["ffn_wu"][L], f * P)
            for c in range(KD):
                panel(w["ffn_wd"][L], c * P, f0, nf_)
            f0 += nf_
    return out

def columns(v):
    v = v.reshape(*v.shape[:-1], -1, P)
    return np.moveaxis(v, -1, 0)

def kernel(**inputs):
    import concourse.bacc as bacc
    from concourse.bass_utils import run_bass_kernel_spmd

    w = {k: np.asarray(v) for k, v in inputs.items()}
    tb = tables()
    tiles = weight_tiles(w)
    assert len(tiles) == NCHUNK * CH
    stream = np.empty((NCHUNK, P, CH, P), np.float32)
    for n, t in enumerate(tiles):
        stream[n // CH, :, n % CH] = t
    rw = np.stack([w["rwkv_w0"][0, 0], w["rwkv_w0"][0, 1], w["rwkv_a0"][0, 0], w["rwkv_a0"][0, 1],
                   w["rwkv_k_k"][0], w["rwkv_k_a"][0], w["rwkv_r_k"][0].reshape(D)], 0)
    rwc = columns(rw)
    parts = dict(
        ident=tb["ident"], ones=tb["ones"], blk=tb["blk"], hsel=tb["hsel"],
        lnp=columns(np.stack([w["ln_g"], w["ln_b"]], 2)), adab=columns(w["ada_b"]),
        qn=columns(w["mla_q_norm"]), kvn=columns(w["mla_kv_norm"]), mu=columns(w["rwkv_mu"][0]),
        psc=columns(w["pool_scale"][0]), rw=np.moveaxis(rwc, 1, 2),
        cond=np.moveaxis(columns(np.stack([w["c"][0], w["c_ctx"]])), 1, 2))
    cst = np.concatenate([parts[k].reshape(P, -1) for k in _CST], 1)
    assert cst.shape == (P, NCST), cst.shape
    xs = np.concatenate([w["x_sample"][0], w["x_prompt"][0]], 0)
    s0 = w["state_wkv"][0, 0].reshape(2, KD, 2, 64, 64)
    s0b = np.zeros((KD, P, 2, P), np.float32)
    for h in range(2):
        s0b[:, 64 * h:64 * h + 64, :, 64 * h:64 * h + 64] = s0[:, :, h].transpose(1, 3, 0, 2)
    arrays = dict(
        cst=cst, x=np.ascontiguousarray(xs.T).reshape(KD, P, T), w=stream.reshape(NCHUNK, P, CH * P), ada_w=w["ada_w"],
        tab=tb["tab"], dup=tb["dup"], ckvT=w["cache_ckv"][0].reshape(2, PAST, 2, P).transpose(0, 3, 2, 1),
        kpeT=w["cache_kpe"][0].transpose(0, 2, 1), pmask=tb["pmask"], lmask=tb["lmask"], ident2=tb["ident2"],
        s0=s0b,
        lnx=np.stack([w["rwkv_lnx_g"][0], w["rwkv_lnx_b"][0]]).reshape(2, KD, P).transpose(1, 0, 2)[:, None].repeat(P, 1),
        rw=np.moveaxis(rwc, 2, 0), icnt=tb["icnt"][None].repeat(P, 0))
    outs = dict(x=(KD, P, T), ckv=(2, P, 2, TP), kpe=(2, ROPE, TP), wkv=(KD, 2, P, P))

    nc = bacc.Bacc("TRN2", target_bir_lowering=False, num_devices=1)
    a, o = {}, {}
    for k, v in arrays.items():
        arrays[k] = np.ascontiguousarray(v)
        a[k] = nc.dram_tensor("in_" + k, arrays[k].shape, mybir.dt.from_np(arrays[k].dtype), kind="ExternalInput").ap()
    for k, v in outs.items():
        o[k] = nc.dram_tensor("out_" + k, v, F32, kind="ExternalOutput").ap()
    build(nc, a, o)
    r = run_bass_kernel_spmd(nc, [{"in_" + k: v for k, v in arrays.items()}], core_ids=[0]).results[0]
    y = r["out_x"].reshape(D, T).T
    ckv = r["out_ckv"].transpose(0, 3, 2, 1).reshape(2, TP, KVR)
    kpe = r["out_kpe"].transpose(0, 2, 1)
    wkv = np.stack([r["out_wkv"][:, :, 64 * h:64 * h + 64, 64 * h:64 * h + 64] for h in range(2)], 2)
    wkv = wkv.transpose(1, 0, 2, 4, 3).reshape(2, HEADS, 64, 64)
    return (np.ascontiguousarray(y[TS:])[None], np.ascontiguousarray(y[:TS])[None], np.ascontiguousarray(ckv)[None],
            np.ascontiguousarray(kpe)[None], np.ascontiguousarray(wkv)[None, None])
```

```python
from collections import namedtuple
from contextlib import ExitStack

import numpy as np

import concourse.bass as bass
from concourse import mybir

F32 = mybir.dt.float32
F32R = mybir.dt.float32r
U32 = mybir.dt.uint32
ALU = mybir.AluOpType
ACT = mybir.ActivationFunctionType
AX = mybir.AxisListType

P = 128
D = 1024
KD = D // P
TS, TP = 512, 128
T = TS + TP
HT = T // 2
DEPTH = 4
PAST = 128
GRID_W = 64
HEADS = 16
QR, KVR = 384, 256
NOPE, ROPE, VD = 64, 32, 64
FF = 2816
NF = FF // P
FHALF = (12, 10)
ALPHA = (2 * DEPTH) ** 0.25
LN_EPS, RMS_EPS, GN_EPS = 1e-5, 1e-6, 64e-5
SM_SCALE = float(NOPE + ROPE) ** -0.5
KAPPA = float(np.exp(-0.5))
WINDOWS = (2, 4, 8, 16)
NCH = TS // P + 1
KEYS = PAST + T
OUT_BUFFERS = 4
CH = 8
RAW, RS = 3, 4
MIXER = [i % 3 for i in range(DEPTH)]
ADA_SLOTS, ADA_EARLY = 4, 3
ADA_UNITS, ADA_SPLITS = 24, 3
UNIT = 4 * 512
FFN_WORDS = (2 * KD + 2 * FHALF[0] + 6) * T
GROUPS = [(d, h) for h in range(2) for d in range(2)]
LEVELS = 6

C_MLA_IN, C_MLA_V, C_MLA_HEADS, C_OUT = 6, 2, HEADS // 2, KD
C_RWKV_LORA, C_RWKV_UP, C_RWKV_RKV = 3, 5, 24
C_POOL = 2
C_FFN = (NF * 2 * KD + NF * KD) // CH
C_MIX = [C_MLA_IN + C_MLA_V + C_MLA_HEADS + C_OUT, C_RWKV_LORA + C_RWKV_UP + C_RWKV_RKV + C_OUT, C_POOL]
LAYER_BASE = [0]
for _l in range(DEPTH):
    LAYER_BASE.append(LAYER_BASE[-1] + C_MIX[MIXER[_l]] + C_FFN)
NCHUNK = LAYER_BASE[-1]
RW_CHAIN, RW_POOL = 60, 26

_CST = {}
_n = 0
for _k, _w in (("ident", 128), ("ones", 128), ("blk", 128), ("hsel", 2), ("lnp", DEPTH * 2 * 2 * KD),
               ("adab", DEPTH * 48), ("qn", 2 * 3), ("kvn", 2 * 2), ("mu", 6 * KD), ("psc", KD), ("rw", KD * 7),
               ("cond", 2 * KD)):
    _CST[_k] = (_n, _n + _w)
    _n += _w
NCST = _n

class Chain:

    def __init__(self, eng, sem):
        self.eng, self.sem, self.n, self.loop = eng, sem, 0, None

    def enter(self, i, per):
        self.loop, self.start = (i, per), self.n

    def leave(self, iters):
        i, per = self.loop
        assert self.n - self.start == per, (self.n - self.start, per)
        self.n, self.loop = self.start + per * iters, None

    def __call__(self, ins):
        self.n += 1
        ins.then_inc(self.sem, 1)
        self.eng.wait_ge(self.sem, self.n if self.loop is None else self.loop[0] * self.loop[1] + self.n)

def every_pair(eng, body, prepare, finish, chain=None, per=0):
    prepare(0, 0)
    body(0, 0, True, False)
    with eng.Fori(0, KD // 2 - 1) as i:
        if chain:
            chain.enter(i, per)
        body(i * 2 + 1, 1, False, False)
        body(i * 2 + 2, 0, False, False)
    if chain:
        chain.leave(KD // 2 - 1)
    body(KD - 1, 1, False, True)
    finish(KD - 1, 1)

class Weights:

    def __init__(self, pe, hi, lo, split, used):
        self.pe, self.hi, self.lo, self.split, self.used = pe, hi, lo, split, used
        self.tile, self.loop, self.owed = 0, None, False

    def enter(self, i, per):
        self.loop, self.start = (i, per), self.tile

    def leave(self, iters):
        i, per = self.loop
        assert self.tile - self.start == per * CH
        self.tile, self.loop = self.start + per * iters * CH, None

    def next(self, n=1):
        c, k = divmod(self.tile, CH)
        if k == 0:
            w = c + 1
            self.pe.wait_ge(self.split, w if self.loop is None else self.loop[0] * self.loop[1] + w)
            self.owed = c > 0
        self.tile += n
        s = c % RS
        return self.hi[:, s, k * P:(k + n) * P], self.lo[:, s, k * P:(k + n) * P]

    def first(self, ins):
        if self.owed:
            ins.then_inc(self.used, 1)
            self.owed = False

def build(nc, a, o):
    ctx = ExitStack()
    with ctx:
        def sb(name, shape, dt=F32, st=None):
            return (st or ctx).enter_context(nc.sbuf_tensor(name, shape, dt))

        def sem(name):
            return ctx.enter_context(nc.semaphore(name))

        def halves(t):
            return t.rearrange("p (h t) -> p h t", h=2)

        x = sb("x", [P, KD, T])
        raw = sb("w_raw", [P, RAW, CH * P])
        whi = sb("w_hi", [P, RS, CH * P], F32R)
        wlo = sb("w_lo", [P, RS, CH * P], F32R)
        zrow = sb("zrow", [P, 1])
        cst = sb("cst", [P, NCST])
        mod = sb("mod", [P, 48, 2])
        eps = sb("eps", [P, 5])
        sc_c = sb("silu_c", [P, KD, 2])
        sc_hi, sc_lo = sb("silu_hi", [P, KD, 2], F32R), sb("silu_lo", [P, KD, 2], F32R)
        hmod = sb("hmod", [P, 2, KD, 2])
        lna = sb("lna", [P, 2, KD])
        ps = ctx.enter_context(nc.psum_tensor("ps", [P, 8, 512], F32))

        def C(k):
            return cst[:, _CST[k][0]:_CST[k][1]]
        ident, ones = C("ident"), C("ones")
        lnp = C("lnp").rearrange("p (l s g k) -> p l s g k", l=DEPTH, s=2, g=2)
        adab = C("adab").rearrange("p (l n) -> p l n", l=DEPTH)
        mu_c = C("mu").rearrange("p (i k) -> p i k", i=6)
        psc = C("psc")
        rwp = C("rw").rearrange("p (j n) -> p j n", j=KD)
        cond = C("cond").rearrange("p (k c) -> p k c", c=2)

        def pair(b, n=HT, m=P):
            return ps[0:m, 2 * b:2 * b + 2, 0:n]

        PIECES = ((0, 0, HT, 0), (1, 0, TS - HT, 0), (1, TS - HT, HT, 1))

        w_land = [sem(f"w_land{i}") for i in range(RAW)]
        w_split = sem("w_split")
        w_hi_done = sem("w_hi_done")
        w_used = sem("w_used")
        chain_dve, chain_act, chain_pool = sem("chain_dve"), sem("chain_act"), sem("chain_pool")
        stage_end = sem("stage_end")
        stage_free = sem("stage_free")
        s_init, s_const = sem("s_init"), sem("s_const")
        ada_land = [sem(f"ada_land{i}") for i in range(ADA_SLOTS)]
        ada_mm, ada_row, ada_hi, ada_lo = sem("ada_mm"), sem("ada_row"), sem("ada_hi"), sem("ada_lo")
        outs_done = sem("outs_done")

        class M:
            pass

        def scope(fill):
            m = M()
            with ExitStack() as st:
                fill(m, lambda n, s, dt=F32: sb(n, s, dt, st))
            return m

        def f_ada(L):
            def f(m, g):
                m.rows = g(f"ada_rows{L}", [2, 6 * D])
                low = [g(f"ada_ring{L}_{i}", [P, 4, 512]) for i in range(ADA_EARLY, ADA_SLOTS)]
                parts = [g(f"ada_part{L}_{i}", [P, 4, 512], F32R) for i in range(2)]
                above = (3 * KD + 7) * T
                g(f"ada_norm{L}", [P, above - 6 * D - (ADA_SLOTS - ADA_EARLY + 2) * UNIT])
                parts += [g(f"ada_part{L}_{i}", [P, 4, 512], F32R) for i in range(2, 2 * ADA_SPLITS)]
                m.hi, m.lo = parts[:ADA_SPLITS], parts[ADA_SPLITS:]
                g(f"ada_gap{L}", [P, FFN_WORDS - above - (2 * ADA_SPLITS - 2) * UNIT])
                m.ring = [g(f"ada_ring{L}_{i}", [P, 4, 512]) for i in range(ADA_EARLY)] + low
            return f

        def f_ffn(L):
            def f(m, g):
                m.hhi, m.hlo = g(f"f_hhi{L}", [P, KD, T], F32R), g(f"f_hlo{L}", [P, KD, T], F32R)
                m.t32 = g(f"f_t32{L}", [P, 2, T])
                m.sil, m.a32 = g(f"f_sil{L}", [P, 2, T]), g(f"f_a32{L}", [P, 2, T])
                m.ahi, m.alo = g(f"f_ahi{L}", [P, FHALF[0], T], F32R), g(f"f_alo{L}", [P, FHALF[0], T], F32R)
            return f

        def f_ln(t):
            def f(m, g):
                g(f"ln_gap{t}", [P, (2 * KD + 6) * T])
                m.sq = g(f"ln_sq{t}", [P, KD, T])
                m.rs = g(f"ln_rs{t}", [P, T])
            return f

        def f_mla(L):
            def f(m, g):
                m.hhi, m.hlo = g(f"m_hhi{L}", [P, KD, T], F32R), g(f"m_hlo{L}", [P, KD, T], F32R)
                m.t32 = g(f"m_t32{L}", [P, 2, T])
                m.tab, m.dup = g(f"m_tab{L}", [P, 3, T]), g(f"m_dup{L}", [P, P])
                m.qhi, m.qlo = g(f"m_qhi{L}", [P, 3, T], F32R), g(f"m_qlo{L}", [P, 3, T], F32R)
                m.khi, m.klo = g(f"m_khi{L}", [P, 2, KEYS], F32R), g(f"m_klo{L}", [P, 2, KEYS], F32R)
                m.K = g(f"m_K{L}", [P, 2, KEYS])
                with ExitStack() as e:
                    h = lambda n, s, dt=F32: sb(n, s, dt, e)
                    m.q32 = h(f"m_q32{L}", [P, 3, T])
                    m.c32 = h(f"m_c32{L}", [P, 2, KEYS])
                    m.sq = h(f"m_sq{L}", [P, 3, T])
                    m.rs = h(f"m_rs{L}", [P, 2, T])
                    m.kraw = h(f"m_kraw{L}", [P, T])
                m.V = g(f"m_V{L}", [P, 6, D])
                m.Q = g(f"m_Q{L}", [P, 2, T])
                m.pr = g(f"m_P{L}", [P, 2, T])
                m.pt = g(f"m_PT{L}", [P, 2, T])
                m.O = g(f"m_O{L}", [P, 5, P])
                m.nm = g(f"m_nm{L}", [P, 4, 2])
                m.rc = g(f"m_rc{L}", [P, 4])
                m.mx = g(f"m_mx{L}", [P, 2])
            return f

        def f_rwa(m, g):
            m.hid = {k: (g(f"r_{k}hi", [P, T], F32R), g(f"r_{k}lo", [P, T], F32R)) for k in "wag"}
            m.hset = [(g(f"r_hhi{i}", [P, KD, T], F32R), g(f"r_hlo{i}", [P, KD, T], F32R)) for i in range(2)]
            m.t32 = g("r_t32", [P, 2, T])
            m.xx = g("r_xx", [P, KD, T])
            m.o32 = g("r_o32", [P, OUT_BUFFERS, T])

        def f_rwb(m, g):
            m.par = g("s_par", [P, 7])
            m.LR = g("s_LR", [P, 4, T])
            m.r, m.k = g("s_r", [P, T]), g("s_k", [P, T])
            m.S0 = g("s_S0", [P, 2, P])
            m.v = [g(f"s_v{b}", [P, NCH, P]) for b in range(2)]
            m.gate = [g(f"s_gate{b}", [P, T]) for b in range(2)]
            m.lnx = [g(f"s_lnx{b}", [P, 2, P]) for b in range(2)]
            m.bon = [g(f"s_bon{b}", [P, NCH * 2]) for b in range(2)]
            m.F = [g(f"s_F{b}", [P, 2, 2, NCH]) for b in range(2)]
            m.Fc = [g(f"s_Fc{b}", [P, 2, NCH]) for b in range(2)]
            flat = lambda t: t.rearrange("p a t -> p (a t)").rearrange("p (c a t) -> p c a t", c=NCH, a=2)
            m.AR = [[g(f"s_AR{d}", [P, NCH, 2, P])[:, :, :, :] for d in range(2)], [flat(x[:, 2 * d:2 * d + 2, :]) for d in range(2)]]
            m.BT = [[g(f"s_BT{d}", [P, T])[:, :] for d in range(2)], [x[:, 4 + d, :] for d in range(2)]]
            m.KT = [[g(f"s_KT{d}", [P, T])[:, :] for d in range(2)], [x[:, 6 + d, :] for d in range(2)]]
            m.kk, m.nkk, m.nrm = g("s_kk", [P, T]), g("s_nkk", [P, T]), g("s_nrm", [P, T])
            m.kd = [g(f"s_kd{d}", [P, T]) for d in range(2)]
            m.b = g("s_b", [P, T])
            m.PS, m.D1, m.D2 = g("s_PS", [P, T]), g("s_D1", [P, T]), g("s_D2", [P, T])
            m.cols, m.hs = g("s_cols", [P, 1]), g("s_hs", [P, 2])
            m.onesT = g("s_ones", [P, P])
            m.E = g("s_E", [P, 3, T])
            m.AM = [[g(f"s_AM{d}{b}", [P, 2, 512]) for b in range(2)] for d in range(2)]
            m.X, m.XT, m.XF = ([g(f"s_{n}{d}", [P, 256]) for d in range(2)] for n in ("X", "XT", "XF"))
            m.Y = [g(f"s_Y{d}", [P, 256]) for d in range(2)]
            m.BK = [[g(f"s_BK{d}{b}", [P, 256]) for b in range(2)] for d in range(2)]
            m.R = [g(f"s_R{d}", [P, P]) for d in range(2)]
            m.U = [g(f"s_U{d}", [P, P]) for d in range(2)]
            m.S = [g(f"s_Sc{d}", [P, P]) for d in range(2)]
            m.So = [g(f"s_So{d}", [P, P]) for d in range(2)]
            m.st, m.pad = g("s_st", [P, 2, P]), [g(f"s_pad{n}", [P, 1]) for n in range(2)]
            m.yd = [g(f"s_y{d}", [P, NCH, P]) for d in range(2)]
            m.ys, m.y2 = g("s_ys", [P, NCH, P]), g("s_y2", [P, NCH, P])
            m.mu, m.var = g("s_mu", [P, NCH * 2]), g("s_var", [P, NCH * 2])
            m.z = g("s_z", [P, T])
            m.pm = g("s_pm", [P, 2, 512])
            m.lm = g("s_lm", [P, 2, LEVELS + 1, P])
            m.i2 = g("s_i2", [P, 256])

        def f_rwc(m, g):
            m.hhi, m.hlo = g("t_hhi", [P, KD, T], F32R), g("t_hlo", [P, KD, T], F32R)
            m.z32 = g("t_z32", [P, KD, T])

        def f_pool(m, g):
            m.hhi, m.hlo = g("p_hhi", [P, KD, T], F32R), g("p_hlo", [P, KD, T], F32R)
            m.t32 = g("p_t32", [P, 2, T])
            m.hp = g("p_hp", [P, 2, T + 64])
            m.b = g("p_b", [P, 2, T + 64])
            m.cnt = g("p_cnt", [P, 4, T])
            m.gs = g("p_gs", [P, KD, 2])

        m_ada = [scope(f_ada(L)) for L in range(DEPTH)]
        m_ffn = [scope(f_ffn(L)) for L in range(DEPTH)]
        m_ln = [scope(f_ln(t)) for t in range(2 * DEPTH)]
        m_mla = {L: scope(f_mla(L)) for L in range(DEPTH) if MIXER[L] == 0}
        m_rwa, m_rwb, m_rwc, m_pool = scope(f_rwa), scope(f_rwb), scope(f_rwc), scope(f_pool)

        r_d = nc.dram_tensor("r_scratch", (KD, P, T), F32, kind="Internal").ap()
        k_d = nc.dram_tensor("k_scratch", (KD, P, T), F32, kind="Internal").ap()
        v_d = nc.dram_tensor("v_scratch", (NCH, P, D), F32, kind="Internal").ap()
        up_d = nc.dram_tensor("up_scratch", (KD, 5, P, T), F32, kind="Internal").ap()
        x_d = nc.dram_tensor("x_scratch", (KD, P, T), F32, kind="Internal").ap()
        z_d = nc.dram_tensor("z_scratch", (KD, P, T), F32, kind="Internal").ap()

        def sems(tag, names):
            return namedtuple("Sems", names)(*[sem(f"{tag}_{n}") for n in names.split()])

        def uses(tag, counts, n, primed=()):
            q = sems(tag, " ".join(counts))
            at = namedtuple("At", list(counts))
            use = namedtuple("Use", ["at", *counts])
            return [use(at(*[(k in primed) + u * v for k, v in counts.items()]), *q) for u in range(n)]

        splits = [t for t in range(2 * DEPTH) if t % 2 or MIXER[t // 2] != 1]
        q_split = dict(zip(splits, uses("split", dict(val=KD, hi=KD, lo=KD), len(splits))))
        q_ln = uses("ln", dict(mean=1, cen=KD, sq=KD, var=1, rsd=1, nrm=KD), 2 * DEPTH)
        q_ffn = uses("ffn", dict(mm=NF, sil=NF, act=NF, hi=NF, lo=NF, down=2 * KD, upd=2 * KD), DEPTH)
        q_out = uses("out", dict(mm=KD, upd=KD), DEPTH)
        q_mla = dict(zip(m_mla, uses("mla", dict(
            tab=112, in_mm=6, in_ev=6, st=2, v_mm=15, v_ev=12, head_mm=24, q_ev=16, sc=80, nmax=80, pexp=80, tr=80,
            ptc=80, av=80, oev=80, ot=8, ohi=16, olo=16, cd=3, rsd=1, hi2=2, rec=80, mx=80), len(m_mla), ("oev", "olo"))))
        q_rwa = sems("rwa", "val hi lo mm ev hid hidlo st xst")
        s_rst = [sem(f"rwa_store{i}") for i in range(OUT_BUFFERS)]
        q_rwb = sems("rwb", "zlo ld ld2 e0 kksq nrm nr nrd scan dec ka ex til tsum tmu tsq tvar trc zc zg sst sc0 sc1 x10 x11 tok0 tok1 inv0 inv1 x0 x1 r0 r1 rev0 rev1 "
                            "t0 t1 tev0 tev1 u0 u1 uev0 uev1 y0 y1 yev0 yev1 S0 S1 rsd bon bonc zt z zst st")
        s_zld = [sem(f"rwb_zload{i}") for i in range(KD // 2)]
        q_pool = sems("pool", "cst st hp")

        class Ends:

            def __init__(self, eng):
                self.eng, self.n = eng, 0

            def __call__(self):
                self.n += 1
                self.eng.drain().then_inc(stage_end, 1)
                self.eng.wait_ge(stage_end, 3 * self.n)

        ENDS_OF_MIXER = [4, 3, 1]

        def ends_of_layers(L):
            return 1 + sum(2 + ENDS_OF_MIXER[MIXER[l]] + 1 for l in range(L))

        block = ctx.enter_context(nc.Block())

        @block.sync
        def _(sp):
            sp.dma_start(cst[:, :], a["cst"]).then_inc(s_const, 16)
            sp.dma_start(x[:, :, :], a["x"].rearrange("k p t -> p k t")).then_inc(s_const, 16)
            done = 0

            def chunk(slot, n, src, wait):
                if wait is not None:
                    sp.wait_ge(w_split, wait)
                sp.dma_start(raw[:, slot, :], src).then_inc(w_land[slot], 16)

            def stream(first, last):
                n = first
                while n < last:
                    loops = (last - n) // RAW
                    if n >= RAW and n % RAW == 0 and loops > 1:
                        with sp.Fori(0, loops) as i:
                            for u in range(RAW):
                                chunk(u, n, a["w"][i * RAW + (n + u)], i * RAW + (n + u - RAW + 1))
                        n += loops * RAW
                    else:
                        chunk(n % RAW, n, a["w"][n], n - RAW + 1 if n >= RAW else None)
                        n += 1

            for L in range(DEPTH):
                src = a["ada_w"][L].rearrange("(k p) n -> p k n", p=P)
                for u in range(ADA_UNITS):
                    unit, slot = ADA_UNITS * L + u, u % ADA_SLOTS
                    if L and u == 0:
                        sp.wait_ge(stage_end, 3 * (ends_of_layers(L) - 1))
                    if L and u == ADA_EARLY:
                        sp.wait_ge(stage_end, 3 * ends_of_layers(L))
                    if u >= ADA_SLOTS:
                        sp.wait_ge(ada_lo, unit - ADA_SLOTS + 1)
                    sp.dma_start(m_ada[L].ring[slot][:, :, :],
                                 src[:, 4 * (u % 2):4 * (u % 2) + 4, (u // 2) * 512:(u // 2 + 1) * 512]
                                 ).then_inc(ada_land[slot], 16)
                stream(LAYER_BASE[L], LAYER_BASE[L + 1])

        @block.gpsimd
        def _(pool):
            nc.gpsimd.memset(zrow[:, :], 0.0).then_inc(s_init, 1)
            pool.wait_ge(s_init, 1)

            def split(raw_slot, slot, land, used, n1):
                pool.wait_ge(w_land[raw_slot], land)
                if used is not None:
                    pool.wait_ge(w_used, used)
                nc.gpsimd.tensor_tensor(whi[:, slot, :], raw[:, raw_slot, :], zrow[:, 0:1].to_broadcast([P, CH * P]), ALU.add).then_inc(w_hi_done, 1)
                pool.wait_ge(w_hi_done, n1)
                nc.gpsimd.tensor_tensor(wlo[:, slot, :], raw[:, raw_slot, :], whi[:, slot, :].bitcast(F32),
                                        ALU.subtract).then_inc(w_split, 1)

            body = RAW * RS

            def stream(first, last):
                n = first
                while n < last:
                    if n >= body and n % body == 0 and last - n >= 2 * body:
                        with pool.Fori(n // body, last // body) as i:
                            for u in range(body):
                                split(u % RAW, u % RS, i * (16 * RS) + 16 * (u // RAW + 1), i * body + (u - RS + 1), i * body + (u + 1))
                        n = last // body * body
                    else:
                        split(n % RAW, n % RS, 16 * (n // RAW + 1), n - RS + 1 if n >= RS else None, n + 1)
                        n += 1

            def heads():
                m, q = m_rwb, q_rwb
                ch = Chain(pool, chain_pool)
                tt = nc.gpsimd.tensor_tensor

                def c3(t):
                    return t.rearrange("p (c t) -> p c t", c=NCH)

                def decays(j, d):
                    pool.wait_ge(q.scan, j * 2 + (d + 1))
                    PS = c3(m.PS[:, :])
                    ch(tt(c3(m.D1[:, :]), PS, PS[:, :, 63:64].to_broadcast([P, NCH, P]), ALU.subtract))
                    tt(m.D2[:, :], m.D1[:, :], m.LR[:, d, :], ALU.subtract).then_inc(q.dec, 1)

                def keys(j, d):
                    pool.wait_ge(q.ka, j * 2 + (d + 1))
                    tt(m.kd[d][:, :], m.kd[d][:, :], m.k[:, :], ALU.mult)
                    ch(tt(m.b[:, :], m.kk[:, :], m.LR[:, 2 + d, :], ALU.mult))

                def scaled(j, b, d):
                    E = m.E
                    tt(m.BT[b][d], m.b[:, :], E[:, 2, :], ALU.mult)
                    tt(m.KT[b][d], m.kd[d][:, :], E[:, 2, :], ALU.mult)
                    tt(m.AR[b][d][:, :, 1, :], c3(m.r[:, :]), c3(E[:, 0, :]), ALU.mult)
                    before, after = (slice(1, 4), slice(0, 3)) if d == 0 else (slice(0, 3), slice(1, 4))
                    tt(m.Fc[b][:, d, after], m.F[b][:, d, 1, after], m.F[b][:, d, 0, before], ALU.mult)
                    return tt(m.AR[b][d][:, :, 0, :], c3(m.nkk[:, :]), c3(E[:, 1, :]), ALU.mult)

                def prepare_a(j):
                    decays(j, 0)
                    pool.wait_ge(q.nrd, j + 1)
                    ch(tt(m.kk[:, :], m.kk[:, :], m.nrm[:, :], ALU.mult))
                    ch(tt(m.nkk[:, :], zrow[:, 0:1].to_broadcast([P, T]), m.kk[:, :], ALU.subtract))
                    keys(j, 0)

                def prepare_b(j, b):
                    pool.wait_ge(q.ex, j * 2 + 1)
                    decays(j, 1)
                    scaled(j, b, 0).then_inc(q.e0, 1)
                    pool.wait_ge(q.e0, j + 1)
                    keys(j, 1)
                    pool.wait_ge(q.ex, j * 2 + 2)
                    ch(scaled(j, b, 1))
                    ch(tt(m.b[:, :], m.kd[0][:, :], m.kd[1][:, :], ALU.add))
                    tt(m.b[:, :], m.b[:, :], m.r[:, :], ALU.mult).then_inc(q.til, 1)

                def prepare(j, b):
                    prepare_a(j)
                    prepare_b(j, b)

                def h2(t):
                    return t[:, :, :].rearrange("p c (h n) -> p (c h) n", h=2)

                def finish_a(j, b):
                    y, y2, B10 = h2(m.ys), h2(m.y2), [P, 2 * NCH, 64]
                    pool.wait_ge(q.yev0, j * 5 + 5)
                    pool.wait_ge(q.yev1, j * 5 + 5)
                    tt(m.ys[:, :, :], m.yd[0][:, :, :], m.yd[1][:, :, :], ALU.add).then_inc(q.tsum, 1)
                    pool.wait_ge(q.tmu, j + 1)
                    ch(tt(y, y, m.mu[:, :].unsqueeze(2).to_broadcast(B10), ALU.subtract))
                    tt(y2, y, y, ALU.mult).then_inc(q.tsq, 1)
                    pool.wait_ge(q.tvar, j + 1)
                    pool.wait_ge(q.bonc, j + 1)
                    ch(tt(y2, h2(m.v[b]), m.bon[b][:, :].unsqueeze(2).to_broadcast(B10), ALU.mult))
                    pool.wait_ge(q.trc, j + 1)
                    ch(tt(y, y, m.var[:, :].unsqueeze(2).to_broadcast(B10), ALU.mult))
                    lx = lambda n: m.lnx[b][:, n:n + 1, :].to_broadcast([P, NCH, P])
                    ch(tt(m.ys[:, :, :], m.ys[:, :, :], lx(0), ALU.mult))
                    ch(tt(m.ys[:, :, :], m.ys[:, :, :], lx(1), ALU.add))
                    tt(m.y2[:, :, :], m.y2[:, :, :], m.ys[:, :, :], ALU.add).then_inc(q.zt, 1)

                def finish_b(j, b):
                    pool.wait_ge(q.zc, j + 1)
                    tt(m.z[:, :], m.z[:, :], m.gate[b][:, :], ALU.mult).then_inc(q.zg, 1)

                def finish(j, b):
                    finish_a(j, b)
                    finish_b(j, b)

                def one(j, b, first, last):
                    if not first:
                        finish_a(j - 1, 1 - b)
                    if not last:
                        prepare_a(j + 1)
                    if not first:
                        finish_b(j - 1, 1 - b)
                    if not last:
                        prepare_b(j + 1, 1 - b)
                every_pair(pool, one, prepare, finish, ch, RW_POOL)

            heads_at = LAYER_BASE[1] + C_RWKV_LORA + C_RWKV_UP + C_RWKV_RKV + RS - 1
            stream(0, heads_at)
            heads()
            stream(heads_at, NCHUNK)

        @block.tensor
        def _(pe):
            W = Weights(pe, whi, wlo, w_split, w_used)
            end = Ends(pe)
            mm = nc.tensor.matmul

            def panel(KT, hi, lo, b, ready=None):
                for kt in range(KT):
                    if ready is not None:
                        pe.wait_ge(ready[0], ready[1] + kt + 1)
                    wh, wl = W.next()
                    n = 0
                    for w, r in ((wh, hi(kt)), (wl, hi(kt)), (wh, lo(kt))):
                        for h in range(2):
                            last = mm(ps[:, 2 * b + h, 0:HT], w, r[:, h * HT:(h + 1) * HT],
                                      start=kt == 0 and n < 2, stop=kt == KT - 1 and n >= 4)
                            W.first(last)
                            n += 1
                return last

            def ada(L, t):
                m = m_ada[L]
                for cb in range(12):
                    if t is not None and cb == 0:
                        means(t)
                    if t is not None and cb == 3:
                        variances(t)
                    g = 12 * L + cb
                    if cb >= 2:
                        pe.wait_ge(ada_row, g - 1)
                    for kh in range(2):
                        unit = 2 * g + kh
                        pe.wait_ge(ada_lo, unit + 1)
                        hi, lo = m.hi[unit % ADA_SPLITS], m.lo[unit % ADA_SPLITS]
                        for n, (w, r) in enumerate(((sc_hi, hi), (sc_lo, hi), (sc_hi, lo))):
                            for k in range(4):
                                last = mm(ps[0:2, 4 + cb % 2, :], w[:, 4 * kh + k, :], r[:, k, :],
                                          start=kh == 0 and n == 0 and k == 0, stop=kh == 1 and n == 2 and k == 3)
                        last.then_inc(ada_mm, 1)
                pe.wait_ge(ada_row, 12 * (L + 1))
                for n in range(48):
                    mm(ps[:, 6, 2 * n:2 * n + 2], m.rows[0:2, n * P:(n + 1) * P], ident[0:2, 0:2], start=True, stop=True)
                end()
                end()

            def means(t):
                q = q_ln[t]
                for kt in range(KD):
                    for h in range(2):
                        last = mm(ps[:, h, 0:HT], ones, x[:, kt, h * HT:(h + 1) * HT], start=kt == 0, stop=kt == KD - 1)
                last.then_inc(q.mean, 1)

            def variances(t):
                m, q = m_ln[t], q_ln[t]
                for kt in range(KD):
                    pe.wait_ge(q.sq, q.at.sq + kt + 1)
                    for h in range(2):
                        last = mm(ps[:, 2 + h, 0:HT], ones, m.sq[:, kt, h * HT:(h + 1) * HT], start=kt == 0, stop=kt == KD - 1)
                last.then_inc(q.var, 1)

            def ffn(L):
                m, q = m_ffn[L], q_ffn[L]
                means(2 * L)
                variances(2 * L)
                f0, dn = 0, 0
                for nf in FHALF:
                    def gate_up(u, i):
                        if i is not None:
                            pe.wait_ge(q.act, q.at.act + i * 2 + (f0 + u - 1))
                        elif f0 + u >= 2:
                            pe.wait_ge(q.act, q.at.act + f0 + u - 1)
                        panel(KD, lambda k: m.hhi[:, k, :], lambda k: m.hlo[:, k, :], 2 * (u % 2),
                              splits(q_split[2 * L + 1]) if f0 + u == 0 else None)
                        panel(KD, lambda k: m.hhi[:, k, :], lambda k: m.hlo[:, k, :], 2 * (u % 2) + 1).then_inc(q.mm, 1)
                    if f0:
                        pe.wait_ge(q.upd, q.at.upd + dn)
                    gate_up(0, None)
                    gate_up(1, None)
                    with pe.Fori(0, nf // 2 - 1) as i:
                        W.enter(i, 4)
                        gate_up(2, i)
                        gate_up(3, i)
                        W.leave(nf // 2 - 1)
                    f0 += nf
                    pe.wait_ge(q.act, q.at.act + f0)
                    pe.wait_ge(q.lo, q.at.lo + f0)
                    for c in range(KD):
                        if c >= 4:
                            pe.wait_ge(q.upd, q.at.upd + dn - 3)
                        panel(nf, lambda k: m.ahi[:, k, :], lambda k: m.alo[:, k, :], c % 4).then_inc(q.down, 1)
                        dn += 1
                end()

            def splits(q):
                return q.lo, q.at.lo

            def out_proj(L, hhi, hlo, ready=None):
                q = q_out[L]
                for c in range(KD):
                    if c >= 4:
                        pe.wait_ge(q.upd, q.at.upd + c - 3)
                    panel(KD, lambda k: hhi[:, k, :], lambda k: hlo[:, k, :], c % 4, None if c else ready).then_inc(q.mm, 1)
                end()

            def mla(L):
                m, q = m_mla[L], q_mla[L]
                for p in range(6):
                    if p >= 4:
                        pe.wait_ge(q.in_ev, q.at.in_ev + p - 3)
                    panel(KD, lambda k: m.hhi[:, k, :], lambda k: m.hlo[:, k, :], p % 4,
                          None if p else splits(q_split[2 * L])).then_inc(q.in_mm, 1)
                pe.wait_ge(q.in_ev, q.at.in_ev + 6)
                pe.wait_ge(q.st, q.at.st + 1)
                for kt in range(3):
                    for h in range(2):
                        last = mm(ps[:, h, 0:HT], ones, m.sq[:, kt, h * HT:(h + 1) * HT], start=kt == 0, stop=kt == 2)
                last.then_inc(q.v_mm, 1)
                pe.wait_ge(q.st, q.at.st + 2)
                for kt in range(2):
                    for h in range(2):
                        last = mm(ps[:, 2 + h, 0:HT], ones, m.sq[:, kt, h * HT:(h + 1) * HT], start=kt == 0, stop=kt == 1)
                last.then_inc(q.v_mm, 1)
                for h in range(2):
                    last = mm(ps[:, 4 + h, 0:HT], m.dup[0:64, :], m.kraw[0:64, h * HT:(h + 1) * HT], start=True, stop=True)
                last.then_inc(q.v_mm, 1)
                end()
                ch = [W.next(8)]
                held = W.owed
                ch.append(W.next(8))
                assert held
                n = 0
                for kb in range(6):
                    for h in range(2):
                        if n >= 4:
                            pe.wait_ge(q.v_ev, q.at.v_ev + n - 3)
                        i = 0
                        for kt in range(2):
                            wh, wl = ch[kt]
                            khi, klo = m.khi[:, kt, kb * P:(kb + 1) * P], m.klo[:, kt, kb * P:(kb + 1) * P]
                            for l, r in ((khi, wh), (klo, wh), (khi, wl)):
                                last = mm(ps[:, n % 4, :], l, r[:, h * 512:(h + 1) * 512], start=i == 0, stop=i == 5)
                                W.first(last)
                                i += 1
                        last.then_inc(q.v_mm, 1)
                        n += 1
                pe.drain().then_inc(w_used, 1)
                end()
                with pe.Fori(0, 2) as j4:
                  W.enter(j4, 4)
                  for ju in range(4):
                    j = j4 * 4 + ju
                    pe.wait_ge(q.oev, q.at.oev + j * 10)
                    for kt in range(2):
                        wh, wl = W.next()
                        n = 0
                        for w, r in ((wh, m.khi), (wl, m.khi), (wh, m.klo)):
                            for h in range(2):
                                last = mm(ps[:, 4 + h, 0:KEYS // 2], w, r[:, kt, h * (KEYS // 2):(h + 1) * (KEYS // 2)],
                                          start=kt == 0 and n < 2, stop=kt == 1 and n >= 4)
                                W.first(last)
                                n += 1
                    last.then_inc(q.head_mm, 1)
                    for hh in range(2):
                        panel(3, lambda k: m.qhi[:, k, :], lambda k: m.qlo[:, k, :], hh).then_inc(q.head_mm, 1)

                    def scores(u):
                        hh, qt = divmod(u, 5)
                        if u < 2:
                            pe.wait_ge(q.q_ev, q.at.q_ev + j * 2 + (u + 1))
                        else:
                            pe.wait_ge(q.pexp, q.at.pexp + j * 10 + (u - 1))
                        k0, nk = (0, T) if qt < 4 else (T, P)
                        b = 2 * (u % 2)
                        if nk == P:
                            last = mm(ps[:, b, 0:P], m.Q[:, hh, qt * P:(qt + 1) * P], m.K[:, hh, k0:k0 + P], start=True, stop=True)
                        else:
                            for h in range(2):
                                last = mm(ps[:, b + h, 0:HT], m.Q[:, hh, qt * P:(qt + 1) * P],
                                          m.K[:, hh, h * HT:(h + 1) * HT], start=True, stop=True)
                        last.then_inc(q.sc, 1)

                    def turn(u):
                        hh, qt = divmod(u, 5)
                        pe.wait_ge(q.pexp, q.at.pexp + j * 10 + (u + 1))
                        if u >= 1:
                            pe.wait_ge(q.ptc, q.at.ptc + j * 10 + u)
                        for kb in range(5 if qt < 4 else 1):
                            last = nc.tensor.transpose(ps[:, 4 + kb // 4, (kb % 4) * P:(kb % 4 + 1) * P],
                                                       m.pr[:, u % 2, kb * P:(kb + 1) * P], ident)
                        last.then_inc(q.tr, 1)

                    def av(u):
                        hh, qt = divmod(u, 5)
                        pe.wait_ge(q.ptc, q.at.ptc + j * 10 + (u + 1))
                        if u >= 1:
                            pe.wait_ge(q.oev, q.at.oev + j * 10 + u)
                        else:
                            pe.wait_ge(q.olo, q.at.olo + j * 2)
                        nk = 5 if qt < 4 else 1
                        for kb in range(nk):
                            kt = kb if qt < 4 else 5
                            last = mm(ps[:, 6, 0:64], m.pt[:, u % 2, kb * P:(kb + 1) * P],
                                      m.V[:, kt, bass.ds(j * P + hh * 64, 64)], start=kb == 0, stop=kb == nk - 1)
                        last.then_inc(q.av, 1)

                    scores(0)
                    for u in range(11):
                        if u < 9:
                            scores(u + 1)
                        if u < 10:
                            turn(u)
                        if u:
                            av(u - 1)
                    pe.wait_ge(q.oev, q.at.oev + j * 10 + 10)
                    for qt in range(5):
                        last = nc.tensor.transpose(ps[:, 7 - qt // 4, (qt % 4) * P:(qt % 4 + 1) * P], m.O[:, qt, :], ident)
                    last.then_inc(q.ot, 1)
                  W.leave(2)
                pe.wait_ge(q.olo, q.at.olo + 2 * (HEADS // 2))
                end()
                out_proj(L, m.hhi, m.hlo)

            def rwkv(L):
                m, q = m_rwa, q_rwa
                n = 0

                def groups(hi, lo, count, KT=KD, ready=None):
                    nonlocal n
                    for c in range(count):
                        if n >= 4:
                            pe.wait_ge(q.ev, n - 3)
                        panel(KT, lambda k: hi(c, k), lambda k: lo(c, k), n % 4, None if c else ready).then_inc(q.mm, 1)
                        n += 1

                for idx in range(6):
                    hi, lo = m.hset[idx % 2]
                    if idx < 5:
                        groups(lambda c, k: hi[:, k, :], lambda c, k: lo[:, k, :], 1 if idx < 3 else KD, ready=(q.lo, KD * idx))
                        if idx == 2:
                            pe.wait_ge(q.hidlo, 3)
                            groups(lambda c, k: m.hid["wwaag"[c % 5]][0][:, :], lambda c, k: m.hid["wwaag"[c % 5]][1][:, :],
                                   5 * KD, 1)
                    else:
                        pe.wait_ge(q.lo, 6 * KD)
                        pe.wait_ge(q.ev, n)
                        for h in range(2):
                            if h:
                                pe.wait_ge(q.ev, n + 5)
                            for kt in range(KD):
                                wh, wl = W.next(4)
                                for tt in range(NCH):
                                    t0 = tt * P
                                    for p, (l, r) in enumerate(((hi, wh), (lo, wh), (hi, wl))):
                                        last = mm(ps[:, tt, :], l[:, kt, t0:t0 + P], r, start=kt == 0 and p == 0,
                                                  stop=kt == KD - 1 and p == 2)
                                        W.first(last)
                            last.then_inc(q.mm, 1)
                end()
                m, q = m_rwb, q_rwb
                sc, x1, tok, inv, xs = (q.sc0, q.sc1), (q.x10, q.x11), (q.tok0, q.tok1), (q.inv0, q.inv1), (q.x0, q.x1)
                rr, rev, uu, uev = (q.r0, q.r1), (q.rev0, q.rev1), (q.u0, q.u1), (q.uev0, q.uev1)
                yy, yev, SS = (q.y0, q.y1), (q.yev0, q.yev1), (q.S0, q.S1)
                tt_, tev = (q.t0, q.t1), (q.tev0, q.tev1)

                def wait(semaphore, v):
                    if not isinstance(v, int) or v > 0:
                        pe.wait_ge(semaphore, v)

                def scores(j, b, s):
                    for d in range(2):
                        c = chunk_of(d, s)
                        if s == 0:
                            pe.wait_ge(q.til, j + 1)
                        wait(xs[d], j * 130 + 26 * s)
                        wait(yev[d], j * 5 + (s - 1))
                        for hh in range(2):
                            rows = slice(64 * hh, 64 * hh + 64)
                            rhs = m.AR[b][d][rows, c, :, :].rearrange("p a t -> p (a t)")
                            mm(ps[:, 4 * d + hh, 0:256], m.BT[b][d][rows, c * P:(c + 1) * P], rhs, start=True, stop=True)
                            mm(ps[:, 4 * d + hh, 256:512], m.KT[b][d][rows, c * P:(c + 1) * P], rhs, start=True, stop=True)
                        nc.tensor.transpose(ps[:, 4 * d + 2, 0:P], m.BT[b][d][:, c * P:(c + 1) * P], ident)
                        nc.tensor.transpose(ps[:, 4 * d + 2, P:2 * P], m.KT[b][d][:, c * P:(c + 1) * P], ident).then_inc(sc[d], 1)

                def start_inverse(j, b, s):
                    for d, hh in GROUPS:
                        pe.wait_ge(x1[d], j * 5 + (s + 1))
                        nc.tensor.transpose(ps[:, 4 * d + hh, 0:P], m.XT[d][:, hh * P:(hh + 1) * P], ident).then_inc(inv[d], 1)

                def level_a(j, b, s, l, first):
                    for d, hh in GROUPS:
                        X = m.X[d][:, hh * P:(hh + 1) * P]
                        pe.wait_ge(xs[d], j * 130 + (26 * s + 4 * l - 3 + hh))
                        mm(ps[:, 4 * d + hh, 0:P], m.AM[d][(b + s) % 2][:, hh, 0:P], X, start=True, stop=True).then_inc(inv[d], 1)
                        if l > 1:
                            if l == 2 and hh and s == 0 and first:
                                pe.wait_ge(tok[d], j * 5 + 1)
                            elif l == 2 and hh:
                                pe.wait_ge(yev[d], j * 5 + s)
                            elif l == 2 and not (s == 0 and first):
                                pe.wait_ge(SS[d], j * 6 + (s + 1))
                            nc.tensor.transpose(ps[:, 4 * d + 3 - hh, 0:P], X, ident).then_inc(tt_[d], 1)

                def level_b(j, b, s, l):
                    for d, hh in GROUPS:
                        XT, Y = m.XT[d][:, hh * P:(hh + 1) * P], m.Y[d][:, hh * P:(hh + 1) * P]
                        pe.wait_ge(xs[d], j * 130 + (26 * s + 4 * l - 1 + hh))
                        if l >= 2:
                            pe.wait_ge(tev[d], j * 50 + (10 * s + 2 * l - 3 + hh))
                        w, r = (XT, Y) if l < LEVELS else (Y, XT)
                        mm(ps[:, 4 * d + hh, P:2 * P], w, r, start=True, stop=True).then_inc(inv[d], 1)

                def rhs(j, b, s, final=False):
                    for d in range(2):
                        c = chunk_of(d, s)
                        pe.wait_ge(SS[d], j * 6 + (s + 1))
                        pe.wait_ge(tok[d], j * 5 + (s + 1 if final else s + 2))
                        out = ps[:, 4 * d + 2, 256:384]
                        mm(out, m.AR[b][d][:, c, 0, :], m.S[d][:, :], start=True, stop=False)
                        for hh in range(2):
                            last = mm(out[:, 64 * hh:64 * hh + 64], m.AM[d][(b + s) % 2][:, hh, 256:384],
                                      m.v[b][:, c, 64 * hh:64 * hh + 64], start=False, stop=hh == 1)
                        last.then_inc(rr[d], 1)

                def solve(j, b, s):
                    for d in range(2):
                        pe.wait_ge(rev[d], j * 5 + (s + 1))
                        pe.wait_ge(xs[d], j * 130 + (26 * s + 26))
                        for hh in range(2):
                            last = mm(ps[:, 4 * d + 2, 384 + 64 * hh:448 + 64 * hh], m.XF[d][:, hh * P:(hh + 1) * P],
                                      m.R[d][:, 64 * hh:64 * hh + 64], start=True, stop=True)
                        last.then_inc(uu[d], 1)

                def output(j, b, s):
                    for d in range(2):
                        c = chunk_of(d, s)
                        am, bk = m.AM[d][(b + s) % 2], m.BK[d][(b + s) % 2]
                        pe.wait_ge(uev[d], j * 5 + (s + 1))
                        out = ps[:, 4 * d + 2, 256:384]
                        mm(out, m.AR[b][d][:, c, 1, :], m.S[d][:, :], start=True, stop=False)
                        for hh in range(2):
                            half = slice(64 * hh, 64 * hh + 64)
                            mm(out[:, half], am[:, hh, P:2 * P], m.U[d][:, half], start=False, stop=False)
                            mm(out[:, half], am[:, hh, 384:512], m.v[b][:, c, half], start=False, stop=hh == 1)
                        out = ps[:, 4 * d + 3, 0:P]
                        mm(out, bk[:, 0:P], m.U[d][:, :], start=True, stop=False)
                        last = mm(out, bk[:, P:2 * P], m.v[b][:, c, :], start=False, stop=True)
                        last.then_inc(yy[d], 1)

                def norms(j):
                    pe.wait_ge(q.kksq, j + 1)
                    for h in range(2):
                        last = mm(ps[:, 3 + 4 * h, 192:512], C("blk"), m.nkk[:, h * HT:(h + 1) * HT], start=True, stop=True)
                    last.then_inc(q.nrm, 1)

                def bonus(j):
                    for c in range(NCH):
                        last = mm(ps[:, 3, 128 + 2 * c:130 + 2 * c], m.b[:, c * P:(c + 1) * P], m.hs[:, :], start=True, stop=True)
                    last.then_inc(q.bon, 1)

                def turned_output(j):
                    pe.wait_ge(q.zt, j + 2)
                    for c in range(NCH):
                        last = nc.tensor.transpose(ps[:, 3 + 4 * (c // 3), (1 + c % 3) * P:(2 + c % 3) * P], m.y2[:, c, :], ident)
                    last.then_inc(q.z, 1)

                def prepare(j, b):
                    norms(j)

                def finish(j, b):
                    rhs(j, b, NCH - 1, final=True)
                    solve(j, b, NCH - 1)
                    output(j, b, NCH - 1)
                    turned_output(j)

                def one(j, b, first, last):
                    for s in range(NCH):
                        before = (j, b, s - 1) if s else (j - 1, 1 - b, NCH - 1)
                        go = s > 0 or not first
                        scores(j, b, s)
                        if go:
                            rhs(*before)
                        start_inverse(j, b, s)
                        level_a(j, b, s, 1, first)
                        if go:
                            solve(*before)
                        level_b(j, b, s, 1)
                        if go:
                            output(*before)
                        for l in range(2, LEVELS + 1):
                            if l == 3:
                                if s == 0:
                                    pe.wait_ge(q.bonc, j + 1)
                                if s == 1 and not last:
                                    pe.wait_ge(q.nr, j + 2)
                                if s == 2 and not first:
                                    pe.wait_ge(q.zc, j)
                            level_a(j, b, s, l, first)
                            if l == 2:
                                for d in range(2):
                                    pe.wait_ge(tev[d], j * 50 + (10 * s + 1))
                                if s == 0:
                                    bonus(j)
                                if s == 1 and not last:
                                    norms(j + 1)
                                if s == 2 and not first:
                                    turned_output(j - 1)
                            level_b(j, b, s, l)
                every_pair(pe, one, prepare, finish)
                end()
                out_proj(L, m_rwc.hhi, m_rwc.hlo, (q.zlo, 0))

            def pooling(L):
                m, q, (lo, at) = m_pool, q_out[L], splits(q_split[2 * L])
                for c in range(KD):
                    if c >= 4:
                        pe.wait_ge(q.upd, q.at.upd + c - 3)
                    g = c // 2
                    pe.wait_ge(lo, at + 2 * g + 2)
                    panel(2, lambda k: m.hhi[:, 2 * g + k, :], lambda k: m.hlo[:, 2 * g + k, :], c % 4).then_inc(q.mm, 1)
                end()

            pe.wait_ge(s_const, 32)
            end()
            for L in range(DEPTH):
                ada(L, 2 * L - 1 if L else None)
                (mla, rwkv, pooling)[MIXER[L]](L)
                ffn(L)
            means(2 * DEPTH - 1)
            variances(2 * DEPTH - 1)
            end()

        @block.scalar
        def _(act):
            end = Ends(act)
            ch = Chain(act, chain_act)
            af = nc.scalar.activation

            def ada(L, t):
                m = m_ada[L]
                for u in range(ADA_UNITS + 3):
                    unit = ADA_UNITS * L + u
                    if t is not None and u == 3:
                        squares(t)
                    if t is not None and u == 8:
                        deviations(t)
                    if u < ADA_UNITS:
                        act.wait_ge(ada_land[unit % ADA_SLOTS], 16 * (unit // ADA_SLOTS + 1))
                        if unit >= ADA_SPLITS:
                            act.wait_ge(ada_mm, unit - ADA_SPLITS + 1)
                        nc.scalar.copy(m.hi[unit % ADA_SPLITS][:, :, :], m.ring[unit % ADA_SLOTS][:, :, :]).then_inc(ada_hi, 1)
                    if u >= 4 and u % 2 == 0:
                        cb = u // 2 - 2
                        act.wait_ge(ada_mm, ADA_UNITS * L + 2 * cb + 2)
                        nc.scalar.copy(m.rows[0:2, cb * 512:(cb + 1) * 512], ps[0:2, 4 + cb % 2, :]).then_inc(ada_row, 1)
                end()
                if MIXER[L] == 1:
                    act.dma_start(x_d.rearrange("k p t -> p k t"), x[:, :, :]).then_inc(q_rwa.xst, 16)
                end()

            def split_h(t, src, col, t32, hhi, ready=None):
                q = q_split[t]
                for kt in range(KD + 1):
                    if kt >= 1:
                        act.wait_ge(q.val, q.at.val + kt)
                        nc.scalar.copy(hhi[:, kt - 1, :], t32[:, (kt - 1) % 2, :]).then_inc(q.hi, 1)
                    if kt < KD:
                        if kt >= 2:
                            act.wait_ge(q.lo, q.at.lo + kt - 1)
                        if ready is not None:
                            act.wait_ge(ready.nrm, ready.at.nrm + kt + 1)
                        for cd, (t0, t1) in enumerate(((0, TS), (TS, T))):
                            scale, shift = col(kt, cd)
                            last = af(t32[:, kt % 2, t0:t1], src[:, kt, t0:t1], ACT.Identity, bias=shift, scale=scale)
                        last.then_inc(q.val, 1)

            def squares(t):
                m, q = m_ln[t], q_ln[t]
                for kt in range(KD):
                    act.wait_ge(q.cen, q.at.cen + kt + 1)
                    af(m.sq[:, kt, :], x[:, kt, :], ACT.Square).then_inc(q.sq, 1)

            def deviations(t):
                m, q = m_ln[t], q_ln[t]
                act.wait_ge(q.var, q.at.var + 1)
                af(halves(m.rs[:, :]), pair(1), ACT.Sqrt, bias=eps[:, 0:1], scale=1.0 / D).then_inc(q.rsd, 1)

            def ffn(L):
                m, q = m_ffn[L], q_ffn[L]
                squares(2 * L)
                deviations(2 * L)
                split_h(2 * L + 1, m_ln[2 * L].sq, lambda kt, cd: (hmod[:, 0, kt, cd:cd + 1], hmod[:, 1, kt, cd:cd + 1]),
                        m.t32, m.hhi, q_ln[2 * L])
                f0 = 0
                for nf in FHALF:
                    with act.Fori(0, nf // 2) as i:
                        for u in range(2):
                            act.wait_ge(q.mm, q.at.mm + i * 2 + (f0 + u + 1))
                            af(halves(m.sil[:, u, :]), pair(2 * u), ACT.Silu).then_inc(q.sil, 1)
                            act.wait_ge(q.act, q.at.act + i * 2 + (f0 + u + 1))
                            nc.scalar.copy(m.ahi[:, i * 2 + u, :], m.a32[:, u, :]).then_inc(q.hi, 1)
                    f0 += nf
                    act.wait_ge(q.down, q.at.down + KD * (1 if f0 < NF else 2))
                end()

            def mla(L):
                m, q = m_mla[L], q_mla[L]
                jj = L // 3
                act.dma_start(m.tab[:, :, :], a["tab"]).then_inc(q.tab, 16)
                act.dma_start(m.dup[:, :], a["dup"]).then_inc(q.tab, 16)
                act.dma_start(m.c32[:, :, 0:PAST], a["ckvT"][jj]).then_inc(q.tab, 16)
                for hh, r0 in ((0, 64), (0, 96), (1, 0), (1, 32)):
                    act.dma_start(m.K[r0:r0 + 32, hh, 0:PAST], a["kpeT"][jj]).then_inc(q.tab, 16)
                split_h(2 * L, x, lambda kt, cd: (mod[:, KD + kt, cd:cd + 1], mod[:, kt, cd:cd + 1]), m.t32, m.hhi)
                for p in range(5):
                    act.wait_ge(q.in_mm, q.at.in_mm + p + 1)
                    dst = m.q32[:, p, :] if p < 3 else m.c32[:, p - 3, PAST:KEYS]
                    nc.scalar.copy(halves(dst), pair(p % 4)).then_inc(q.in_ev, 1)
                act.wait_ge(q.in_ev, q.at.in_ev + 6)
                for kt in range(3):
                    last = af(m.sq[:, kt, :], m.q32[:, kt, :], ACT.Square)
                last.then_inc(q.st, 1)
                act.wait_ge(q.v_mm, q.at.v_mm + 1)
                for kt in range(2):
                    last = af(m.sq[:, kt, :], m.c32[:, kt, PAST:KEYS], ACT.Square)
                last.then_inc(q.st, 1)
                ch(af(halves(m.rs[:, 0, :]), pair(0), ACT.Sqrt, bias=eps[:, 1:2], scale=1.0 / QR))
                act.wait_ge(q.v_mm, q.at.v_mm + 2)
                af(halves(m.rs[:, 1, :]), pair(1), ACT.Sqrt, bias=eps[:, 1:2], scale=1.0 / KVR).then_inc(q.rsd, 1)
                act.wait_ge(q.v_mm, q.at.v_mm + 3)
                for h in range(2):
                    nc.scalar.copy(m.K[64:128, 0, PAST + h * HT:PAST + (h + 1) * HT], ps[64:128, 4 + h, 0:HT])
                    nc.scalar.copy(m.K[0:64, 1, PAST + h * HT:PAST + (h + 1) * HT], ps[0:64, 4 + h, 0:HT])
                act.wait_ge(q.cd, q.at.cd + 2)
                act.dma_start(o["ckv"][jj], m.c32[:, :, PAST + TS:KEYS]).then_inc(outs_done, 16)
                act.dma_start(o["kpe"][jj], m.kraw[0:32, TS:T]).then_inc(outs_done, 16)
                act.wait_ge(q.cd, q.at.cd + 3)
                nc.scalar.copy(m.qhi[:, :, :], m.q32[:, :, :]).then_inc(q.hi2, 1)
                nc.scalar.copy(m.khi[:, :, :], m.c32[:, :, :]).then_inc(q.hi2, 1)
                act.wait_ge(outs_done, 32 * (jj + 1))
                end()
                for n in range(12):
                    act.wait_ge(q.v_mm, q.at.v_mm + 3 + n + 1)
                    nc.scalar.copy(m.V[:, n // 2, (n % 2) * 512:(n % 2 + 1) * 512], ps[:, n % 4, :]).then_inc(q.v_ev, 1)
                end()
                with act.Fori(0, HEADS // 2) as j:
                    for u in range(10):
                        qt = u % 5
                        act.wait_ge(q.nmax, q.at.nmax + j * 10 + (u + 1))
                        if u >= 2:
                            act.wait_ge(q.tr, q.at.tr + j * 10 + (u - 1))
                        b = 2 * (u % 2)
                        if qt < 4:
                            af(halves(m.pr[:, u % 2, :]), ps[:, b:b + 2, 0:HT], ACT.Exp, bias=m.nm[:, 2 * (u % 2), 0:1],
                               scale=SM_SCALE, accum_out=m.nm[:, 2 * (u % 2), 1:2]).then_inc(q.pexp, 1)
                        else:
                            af(m.pr[:, u % 2, 0:P], ps[:, b, 0:P], ACT.Exp, bias=m.nm[:, 2 * (u % 2), 0:1],
                               scale=SM_SCALE, accum_out=m.nm[:, 2 * (u % 2), 1:2]).then_inc(q.pexp, 1)
                    act.wait_ge(q.ot, q.at.ot + j + 1)
                    nc.scalar.copy(m.hhi[:, j, 0:TS], ps[:, 7, :]).then_inc(q.ohi, 1)
                    nc.scalar.copy(m.hhi[:, j, TS:T], ps[:, 6, 0:P]).then_inc(q.ohi, 1)
                end()
                end()

            def rwkv(L):
                m, q = m_rwa, q_rwa
                act.wait_ge(q.xst, 16)

                def hi_tile(idx, kt):
                    act.wait_ge(q.val, KD * idx + kt + 1)
                    nc.scalar.copy(m.hset[idx % 2][0][:, kt, :], m.t32[:, kt % 2, :]).then_inc(q.hi, 1)

                for kt in range(KD):
                    for cd, (t0, t1) in enumerate(((0, TS), (TS, T))):
                        last = af(x[:, kt, t0:t1], x[:, kt, t0:t1], ACT.Identity,
                                  bias=mod[:, kt, cd:cd + 1], scale=mod[:, KD + kt, cd:cd + 1])
                    last.then_inc(q.st, 1)
                    if kt >= 2:
                        hi_tile(0, kt - 2)
                hi_tile(0, KD - 2)
                hi_tile(0, KD - 1)
                FUNC = (ACT.Tanh, ACT.Copy, ACT.Sigmoid)
                n = 0

                def hi_part(idx):
                    for kt in range(KD):
                        hi_tile(idx, kt)

                def out_buffer(k):
                    if k >= OUT_BUFFERS:
                        act.wait_ge(s_rst[k % OUT_BUFFERS], 16 * (k // OUT_BUFFERS))
                    return m.o32[:, k % OUT_BUFFERS, :]

                def store(k, dst, width=T):
                    act.wait_ge(q.ev, k + 4)
                    act.dma_start(dst, m.o32[:, k % OUT_BUFFERS, 0:width]).then_inc(s_rst[k % OUT_BUFFERS], 16)

                for idx in range(6):
                    if idx + 1 < 6:
                        hi_part(idx + 1)
                    if idx < 3:
                        act.wait_ge(q.mm, n + 1)
                        if idx:
                            act.wait_ge(q.hidlo, idx)
                        dst = halves(m.o32[:, 0, :])
                        if idx == 1:
                            nc.scalar.copy(dst, pair(n % 4)).then_inc(q.ev, 1)
                        else:
                            af(dst, pair(n % 4), FUNC[idx]).then_inc(q.ev, 1)
                        act.wait_ge(q.ev, n + 1)
                        nc.scalar.copy(m.hid["wag"[idx]][0][:, :], m.o32[:, 0, :]).then_inc(q.hid, 1)
                        n += 1
                        if idx == 2:
                            act.wait_ge(q.hidlo, 3)
                            for c in range(5 * KD):
                                act.wait_ge(q.mm, n + 1)
                                dst = halves(out_buffer(n - 3))
                                if c % 5 < 4:
                                    af(dst, pair(n % 4), ACT.Sigmoid, bias=rwp[:, c // 5, c % 5:c % 5 + 1]).then_inc(q.ev, 1)
                                else:
                                    nc.scalar.copy(dst, pair(n % 4)).then_inc(q.ev, 1)
                                store(n - 3, up_d[c // 5, c % 5])
                                n += 1
                    elif idx < 5:
                        for c in range(KD):
                            act.wait_ge(q.mm, n + 1)
                            nc.scalar.copy(halves(out_buffer(n - 3)), pair(n % 4)).then_inc(q.ev, 1)
                            store(n - 3, (r_d if idx == 3 else k_d)[c])
                            n += 1
                    else:
                        for h in range(2):
                            act.wait_ge(q.mm, n + h + 1)
                            for tt in range(NCH):
                                k = n - 3 + h * NCH + tt
                                nc.scalar.copy(out_buffer(k)[:, 0:512], ps[:, tt, :]).then_inc(q.ev, 1)
                                store(k, v_d[tt][:, h * 512:(h + 1) * 512], 512)
                stores = n - 3 + 2 * NCH
                for b in range(OUT_BUFFERS):
                    act.wait_ge(s_rst[b], 16 * ((stores - b + OUT_BUFFERS - 1) // OUT_BUFFERS))
                end()
                m, q = m_rwb, q_rwb
                act.dma_start(m.pm[:, :, :], a["pmask"]).then_inc(q.sst, 16)
                act.dma_start(m.lm[:, :, :, :], a["lmask"]).then_inc(q.sst, 16)
                act.dma_start(m.i2[:, :], a["ident2"]).then_inc(q.zst, 16)
                sc, tok = (q.sc0, q.sc1), (q.tok0, q.tok1)
                rr, rev, uu, uev = (q.r0, q.r1), (q.rev0, q.rev1), (q.u0, q.u1), (q.uev0, q.uev1)
                yy, yev, tt_, tev = (q.y0, q.y1), (q.yev0, q.yev1), (q.t0, q.t1), (q.tev0, q.tev1)

                def load(j):
                    act.dma_start(m.k[:, :], k_d[j]).then_inc(q.ld, 16)
                    act.dma_start(m.r[:, :], r_d[j]).then_inc(q.ld, 16)
                    act.dma_start(m.LR[:, :, :], up_d[j, 0:4].rearrange("n p t -> p n t")).then_inc(q.ld, 16)
                    act.dma_start(m.par[:, :], a["rw"][j]).then_inc(q.ld, 16)

                def load_rest(j, b):
                    act.dma_start(m.v[b][:, :, :], v_d.rearrange("c p (j n) -> j p c n", n=P)[j]).then_inc(q.ld2, 16)
                    act.dma_start(m.gate[b][:, :], up_d[j, 4]).then_inc(q.ld2, 16)
                    act.dma_start(m.S0[:, :, :], a["s0"][j]).then_inc(q.ld2, 16)
                    act.dma_start(m.lnx[b][:, :, :], a["lnx"][j]).then_inc(q.ld2, 16)

                def raw_keys(j):
                    act.wait_ge(q.ld, j * 64 + 64)
                    af(m.nkk[:, :], m.k[:, :], ACT.Square, scale=m.par[:, 4:5])
                    af(m.kk[:, :], m.k[:, :], ACT.Identity, bias=eps[:, 3:4], scale=m.par[:, 4:5]).then_inc(q.kksq, 1)

                def norms(j):
                    act.wait_ge(q.nrm, j + 1)
                    for h in range(2):
                        last = af(m.nrm[:, h * HT:(h + 1) * HT], ps[:, 3 + 4 * h, 192:512], ACT.Sqrt, bias=eps[:, 3:4])
                    last.then_inc(q.nr, 1)

                def key_scales(j):
                    act.wait_ge(q.scan, j * 2 + 1)
                    for d in range(2):
                        af(m.kd[d][:, :], m.LR[:, 2 + d, :], ACT.Identity, bias=m.cols[:, 0:1], scale=m.par[:, 5:6]).then_inc(q.ka, 1)

                def decays(j, b, d):
                    act.wait_ge(q.dec, j * 2 + (d + 1))
                    src = ((m.D1, -1), (m.D2, -1), (m.D1, 1)) if d == 0 else ((m.D2, 1), (m.D1, 1), (m.D2, -1))
                    chunks = lambda t: t[:, :].rearrange("p (c t) -> p c t", c=NCH)
                    ends = (chunks(m.PS)[:, :, 63], chunks(m.D1)[:, :, P - 1])
                    for e in range(2):
                        af(m.F[b][:, d, e if d == 0 else 1 - e, :], ends[e], ACT.Exp, scale=-KAPPA)
                    if d:
                        act.wait_ge(q.e0, j + 1)
                    for e, (t, sg) in enumerate(src):
                        last = af(m.E[:, e, :], t[:, :], ACT.Exp, scale=sg * KAPPA)
                    last.then_inc(q.ex, 1)

                def bonus(j, b):
                    act.wait_ge(q.bon, j + 1)
                    nc.scalar.copy(m.bon[b][:, :], ps[:, 3, 128:128 + 2 * NCH]).then_inc(q.bonc, 1)

                def deviation(j):
                    act.wait_ge(q.tvar, j + 1)
                    af(m.var[:, :], m.var[:, :], ACT.Sqrt, bias=eps[:, 2:3], scale=1.0 / 64).then_inc(q.rsd, 1)

                def turned_output(j):
                    act.wait_ge(q.z, j + 1)
                    act.wait_ge(q.zst, j * 16 + 16)
                    nc.scalar.copy(m.z[:, 0:384], ps[:, 3, 128:512])
                    nc.scalar.copy(m.z[:, 384:T], ps[:, 7, 128:384]).then_inc(q.zc, 1)

                def store(j):
                    act.wait_ge(q.zg, j + 1)
                    act.dma_start(z_d[j], m.z[:, :]).then_inc(q.zst, 16)

                def store_state(j):
                    for d in range(2):
                        act.wait_ge((q.S0, q.S1)[d], j * 6 + 6)
                        act.dma_start(o["wkv"][j][d], m.So[d][:, :]).then_inc(q.sst, 16)

                def turned_keys(j, b, s):
                    for d in range(2):
                        act.wait_ge(sc[d], j * 5 + (s + 1))
                        nc.scalar.copy(m.BK[d][(b + s) % 2][:, :], ps[:, 4 * d + 2, 0:256]).then_inc(tok[d], 1)

                def rest(j, s):
                    for d in range(2):
                        act.wait_ge(rr[d], j * 5 + (s + 1))
                        nc.scalar.copy(m.R[d][:, :], ps[:, 4 * d + 2, 256:384]).then_inc(rev[d], 1)
                    for d in range(2):
                        act.wait_ge(uu[d], j * 5 + (s + 1))
                        nc.scalar.copy(m.U[d][:, :], ps[:, 4 * d + 2, 384:512]).then_inc(uev[d], 1)
                    for d in range(2):
                        act.wait_ge(yy[d], j * 5 + (s + 1))
                        if s == 0:
                            act.wait_ge(q.tsum, j + 1)
                        nc.scalar.copy(m.yd[d][:, chunk_of(d, s), :], ps[:, 4 * d + 2, 256:384]).then_inc(yev[d], 1)

                def prepare(j, b):
                    load(j)
                    load_rest(j, b)
                    raw_keys(j)
                    norms(j)
                    key_scales(j)
                    decays(j, b, 0)
                    decays(j, b, 1)

                def finish(j, b):
                    rest(j, NCH - 1)
                    store_state(j)
                    deviation(j)
                    turned_output(j)
                    store(j)

                def one(j, b, first, last):
                    if not last:
                        act.wait_ge(q.til, j + 1)
                        load(j + 1)
                    for s in range(NCH):
                        turned_keys(j, b, s)
                        if s:
                            rest(j, s - 1)
                        elif not first:
                            rest(j - 1, NCH - 1)
                        for l in range(2, LEVELS + 1):
                            for d, hh in GROUPS:
                                act.wait_ge(tt_[d], j * 50 + (10 * s + 2 * l - 3 + hh))
                                nc.scalar.copy(m.XT[d][:, hh * P:(hh + 1) * P], ps[:, 4 * d + 3 - hh, 0:P]).then_inc(tev[d], 1)
                            if l == 2:
                                if s == 0:
                                    bonus(j, b)
                                if s == 1 and not last:
                                    norms(j + 1)
                                if s == 2 and not first:
                                    turned_output(j - 1)
                            if l == 5 and s == 0 and not first:
                                deviation(j - 1)
                        if s == 0:
                            if not first:
                                store_state(j - 1)
                            if not last:
                                raw_keys(j + 1)
                        if s == 1 and not last:
                            key_scales(j + 1)
                        if s == 2 and not last:
                            decays(j + 1, 1 - b, 0)
                        if s == 3:
                            if not first:
                                store(j - 1)
                            if not last:
                                decays(j + 1, 1 - b, 1)
                                load_rest(j + 1, 1 - b)
                every_pair(act, one, prepare, finish)
                act.wait_ge(q.zst, 16 * KD + 16)
                act.wait_ge(q.sst, 32 * KD + 32)
                end()
                m = m_rwc
                for kt in range(0, KD, 2):
                    act.dma_start(m.z32[:, kt:kt + 2, :], z_d[kt:kt + 2].rearrange("j p t -> p j t")).then_inc(s_zld[kt // 2], 16)
                act.dma_start(x[:, :, :], x_d.rearrange("k p t -> p k t")).then_inc(q.ld, 16)
                for kt in range(KD):
                    act.wait_ge(s_zld[kt // 2], 16)
                    nc.scalar.copy(m.hhi[:, kt, :], m.z32[:, kt, :]).then_inc(q.st, 1)
                end()

            def pooling(L):
                m, q = m_pool, q_pool
                act.dma_start(m.cnt[:, :, :], a["icnt"]).then_inc(q.cst, 16)
                qq = q_split[2 * L]
                for kt in range(KD):
                    if kt >= 2:
                        act.wait_ge(qq.lo, qq.at.lo + kt - 1)
                    else:
                        act.wait_ge(q.st, 1)
                    for cd, (t0, t1, d0) in enumerate(((0, TS, 16), (TS, T, 48))):
                        last = af(m.hp[:, kt % 2, t0 + d0:t1 + d0], x[:, kt, t0:t1], ACT.Identity,
                                  bias=mod[:, kt, cd:cd + 1], scale=mod[:, KD + kt, cd:cd + 1])
                    last.then_inc(q.hp, 1)
                    act.wait_ge(qq.val, qq.at.val + kt + 1)
                    nc.scalar.copy(m.hhi[:, kt, :], m.t32[:, kt % 2, :]).then_inc(qq.hi, 1)
                end()

            act.wait_ge(s_const, 32)
            act.wait_ge(s_init, 2)
            ch(af(sc_c[:, :, :], cond, ACT.Silu))
            nc.scalar.copy(sc_hi[:, :, :], sc_c[:, :, :]).then_inc(s_init, 1)
            end()
            for L in range(DEPTH):
                ada(L, 2 * L - 1 if L else None)
                (mla, rwkv, pooling)[MIXER[L]](L)
                ffn(L)
            squares(2 * DEPTH - 1)
            deviations(2 * DEPTH - 1)
            end()
            act.dma_start(o["x"].rearrange("k p t -> p k t"), x[:, :, :]).then_inc(outs_done, 16)
            act.wait_ge(outs_done, 16 * (2 * len(m_mla) + 1))

        @block.vector
        def _(dve):
            end = Ends(dve)
            ch = Chain(dve, chain_dve)
            tt, ts, stt, cp = nc.vector.tensor_tensor, nc.vector.tensor_scalar, nc.vector.scalar_tensor_tensor, nc.vector.tensor_copy

            def ada(L, t):
                m = m_ada[L]
                for u in range(ADA_UNITS):
                    unit = ADA_UNITS * L + u
                    if t is not None and u == 2:
                        centre(t)
                    if t is not None and u >= ADA_UNITS - 2 * KD:
                        norm_step(t, u - (ADA_UNITS - 2 * KD))
                    dve.wait_ge(ada_hi, unit + 1)
                    tt(m.lo[unit % ADA_SPLITS][:, :, :], m.ring[unit % ADA_SLOTS][:, :, :], m.hi[unit % ADA_SPLITS][:, :, :].bitcast(F32),
                       ALU.subtract).then_inc(ada_lo, 1)
                end()
                cols = ps[:, 6, 0:96].rearrange("p (n c) -> p n c", c=2)
                ch(tt(mod[:, :, :], cols, adab[:, L, :].unsqueeze(2).to_broadcast([P, 48, 2]), ALU.add))
                for part in (1, 4):
                    s = mod[:, part * KD:(part + 1) * KD, :]
                    ch(ts(s, s, 1.0, None, ALU.add))
                ts(lna[:, :, :], lnp[:, L, 0, :, :], ALPHA, None, ALU.mult)
                both = lambda n: lnp[:, L, 0, n, :].unsqueeze(2).to_broadcast([P, KD, 2])
                for n in range(2):
                    last = tt(hmod[:, n, :, :], mod[:, 4 * KD:5 * KD, :], both(n), ALU.mult)
                ch(last)
                tt(hmod[:, 1, :, :], hmod[:, 1, :, :], mod[:, 3 * KD:4 * KD, :], ALU.add)
                end()

            def split_lo(t, t32, hhi, hlo):
                q = q_split[t]
                for kt in range(KD):
                    dve.wait_ge(q.hi, q.at.hi + kt + 1)
                    tt(hlo[:, kt, :], t32[:, kt % 2, :], hhi[:, kt, :].bitcast(F32), ALU.subtract).then_inc(q.lo, 1)

            def scale_x():
                for kt in range(KD):
                    last = ts(x[:, kt, :], x[:, kt, :], ALPHA, None, ALU.mult)
                ch(last)

            def gated(c, b, gate, done):
                for h, t0, t1, cd in PIECES:
                    xs = x[:, c, h * HT + t0:h * HT + t1]
                    last = stt(xs, ps[:, 2 * b + h, t0:t1], gate[:, c, cd:cd + 1], xs, ALU.mult, ALU.add)
                last.then_inc(done, 1)

            def centre(t):
                m, q = m_ln[t], q_ln[t]
                dve.wait_ge(q.mean, q.at.mean + 1)
                ch(ts(halves(m.rs[:, :]), pair(0), 1.0 / D, None, ALU.mult))
                for kt in range(KD):
                    tt(x[:, kt, :], x[:, kt, :], m.rs[:, :], ALU.subtract).then_inc(q.cen, 1)

            def deviations(t):
                m, q = m_ln[t], q_ln[t]
                dve.wait_ge(q.rsd, q.at.rsd + 1)
                ch(nc.vector.reciprocal(m.rs[:, :], m.rs[:, :]))

            def norm_step(t, n):
                m, q, (L, s) = m_ln[t], q_ln[t], divmod(t, 2)
                if n == 0:
                    deviations(t)
                if n < KD:
                    tt(m.sq[:, n, :], x[:, n, :], m.rs[:, :], ALU.mult).then_inc(q.nrm, 1)
                else:
                    kt = n - KD
                    dve.wait_ge(q.nrm, q.at.nrm + kt + 1)
                    ts(x[:, kt, :], m.sq[:, kt, :], lnp[:, L, s, 0, kt:kt + 1], lnp[:, L, s, 1, kt:kt + 1], ALU.mult, ALU.add)

            def norm(t):
                centre(t)
                for n in range(2 * KD):
                    norm_step(t, n)

            def norm_and_split(t, t32, hhi, hlo):
                m, q, qs = m_ln[t], q_ln[t], q_split[t + 1]
                centre(t)
                deviations(t)

                def lo(kt):
                    dve.wait_ge(qs.hi, qs.at.hi + kt + 1)
                    tt(hlo[:, kt, :], t32[:, kt % 2, :], hhi[:, kt, :].bitcast(F32), ALU.subtract).then_inc(qs.lo, 1)

                for kt in range(KD):
                    tt(m.sq[:, kt, :], x[:, kt, :], m.rs[:, :], ALU.mult).then_inc(q.nrm, 1)
                    if kt >= 2:
                        lo(kt - 2)
                lo(KD - 2)
                lo(KD - 1)
                for kt in range(KD):
                    last = ts(x[:, kt, :], m.sq[:, kt, :], lna[:, 0, kt:kt + 1], lna[:, 1, kt:kt + 1], ALU.mult, ALU.add)
                ch(last)

            def ffn(L):
                m, q = m_ffn[L], q_ffn[L]
                norm_and_split(2 * L, m.t32, m.hhi, m.hlo)
                gate = mod[:, 5 * KD:6 * KD, :]
                f0, dn = 0, 0
                for nf in FHALF:
                    with dve.Fori(0, nf // 2) as i:
                        for u in range(2):
                            dve.wait_ge(q.sil, q.at.sil + i * 2 + (f0 + u + 1))
                            tt(halves(m.a32[:, u, :]), halves(m.sil[:, u, :]), pair(2 * u + 1), ALU.mult).then_inc(q.act, 1)
                            dve.wait_ge(q.hi, q.at.hi + i * 2 + (f0 + u + 1))
                            tt(m.alo[:, i * 2 + u, :], m.a32[:, u, :], m.ahi[:, i * 2 + u, :].bitcast(F32), ALU.subtract).then_inc(q.lo, 1)
                    f0 += nf
                    for c in range(KD):
                        dve.wait_ge(q.down, q.at.down + dn + 1)
                        gated(c, c % 4, gate, q.upd)
                        dn += 1
                    dve.wait_ge(q.upd, q.at.upd + dn)
                end()

            def out_proj(L, gate):
                q = q_out[L]
                scale_x()
                for c in range(KD):
                    dve.wait_ge(q.mm, q.at.mm + c + 1)
                    gated(c, c % 4, gate, q.upd)
                end()

            def mla(L):
                m, q = m_mla[L], q_mla[L]
                jj = L // 3
                qn = C("qn").rearrange("p (l k) -> p l k", l=2)[:, jj, :]
                kvn = C("kvn").rearrange("p (l k) -> p l k", l=2)[:, jj, :]
                split_lo(2 * L, m.t32, m.hhi, m.hlo)
                dve.wait_ge(q.tab, q.at.tab + 16 * 7)
                dve.wait_ge(q.in_mm, q.at.in_mm + 6)
                dve.wait_ge(q.in_ev, q.at.in_ev + 5)
                tt(halves(m.kraw[:, :]), pair(1), halves(m.tab[:, 2, :]), ALU.mult).then_inc(q.in_ev, 1)
                dve.wait_ge(q.rsd, q.at.rsd + 1)
                ch(nc.vector.reciprocal(m.rs[:, :, :], m.rs[:, :, :]))
                for kt in range(2):
                    c = m.c32[:, kt, PAST:KEYS]
                    stt(c, c, kvn[:, kt:kt + 1], m.rs[:, 1, :], ALU.mult, ALU.mult).then_inc(q.cd, 1)
                for kt in range(3):
                    c = m.q32[:, kt, :]
                    last = stt(c, c, qn[:, kt:kt + 1], m.rs[:, 0, :], ALU.mult, ALU.mult)
                last.then_inc(q.cd, 1)
                dve.wait_ge(q.hi2, q.at.hi2 + 1)
                tt(m.qlo[:, :, :], m.q32[:, :, :], m.qhi[:, :, :].bitcast(F32), ALU.subtract)
                dve.wait_ge(q.hi2, q.at.hi2 + 2)
                ch(tt(m.klo[:, :, :], m.c32[:, :, :], m.khi[:, :, :].bitcast(F32), ALU.subtract))
                end()
                end()
                with dve.Fori(0, HEADS // 2) as j:
                    dve.wait_ge(q.head_mm, q.at.head_mm + j * 3 + 1)
                    kp = lambda t: t.rearrange("p (h t) -> p h t", h=2)
                    cp(kp(m.K[0:64, 0, :]), ps[0:64, 4:6, 0:KEYS // 2])
                    cp(kp(m.K[64:128, 1, :]), ps[64:128, 4:6, 0:KEYS // 2])
                    for hh in range(2):
                        dve.wait_ge(q.head_mm, q.at.head_mm + j * 3 + (hh + 2))
                        tt(halves(m.Q[:, hh, :]), pair(hh), halves(m.tab[:, hh, :]), ALU.mult).then_inc(q.q_ev, 1)

                    def tail(u):
                        hh, qt = divmod(u, 5)
                        dve.wait_ge(q.rec, q.at.rec + j * 10 + (u + 1))
                        dve.wait_ge(q.av, q.at.av + j * 10 + (u + 1))
                        ts(m.O[:, qt, hh * 64:(hh + 1) * 64], ps[:, 6, 0:64], m.rc[:, u % 4:u % 4 + 1], None,
                           ALU.mult).then_inc(q.oev, 1)

                    for u in range(10):
                        qt = u % 5
                        n, b = u % 2, 2 * (u % 2)
                        dve.wait_ge(q.sc, q.at.sc + j * 10 + (u + 1))
                        if qt < 4:
                            nc.vector.tensor_reduce(m.mx[:, n:n + 1], ps[:, b:b + 2, 0:HT], AX.XY, ALU.max).then_inc(q.mx, 1)
                        else:
                            nc.vector.tensor_reduce(m.mx[:, n:n + 1], ps[:, b, 0:P], AX.X, ALU.max).then_inc(q.mx, 1)
                        dve.wait_ge(q.mx, q.at.mx + j * 10 + (u + 1))
                        ts(m.nm[:, 2 * n, 0:1], m.mx[:, n:n + 1], -SM_SCALE, None, ALU.mult).then_inc(q.nmax, 1)
                        if u:
                            copy_pt(dve, q, m, j, u - 1)
                        if u >= 2:
                            tail(u - 2)
                    tail(8)
                    copy_pt(dve, q, m, j, 9)
                    tail(9)
                    for n, (t0, t1) in enumerate(((0, TS), (TS, T))):
                        dve.wait_ge(q.ohi, q.at.ohi + j * 2 + (n + 1))
                        tt(m.hlo[:, j, t0:t1], ps[:, 7 - n, 0:t1 - t0], m.hhi[:, j, t0:t1].bitcast(F32),
                           ALU.subtract).then_inc(q.olo, 1)
                end()
                out_proj(L, mod[:, 2 * KD:3 * KD, :])

            def copy_pt(dve, q, m, j, u):
                n = u % 2
                dve.wait_ge(q.tr, q.at.tr + j * 10 + (u + 1))
                if u % 5 < 4:
                    cp(m.pt[:, n, 0:512], ps[:, 4, :])
                    cp(m.pt[:, n, 512:640], ps[:, 5, 0:P]).then_inc(q.ptc, 1)
                else:
                    cp(m.pt[:, n, 0:P], ps[:, 4, 0:P]).then_inc(q.ptc, 1)
                nc.vector.reciprocal(m.rc[:, u % 4:u % 4 + 1], m.nm[:, 2 * n, 1:2]).then_inc(q.rec, 1)

            def rwkv(L):
                m, q = m_rwa, q_rwa

                def neighbours(kt):
                    dve.wait_ge(q.st, kt + 1)
                    h, xx = x[:, kt, :], m.xx[:, kt, :]
                    for t0, t1 in ((0, TS), (TS, T)):
                        tt(xx[:, t0 + 1:t1 - 1], h[:, t0:t1 - 2], h[:, t0 + 2:t1], ALU.add)
                        cp(xx[:, t0:t0 + 1], h[:, t0 + 1:t0 + 2])
                        last = cp(xx[:, t1 - 1:t1], h[:, t1 - 2:t1 - 1])
                    ch(last)
                    ch(stt(xx, xx, 0.5, h, ALU.mult, ALU.subtract))

                ORDER = (1, 4, 5, 0, 2, 3)
                MMS = (1, 2, 3 + 5 * KD, 3 + 6 * KD, 3 + 7 * KD)

                def lo_part(n):
                    idx, kt = divmod(n, KD)
                    dve.wait_ge(q.hi, n + 1)
                    hi, lo = m.hset[idx % 2]
                    tt(lo[:, kt, :], m.t32[:, kt % 2, :], hi[:, kt, :].bitcast(F32), ALU.subtract).then_inc(q.lo, 1)

                def hidden(k):
                    dve.wait_ge(q.hid, k + 1)
                    hi, lo = m.hid["wag"[k]]
                    tt(lo[:, :], m.o32[:, 0, :], hi[:, :].bitcast(F32), ALU.subtract).then_inc(q.hidlo, 1)

                for idx in range(6):
                    for kt in range(KD):
                        n = idx * KD + kt
                        if idx == 0:
                            neighbours(kt)
                        if idx >= 2 and kt == 0:
                            lo_part(n - 1)
                            if idx <= 4:
                                hidden(idx - 2)
                            dve.wait_ge(q.mm, MMS[idx - 2])
                        if n >= 2:
                            dve.wait_ge(q.lo, n - 1)
                        stt(m.t32[:, kt % 2, :], m.xx[:, kt, :], mu_c[:, ORDER[idx], kt:kt + 1], x[:, kt, :],
                            ALU.mult, ALU.add).then_inc(q.val, 1)
                        if n >= 1 and not (idx >= 2 and kt == 0):
                            lo_part(n - 1)
                lo_part(6 * KD - 1)
                end()
                m, q = m_rwb, q_rwb
                sc, x1, inv, xs = (q.sc0, q.sc1), (q.x10, q.x11), (q.inv0, q.inv1), (q.x0, q.x1)
                yy, SS = (q.y0, q.y1), (q.S0, q.S1)
                dve.wait_ge(q.sst, 32)
                dve.wait_ge(q.zst, 16)
                ch(nc.vector.memset(m.onesT[:, :], 1.0))
                for d in range(2):
                    for b in range(2):
                        last = nc.vector.memset(m.AM[d][b][:, :, :], 0.0)
                ch(last)

                h2p = lambda t: t.rearrange("p (h t) -> p h t", h=2)

                def masked_scores(j, b, s):
                    for d in range(2):
                        am = m.AM[d][(b + s) % 2]
                        dve.wait_ge(sc[d], j * 5 + (s + 1))
                        nc.vector.memset(m.pad[d][:, :], 0.0)
                        for hh in range(2):
                            last = nc.vector.copy_predicated(am[:, hh, :], m.pm[:, d, :].bitcast(U32), ps[:, 4 * d + hh, :])
                        ch(last)
                        ch(tt(h2p(m.XT[d][:, :]), am[:, :, 0:P], m.lm[:, d, 0:1, :].to_broadcast([P, 2, P]), ALU.mult))
                        tt(m.XT[d][:, :], m.XT[d][:, :], m.i2[:, :], ALU.add).then_inc(x1[d], 1)
                    for d, hh in GROUPS:
                        dve.wait_ge(inv[d], j * 130 + (26 * s + 1 + hh))
                        cp(m.X[d][:, hh * P:(hh + 1) * P], ps[:, 4 * d + hh, 0:P]).then_inc(xs[d], 1)

                def level(j, b, s, l):
                    for d, hh in GROUPS:
                        dve.wait_ge(inv[d], j * 130 + (26 * s + 4 * l - 1 + hh))
                        tt(m.Y[d][:, hh * P:(hh + 1) * P], ps[:, 4 * d + hh, 0:P], m.lm[:, d, l, :], ALU.mult).then_inc(xs[d], 1)
                    for d, hh in GROUPS:
                        dve.wait_ge(inv[d], j * 130 + (26 * s + 4 * l + 1 + hh))
                        old, new = (m.X[d], m.X[d]) if l < LEVELS else (m.XT[d], m.XF[d])
                        tt(new[:, hh * P:(hh + 1) * P], old[:, hh * P:(hh + 1) * P], ps[:, 4 * d + hh, P:2 * P],
                           ALU.add).then_inc(xs[d], 1)

                def state(j, b, s):
                    for d in range(2):
                        c = chunk_of(d, s)
                        dve.wait_ge(yy[d], j * 5 + (s + 1))
                        if s == NCH - 2:
                            nc.vector.memset(m.S[d][:, :], 0.0).then_inc(SS[d], 1)
                            continue
                        by, dst = (m.Fc[b][:, d, c:c + 1], m.S[d]) if s < NCH - 2 else (m.F[b][:, d, 1, c:c + 1], m.So[d])
                        ch(stt(m.st[:, d, :], ps[:, 4 * d + 3, 0:P], by, C("blk"), ALU.mult, ALU.mult))
                        if s == NCH - 1:
                            dve.wait_ge(q.sst, j * 32 + 32)
                        stt(dst[:, :], m.S[d][:, :], by, m.st[:, d, :], ALU.mult, ALU.add).then_inc(SS[d], 1)

                def scan(j, d):
                    if d:
                        dve.wait_ge(q.ex, j * 2 + 1)
                    else:
                        dve.wait_ge(q.ld, j * 64 + 64)
                        ts(m.cols[:, 0:1], m.par[:, 5:6], -1.0, 1.0, ALU.mult, ALU.add)
                        ts(m.hs[:, :], C("hsel"), m.par[:, 6:7], None, ALU.mult)
                    for c in range(NCH):
                        last = nc.vector.tensor_tensor_scan(m.PS[:, c * P:(c + 1) * P], m.onesT[:, :],
                                                            m.LR[:, d, c * P:(c + 1) * P], 0.0, ALU.mult, ALU.add)
                    last.then_inc(q.scan, 1)

                def norms(j):
                    dve.wait_ge(q.nr, j + 1)
                    ch(ts(m.nrm[:, :], m.nrm[:, :], 1e-12, None, ALU.max))
                    nc.vector.reciprocal(m.nrm[:, :], m.nrm[:, :]).then_inc(q.nrd, 1)

                def first_state(j, b, first):
                    dve.wait_ge(q.ld2, j * 64 + 64)
                    for d in range(2):
                        c = chunk_of(d, 0)
                        if not first:
                            dve.wait_ge(SS[d], j * 6)
                        ts(m.S[d][:, :], m.S0[:, d, :], m.F[b][:, d, 0, c:c + 1], None, ALU.mult).then_inc(SS[d], 1)

                def h2(t):
                    return t[:, :, :].rearrange("p c (h n) -> p (c h) n", h=2)

                def mean(j):
                    dve.wait_ge(q.tsum, j + 2)
                    ch(nc.vector.tensor_reduce(m.mu[:, :], h2(m.ys), AX.X, ALU.add))
                    ts(m.mu[:, :], m.mu[:, :], 1.0 / 64, None, ALU.mult).then_inc(q.tmu, 1)

                def squares(j):
                    dve.wait_ge(q.tsq, j + 1)
                    nc.vector.tensor_reduce(m.var[:, :], h2(m.y2), AX.X, ALU.add).then_inc(q.tvar, 1)

                def deviation(j):
                    dve.wait_ge(q.rsd, j + 1)
                    nc.vector.reciprocal(m.var[:, :], m.var[:, :]).then_inc(q.trc, 1)

                def prepare(j, b):
                    scan(j, 0)
                    norms(j)
                    scan(j, 1)

                def finish(j, b):
                    state(j, b, NCH - 1)
                    mean(j)
                    squares(j)
                    deviation(j)

                def one(j, b, first, last):
                    for s in range(NCH):
                        masked_scores(j, b, s)
                        level(j, b, s, 1)
                        if s:
                            state(j, b, s - 1)
                        else:
                            if not first:
                                state(j - 1, 1 - b, NCH - 1)
                            first_state(j, b, first)
                        if s in (1, 3) and not last:
                            scan(j + 1, s // 2)
                        for l in range(2, LEVELS + 1):
                            level(j, b, s, l)
                            if s == 0 and not first:
                                if l == 3:
                                    mean(j - 1)
                                if l == 5:
                                    squares(j - 1)
                            if s == 1 and l == 2 and not first:
                                deviation(j - 1)
                            if s == 1 and l == 4 and not last:
                                norms(j + 1)
                every_pair(dve, one, prepare, finish, ch, RW_CHAIN)
                end()
                m = m_rwc
                for kt in range(KD):
                    dve.wait_ge(q.st, kt + 1)
                    tt(m.hlo[:, kt, :], m.z32[:, kt, :], m.hhi[:, kt, :].bitcast(F32), ALU.subtract).then_inc(q.zlo, 1)
                dve.wait_ge(q.ld, 64 * KD + 16)
                out_proj(L, mod[:, 2 * KD:3 * KD, :])

            def pooling(L):
                m, q = m_pool, q_pool
                ch(tt(m.gs[:, :, :], mod[:, 2 * KD:3 * KD, :], psc.unsqueeze(2).to_broadcast([P, KD, 2]), ALU.mult))
                nc.vector.memset(m.b[:, :, :], 0.0)
                nc.vector.memset(m.hp[:, :, :], 0.0).then_inc(q.st, 1)
                dve.wait_ge(q.st, 1)
                dve.wait_ge(q.cst, 16)
                qq = q_split[2 * L]
                N = T + 64
                for kt in range(KD):
                    g = kt // 2
                    dve.wait_ge(q.hp, kt + 1)
                    hp, cur, w = m.hp[:, kt % 2, :], m.hp[:, kt % 2, :], 1
                    n = 0
                    while w < WINDOWS[g]:
                        dst = m.b[:, n % 2, :]
                        ch(tt(dst[:, 0:N - 16], cur[:, 0:N - 16], cur[:, w:N - 16 + w], ALU.add))
                        cur, w, n = dst, 2 * w, n + 1
                    hw = WINDOWS[g] // 2
                    t32 = m.t32[:, kt % 2, :]
                    if kt >= 2:
                        dve.wait_ge(qq.lo, qq.at.lo + kt - 1)
                    for t0, t1, d0 in ((0, TS, 16), (TS, T, 48)):
                        last = tt(t32[:, t0:t1], cur[:, t0 + d0 - hw:t1 + d0 - hw], m.cnt[:, g, t0:t1], ALU.mult)
                    ch(last)
                    for t0, t1, d0 in ((0, TS, 16), (TS, T, 48)):
                        last = tt(t32[:, t0:t1], t32[:, t0:t1], hp[:, t0 + d0:t1 + d0], ALU.subtract)
                    last.then_inc(qq.val, 1)
                    dve.wait_ge(qq.hi, qq.at.hi + kt + 1)
                    tt(m.hlo[:, kt, :], t32, m.hhi[:, kt, :].bitcast(F32), ALU.subtract).then_inc(qq.lo, 1)
                out_proj(L, m.gs)

            primed = [q_mla[min(q_mla)].oev, q_mla[min(q_mla)].olo, q_rwb.zt, s_init, q_rwb.tsum]
            for k, v in enumerate((LN_EPS, RMS_EPS, GN_EPS, 0.0)):
                nc.vector.memset(eps[:, k:k + 1], v).then_inc(primed[k], 1)
            nc.vector.memset(eps[:, 4:5], 0.0).then_inc(primed[4], 1)
            dve.wait_ge(s_const, 32)
            dve.wait_ge(s_init, 3)
            ch(tt(sc_lo[:, :, :], sc_c[:, :, :], sc_hi[:, :, :].bitcast(F32), ALU.subtract))
            end()
            for L in range(DEPTH):
                ada(L, 2 * L - 1 if L else None)
                (mla, rwkv, pooling)[MIXER[L]](L)
                ffn(L)
            norm(2 * DEPTH - 1)
            end()

def chunk_of(d, s):
    return s if d == 0 or s == NCH - 1 else NCH - 2 - s

def tables():
    nf = ROPE // 4
    inv = (10000.0 ** (-np.arange(nf, dtype=np.float32) / np.float32(nf))).astype(np.float32)
    t = np.arange(TS)
    ang = np.stack([(t // GRID_W).astype(np.float32)[:, None] * inv, (t % GRID_W).astype(np.float32)[:, None] * inv], 1)
    cos, sin = np.cos(ang).astype(np.float32), np.sin(ang).astype(np.float32)
    Ct, St = np.ones((ROPE, T), np.float32), np.zeros((ROPE, T), np.float32)
    for d in range(ROPE):
        ax, half, f = d // (2 * nf), (d // nf) % 2, d % nf
        Ct[d, :TS] = cos[:, ax, f]
        St[d, :TS] = sin[:, ax, f] * (1 if half else -1)
    one = np.ones((NOPE, T), np.float32)
    tab = np.stack([np.concatenate([one, Ct, St]), np.concatenate([Ct, St, one]), np.concatenate([Ct, St, 0 * one])], 1)
    i = np.arange(P)
    row, col = i[:, None], i[None, :]
    pm = np.zeros((P, 2, 512), np.float32)
    lm = np.zeros((P, 2, LEVELS + 1, P), np.float32)
    for d, (lt, le) in enumerate(((row < col, row <= col), (row > col, row >= col))):
        pm[:, d] = np.concatenate([lt, le, lt, le], 1)
        for l in range(LEVELS + 1):
            n = 1 << l
            same = row // (2 * n) == col // (2 * n)
            later_row = (row // n) % 2 > (col // n) % 2
            early_row = (row // n) % 2 < (col // n) % 2
            want = same & (early_row if (l == 0) == (d == 0) else later_row)
            lm[:, d, l] = want
    dup = np.zeros((P, P), np.float32)
    for k in range(P):
        dup[k % 32, k] = dup[32 + k % 32, k] = 1
    hsel = np.zeros((P, 2), np.float32)
    hsel[:64, 0] = hsel[64:, 1] = 1
    blk = (row // 64 == col // 64).astype(np.float32)
    icnt = np.zeros((4, T), np.float32)
    for g, w in enumerate(WINDOWS):
        for n, off in ((TS, 0), (TP, TS)):
            tt = np.arange(n)
            icnt[g, off:off + n] = np.float32(1) / (np.clip(tt - w // 2 + w, 0, n) - np.clip(tt - w // 2, 0, n)).astype(np.float32)
    return dict(tab=np.ascontiguousarray(tab), pmask=pm, lmask=lm, icnt=icnt,
                ident2=np.concatenate([np.eye(P, dtype=np.float32)] * 2, 1),
                ident=np.eye(P, dtype=np.float32), ones=np.ones((P, P), np.float32), blk=blk, dup=dup, hsel=hsel)

def weight_tiles(w):
    out = []

    def panel(W, col, k0=0, kn=None):
        kn = W.shape[0] // P if kn is None else kn
        for k in range(k0, k0 + kn):
            out.append(W[k * P:(k + 1) * P, col:col + P])

    nf = ROPE // 4
    swap = np.array([d // (2 * nf) * 2 * nf + (1 - (d // nf) % 2) * nf + d % nf for d in range(ROPE)])
    for L in range(DEPTH):
        j = L // 3
        if MIXER[L] == 0:
            for c in range(QR // P):
                panel(w["mla_wq_a"][j], c * P)
            kva = w["mla_wkv_a"][j]
            for c in range(KVR // P):
                panel(kva, c * P)
            pe = kva[:, KVR:]
            panel(np.concatenate([pe, pe[:, swap], np.zeros((D, 64), np.float32)], 1), 0)
            kvb = w["mla_wkv_b"][j].reshape(KVR, HEADS, NOPE + VD)
            v = np.ascontiguousarray(kvb[:, :, NOPE:]).reshape(KVR, HEADS * VD)
            for k in range(2):
                for c in range(8):
                    panel(v, c * P, k, 1)
            qb = w["mla_wq_b"][j].reshape(QR, HEADS, NOPE + ROPE)
            for p in range(HEADS // 2):
                a, b = qb[:, 2 * p], qb[:, 2 * p + 1]
                panel(np.concatenate([kvb[:, 2 * p, :NOPE], kvb[:, 2 * p + 1, :NOPE]], 1), 0)
                panel(np.concatenate([a[:, :NOPE], a[:, NOPE:], a[:, NOPE:][:, swap]], 1), 0)
                panel(np.concatenate([b[:, NOPE:], b[:, NOPE:][:, swap], b[:, :NOPE]], 1), 0)
            for c in range(KD):
                panel(w["mla_wo"][j], c * P)
        elif MIXER[L] == 1:
            for n in ("rwkv_w1", "rwkv_a1"):
                panel(np.concatenate([w[n][j, 0], w[n][j, 1]], 1), 0)
            panel(w["rwkv_g1"][j], 0)
            zero = np.zeros((64, P), np.float32)
            for c in range(KD):
                for n in ("rwkv_w2", "rwkv_a2"):
                    u = w[n][j][:, :, c * P:(c + 1) * P]
                    out.append(np.concatenate([u[0], zero]))
                    out.append(np.concatenate([zero, u[1]]))
                panel(w["rwkv_g2"][j], c * P)
            for n in ("rwkv_wr", "rwkv_wk"):
                for c in range(KD):
                    panel(w[n][j], c * P)
            for h in range(2):
                for k in range(KD):
                    for c in range(4):
                        panel(w["rwkv_wv"][j], (4 * h + c) * P, k, 1)
            for c in range(KD):
                panel(w["rwkv_wo"][j], c * P)
        else:
            for c in range(KD):
                panel(w["pool_w"][j, c // 2], (c % 2) * P)
        f0 = 0
        for nf_ in FHALF:
            for f in range(f0, f0 + nf_):
                panel(w["ffn_wg"][L], f * P)
                panel(w["ffn_wu"][L], f * P)
            for c in range(KD):
                panel(w["ffn_wd"][L], c * P, f0, nf_)
            f0 += nf_
    return out

def columns(v):
    v = v.reshape(*v.shape[:-1], -1, P)
    return np.moveaxis(v, -1, 0)

def kernel(**inputs):
    import concourse.bacc as bacc
    from concourse.bass_utils import run_bass_kernel_spmd

    w = {k: np.asarray(v) for k, v in inputs.items()}
    tb = tables()
    tiles = weight_tiles(w)
    assert len(tiles) == NCHUNK * CH
    stream = np.empty((NCHUNK, P, CH, P), np.float32)
    for n, t in enumerate(tiles):
        stream[n // CH, :, n % CH] = t
    rw = np.stack([w["rwkv_w0"][0, 0], w["rwkv_w0"][0, 1], w["rwkv_a0"][0, 0], w["rwkv_a0"][0, 1],
                   w["rwkv_k_k"][0], w["rwkv_k_a"][0], w["rwkv_r_k"][0].reshape(D)], 0)
    rwc = columns(rw)
    parts = dict(
        ident=tb["ident"], ones=tb["ones"], blk=tb["blk"], hsel=tb["hsel"],
        lnp=columns(np.stack([w["ln_g"], w["ln_b"]], 2)), adab=columns(w["ada_b"]),
        qn=columns(w["mla_q_norm"]), kvn=columns(w["mla_kv_norm"]), mu=columns(w["rwkv_mu"][0]),
        psc=columns(w["pool_scale"][0]), rw=np.moveaxis(rwc, 1, 2),
        cond=np.moveaxis(columns(np.stack([w["c"][0], w["c_ctx"]])), 1, 2))
    cst = np.concatenate([parts[k].reshape(P, -1) for k in _CST], 1)
    assert cst.shape == (P, NCST), cst.shape
    xs = np.concatenate([w["x_sample"][0], w["x_prompt"][0]], 0)
    s0 = w["state_wkv"][0, 0].reshape(2, KD, 2, 64, 64)
    s0b = np.zeros((KD, P, 2, P), np.float32)
    for h in range(2):
        s0b[:, 64 * h:64 * h + 64, :, 64 * h:64 * h + 64] = s0[:, :, h].transpose(1, 3, 0, 2)
    arrays = dict(
        cst=cst, x=np.ascontiguousarray(xs.T).reshape(KD, P, T), w=stream.reshape(NCHUNK, P, CH * P), ada_w=w["ada_w"],
        tab=tb["tab"], dup=tb["dup"], ckvT=w["cache_ckv"][0].reshape(2, PAST, 2, P).transpose(0, 3, 2, 1),
        kpeT=w["cache_kpe"][0].transpose(0, 2, 1), pmask=tb["pmask"], lmask=tb["lmask"], ident2=tb["ident2"],
        s0=s0b,
        lnx=np.stack([w["rwkv_lnx_g"][0], w["rwkv_lnx_b"][0]]).reshape(2, KD, P).transpose(1, 0, 2)[:, None].repeat(P, 1),
        rw=np.moveaxis(rwc, 2, 0), icnt=tb["icnt"][None].repeat(P, 0))
    outs = dict(x=(KD, P, T), ckv=(2, P, 2, TP), kpe=(2, ROPE, TP), wkv=(KD, 2, P, P))

    nc = bacc.Bacc("TRN2", target_bir_lowering=False, num_devices=1)
    a, o = {}, {}
    for k, v in arrays.items():
        arrays[k] = np.ascontiguousarray(v)
        a[k] = nc.dram_tensor("in_" + k, arrays[k].shape, mybir.dt.from_np(arrays[k].dtype), kind="ExternalInput").ap()
    for k, v in outs.items():
        o[k] = nc.dram_tensor("out_" + k, v, F32, kind="ExternalOutput").ap()
    build(nc, a, o)
    r = run_bass_kernel_spmd(nc, [{"in_" + k: v for k, v in arrays.items()}], core_ids=[0]).results[0]
    y = r["out_x"].reshape(D, T).T
    ckv = r["out_ckv"].transpose(0, 3, 2, 1).reshape(2, TP, KVR)
    kpe = r["out_kpe"].transpose(0, 2, 1)
    wkv = np.stack([r["out_wkv"][:, :, 64 * h:64 * h + 64, 64 * h:64 * h + 64] for h in range(2)], 2)
    wkv = wkv.transpose(1, 0, 2, 4, 3).reshape(2, HEADS, 64, 64)
    return (np.ascontiguousarray(y[TS:])[None], np.ascontiguousarray(y[:TS])[None], np.ascontiguousarray(ckv)[None],
            np.ascontiguousarray(kpe)[None], np.ascontiguousarray(wkv)[None, None])
```
